# Optimizing a Trainium2 kernel written in Bass

```python
import jax, jax.numpy as jnp
from jax import lax
import numpy as np
import jax
import jax.numpy as jnp

D_MODEL = 1024
BATCH = 1
SEQ = 256
DEPTH = 2

CTX_LEN = 256
GRID_W = 64
EPS = 1e-6

FOURIER_GROUPS = 4
FOURIER_GD = 64
FOURIER_W = FOURIER_GROUPS * FOURIER_GD
ATT_HEADS = 8
ATT_KV_HEADS = 2
ATT_GROUP = ATT_HEADS // ATT_KV_HEADS
HEAD_DIM = 64
ATT_W = ATT_HEADS * HEAD_DIM
ATT_KV_W = ATT_KV_HEADS * HEAD_DIM
HG_HEADS = 4
HG_DK = 64
HG_DV = 64
HG_W = HG_HEADS * HG_DK
MIX_W = FOURIER_W + ATT_W + HG_W

OFF_FOURIER = 0
OFF_Q = OFF_FOURIER + FOURIER_W
OFF_K = OFF_Q + ATT_W
OFF_V = OFF_K + ATT_KV_W
OFF_FF = OFF_V + ATT_KV_W
OFF_FB = OFF_FF + HG_W
OFF_I = OFF_FB + HG_W
OFF_HQ = OFF_I + HG_W
OFF_G = OFF_HQ + HG_W
PROJ_W = OFF_G + HG_W

D_FF = -(-8 * D_MODEL // (3 * 256)) * 256
ROPE_THETA = 10000.0
Q_BLOCK = 128
HG_CHUNK = 64


def rmsnorm(x, gain=None):
    xf = x.astype(jnp.float32)
    y = xf * lax.rsqrt(jnp.mean(xf * xf, axis=-1, keepdims=True) + EPS)
    if gain is not None:
        y = y * gain.astype(jnp.float32)
    return y.astype(x.dtype)

def col(u, off, width, base=0):
    return u[..., off - base: off - base + width]

def axial_rope_tables(n):
    rows = n // GRID_W
    row = jnp.repeat(jnp.arange(rows), GRID_W).astype(jnp.float32)
    colp = jnp.tile(jnp.arange(GRID_W), rows).astype(jnp.float32)
    half = HEAD_DIM // 2
    freqs = ROPE_THETA ** (-jnp.arange(0, half, 2, dtype=jnp.float32) / half)
    ang_r = row[:, None] * freqs
    ang_c = colp[:, None] * freqs
    return (jnp.cos(ang_r), jnp.sin(ang_r), jnp.cos(ang_c), jnp.sin(ang_c))

def rope_axis(x, cos, sin):
    x1, x2 = jnp.split(x, 2, axis=-1)
    return jnp.concatenate([x1 * cos - x2 * sin, x1 * sin + x2 * cos], axis=-1)

def apply_axial_rope(x, tabs):
    cr, sr, cc, sc = tabs
    xf = x.astype(jnp.float32)
    xr, xc = jnp.split(xf, 2, axis=-1)
    return jnp.concatenate([rope_axis(xr, cr, sr), rope_axis(xc, cc, sc)], axis=-1).astype(x.dtype)

def fourier_mix(u, w):
    b, n, _ = u.shape
    z = u.astype(jnp.float32).reshape(b, n, FOURIER_GROUPS, FOURIER_GD)
    z = jnp.fft.fftn(z, axes=(1, 3), norm="ortho").real
    return z.reshape(b, n, FOURIER_W).astype(u.dtype) @ w

def attend(q, k, v):
    s = jnp.einsum('bkgqd,bksd->bkgqs', q, k).astype(jnp.float32) * (HEAD_DIM ** -0.5)
    p = jax.nn.softmax(s, axis=-1).astype(v.dtype)
    return jnp.einsum('bkgqs,bksd->bkgqd', p, v)

def attend_blocked(q, k, v):
    b, kh, g, n, d = q.shape
    nb = n // Q_BLOCK
    qb = jnp.moveaxis(q.reshape(b, kh, g, nb, Q_BLOCK, d), 3, 0)
    ob = lax.map(lambda qi: attend(qi, k, v), qb)
    return jnp.moveaxis(ob, 0, 3).reshape(b, kh, g, n, d)

def q_heads(u, gain):
    b, n, _ = u.shape
    return rmsnorm(u.reshape(b, n, ATT_HEADS, HEAD_DIM), gain).transpose(0, 2, 1, 3)

def kv_heads(u, gain=None):
    b, n, _ = u.shape
    return rmsnorm(u.reshape(b, n, ATT_KV_HEADS, HEAD_DIM), gain).transpose(0, 2, 1, 3) if gain is not None \
        else u.reshape(b, n, ATT_KV_HEADS, HEAD_DIM).transpose(0, 2, 1, 3)

def group_q(qh):
    b, h, n, d = qh.shape
    return qh.reshape(b, ATT_KV_HEADS, ATT_GROUP, n, d)

def ungroup(o):
    b, kh, g, n, d = o.shape
    return o.transpose(0, 3, 1, 2, 4).reshape(b, n, kh * g * d)

def attention_group(ux, uc, base_c, q_gain, k_gain, tabs, ctx_out):
    qx = group_q(apply_axial_rope(q_heads(col(ux, OFF_Q, ATT_W), q_gain), tabs))
    kx = apply_axial_rope(kv_heads(col(ux, OFF_K, ATT_KV_W), k_gain), tabs)
    vx = kv_heads(col(ux, OFF_V, ATT_KV_W))
    kc = kv_heads(col(uc, OFF_K, ATT_KV_W, base_c), k_gain)
    vc = kv_heads(col(uc, OFF_V, ATT_KV_W, base_c))
    k_all = jnp.concatenate([kc, kx], axis=2)
    v_all = jnp.concatenate([vc, vx], axis=2)
    out_x = ungroup(attend_blocked(qx, k_all, v_all))
    out_c = None
    if ctx_out:
        qc = group_q(q_heads(col(uc, OFF_Q, ATT_W, base_c), q_gain))
        out_c = ungroup(attend(qc, kc, vc))
    return out_x, out_c

def hgrn_scan(k, v, log_f, s0, q=None):
    b, h, n, dk = k.shape
    nc = n // HG_CHUNK
    with_out = q is not None

    def chunks(a):
        return jnp.moveaxis(a.reshape(b, h, nc, HG_CHUNK, a.shape[-1]), 2, 0)

    mask = jnp.tril(jnp.ones((HG_CHUNK, HG_CHUNK), dtype=bool))[:, :, None]

    def step(s, inp):
        kc, vc, lf = inp[0], inp[1], inp[2]
        cum = jnp.cumsum(lf, axis=2)
        last = cum[:, :, -1:, :]
        s_new = jnp.exp(last[:, :, 0, :])[..., None] * s + \
            jnp.einsum('bhsd,bhse->bhde', kc * jnp.exp(last - cum), vc)
        if not with_out:
            return s_new, None
        qc = inp[3]
        o_inter = jnp.einsum('bhtd,bhde->bhte', qc * jnp.exp(cum), s)
        diff = cum[:, :, :, None, :] - cum[:, :, None, :, :]
        decay = jnp.exp(jnp.where(mask, diff, -jnp.inf))
        att = jnp.einsum('bhtd,bhsd,bhtsd->bhts', qc, kc, decay)
        return s_new, o_inter + jnp.einsum('bhts,bhse->bhte', att, vc)

    xs = (chunks(k), chunks(v), chunks(log_f)) + ((chunks(q),) if with_out else ())
    s_fin, o = lax.scan(step, s0, xs)
    if with_out:
        o = jnp.moveaxis(o, 0, 2).reshape(b, h, n, v.shape[-1])
    return o, s_fin

def hg_heads(u):
    b, n, _ = u.shape
    return u.reshape(b, n, HG_HEADS, -1).transpose(0, 2, 1, 3).astype(jnp.float32)

def hg_gate(z, lb):
    lb = lb.reshape(HG_HEADS, 1, HG_DK)
    k = (1.0 - lb) * jax.nn.sigmoid(-z)
    log_f = jnp.log(lb + (1.0 - lb) * jax.nn.sigmoid(z))
    return k, log_f

def hg_readout(o, g, gain, dtype):
    b, h, n, dv = o.shape
    y = rmsnorm(o, gain).transpose(0, 2, 1, 3).reshape(b, n, h * dv)
    return (y * jax.nn.silu(g.astype(jnp.float32))).astype(dtype)

def hgrn_group(ux, uc, base_c, lb_dirs, gain, ctx_out):
    b = ux.shape[0]
    vx = hg_heads(col(ux, OFF_I, HG_W))
    qx = hg_heads(col(ux, OFF_HQ, HG_W))
    vc = hg_heads(col(uc, OFF_I, HG_W, base_c))
    qc = hg_heads(col(uc, OFF_HQ, HG_W, base_c)) if ctx_out else None
    s0 = jnp.zeros((b, HG_HEADS, HG_DK, HG_DV), jnp.float32)
    o_x = jnp.zeros_like(vx)
    o_c = jnp.zeros_like(vc) if ctx_out else None
    for d, (off, rev) in enumerate(((OFF_FF, False), (OFF_FB, True))):
        fl = (lambda a: jnp.flip(a, axis=2)) if rev else (lambda a: a)
        kx, lfx = hg_gate(hg_heads(col(ux, off, HG_W)), lb_dirs[d])
        kc, lfc = hg_gate(hg_heads(col(uc, off, HG_W, base_c)), lb_dirs[d])
        oc, s_ctx = hgrn_scan(fl(kc), fl(vc), fl(lfc), s0, fl(qc) if ctx_out else None)
        ox, _ = hgrn_scan(fl(kx), fl(vx), fl(lfx), s_ctx, fl(qx))
        o_x = o_x + fl(ox)
        if ctx_out:
            o_c = o_c + fl(oc)
    out_x = hg_readout(o_x, col(ux, OFF_G, HG_W), gain, ux.dtype)
    out_c = hg_readout(o_c, col(uc, OFF_G, HG_W, base_c), gain, uc.dtype) if ctx_out else None
    return out_x, out_c

def swiglu(h, wg, wu, wd):
    return (jax.nn.silu(h @ wg) * (h @ wu)) @ wd

def first_inputs(seed: int = 0) -> dict:
    key = jax.random.key(seed)
    ks = jax.random.split(key, 18)
    nrm = jax.random.normal
    f32 = jnp.float32
    return {
        "x": nrm(ks[0], (BATCH, SEQ, D_MODEL), f32),
        "c": nrm(ks[1], (BATCH, D_MODEL), f32),
        "ctx": nrm(ks[2], (BATCH, CTX_LEN, D_MODEL), f32),
        "c_ctx": nrm(ks[3], (D_MODEL,), f32),
        "w_ada": nrm(ks[4], (DEPTH, D_MODEL, 6 * D_MODEL), f32) * D_MODEL ** -0.5,
        "b_ada": nrm(ks[5], (DEPTH, 6 * D_MODEL), f32) * 0.02,
        "w_in": nrm(ks[6], (DEPTH, D_MODEL, PROJ_W), f32) * D_MODEL ** -0.5,
        "w_four": nrm(ks[7], (DEPTH, FOURIER_W, FOURIER_W), f32) * FOURIER_W ** -0.5,
        "q_norm": 1.0 + 0.02 * nrm(ks[8], (DEPTH, HEAD_DIM), f32),
        "k_norm": 1.0 + 0.02 * nrm(ks[9], (DEPTH, HEAD_DIM), f32),
        "hg_lb_logits": 0.5 * nrm(ks[10], (2, DEPTH, HG_W), f32),
        "hg_norm": 1.0 + 0.02 * nrm(ks[11], (DEPTH, HG_DV), f32),
        "w_out": nrm(ks[12], (DEPTH, MIX_W, D_MODEL), f32) * MIX_W ** -0.5,
        "w_gate": nrm(ks[13], (DEPTH, D_MODEL, D_FF), f32) * D_MODEL ** -0.5,
        "w_up": nrm(ks[14], (DEPTH, D_MODEL, D_FF), f32) * D_MODEL ** -0.5,
        "w_down": nrm(ks[15], (DEPTH, D_FF, D_MODEL), f32) * D_FF ** -0.5,
        "final_norm": 1.0 + 0.02 * nrm(ks[16], (D_MODEL,), f32),
    }

def first_block(x, c, ctx, c_ctx, w_ada, b_ada, w_in, w_four, q_norm, k_norm,
              hg_lb_logits, hg_norm, w_out, w_gate, w_up, w_down, final_norm):
    d = D_MODEL
    tabs = axial_rope_tables(x.shape[1])
    silu_c = jax.nn.silu(c)
    silu_cc = jax.nn.silu(c_ctx)
    lb_sm = jax.nn.softmax(hg_lb_logits.astype(jnp.float32), axis=1)
    lb_all = jnp.cumsum(lb_sm, axis=1) - lb_sm[:, :1]
    for l in range(DEPTH):
        ctx_out = l < DEPTH - 1
        mod = silu_c @ w_ada[l] + b_ada[l]
        sh_a, sc_a, g_a, sh_f, sc_f, g_f = jnp.split(mod[:, None, :], 6, axis=-1)
        n_c = 6 * d if ctx_out else 2 * d
        mc = jnp.split(silu_cc @ w_ada[l][:, :n_c] + b_ada[l][:n_c], n_c // d)
        hx = rmsnorm(x) * (1 + sc_a) + sh_a
        hc = rmsnorm(ctx) * (1 + mc[1]) + mc[0]
        ux = hx @ w_in[l]
        base_c = 0 if ctx_out else OFF_K
        uc = hc @ (w_in[l] if ctx_out else w_in[l][:, OFF_K:OFF_HQ])
        fx = fourier_mix(col(ux, OFF_FOURIER, FOURIER_W), w_four[l])
        ax, ac = attention_group(ux, uc, base_c, q_norm[l], k_norm[l], tabs, ctx_out)
        rx, rc = hgrn_group(ux, uc, base_c, lb_all[:, l], hg_norm[l], ctx_out)
        x = x + g_a * (jnp.concatenate([fx, ax, rx], axis=-1) @ w_out[l])
        x = x + g_f * swiglu(rmsnorm(x) * (1 + sc_f) + sh_f, w_gate[l], w_up[l], w_down[l])
        if ctx_out:
            fc = fourier_mix(col(uc, OFF_FOURIER, FOURIER_W), w_four[l])
            ctx = ctx + mc[2] * (jnp.concatenate([fc, ac, rc], axis=-1) @ w_out[l])
            ctx = ctx + mc[5] * swiglu(rmsnorm(ctx) * (1 + mc[4]) + mc[3], w_gate[l], w_up[l], w_down[l])
    return rmsnorm(x, final_norm)


N_MIXERS = 2
A_Q_HEADS = 16
A_KV_HEADS = 4
A_HALF_WINDOW = 128
B_GROUPS = ((128, 1), (512, 4), (2048, 16))
B_Q_HEADS = 8
B_KV_HEADS = 2
D_FF_2 = -(-8 * D_MODEL // (3 * 256)) * 256
A_QKV = (A_Q_HEADS + 2 * A_KV_HEADS) * HEAD_DIM
B_QKV = len(B_GROUPS) * (B_Q_HEADS + 2 * B_KV_HEADS) * HEAD_DIM
A_OUT = A_Q_HEADS * HEAD_DIM
B_OUT = B_Q_HEADS * HEAD_DIM
N_A_LAYERS = (DEPTH + 1) // 2
N_B_LAYERS = DEPTH // 2
RMS_EPS = 1e-6
NEG = -1e30


def rmsnorm_2(x, g):
    xf = x.astype(jnp.float32)
    y = xf * lax.rsqrt(jnp.mean(xf * xf, axis=-1, keepdims=True) + RMS_EPS)
    return (y * g.astype(jnp.float32)).astype(x.dtype)

def alibi_slopes(n):
    return jnp.asarray(2.0 ** (-8.0 * np.arange(1, n + 1) / n), dtype=jnp.float32)

def banded_attention(q, k, v, half_window, slopes, dist_scale, sink=None):
    n, L, hkv, g, dh = q.shape
    blk = half_window
    nb = -(-L // blk)
    lp = nb * blk
    qb = jnp.pad(q, ((0, 0), (0, lp - L), (0, 0), (0, 0), (0, 0))).reshape(n, nb, blk, hkv, g, dh)
    pad_kv = ((0, 0), (blk, lp - L + blk), (0, 0), (0, 0))
    kb = jnp.pad(k, pad_kv).reshape(n, nb + 2, blk, hkv, dh)
    vb = jnp.pad(v, pad_kv).reshape(n, nb + 2, blk, hkv, dh)
    kw = jnp.concatenate([kb[:, :-2], kb[:, 1:-1], kb[:, 2:]], axis=2)
    vw = jnp.concatenate([vb[:, :-2], vb[:, 1:-1], vb[:, 2:]], axis=2)
    rel = jnp.arange(3 * blk)[None, :] - blk - jnp.arange(blk)[:, None]
    kpos = jnp.arange(nb)[:, None] * blk - blk + jnp.arange(3 * blk)[None, :]
    mask = (jnp.abs(rel) <= half_window)[None] & ((kpos >= 0) & (kpos < L))[:, None, :]
    dist = (dist_scale * jnp.abs(rel)).astype(jnp.float32)
    bias = -slopes.astype(jnp.float32)[:, :, None, None] * dist
    s = jnp.einsum('nbqhgd,nbkhd->nbhgqk', qb, kw,
                   preferred_element_type=jnp.float32) * (dh ** -0.5) + bias
    s = jnp.where(mask[None, :, None, None], s, NEG)
    m = s.max(axis=-1)
    if sink is not None:
        sk = sink.astype(jnp.float32)[:, :, None]
        m = jnp.maximum(m, sk)
    p = jnp.exp(s - m[..., None])
    l = p.sum(axis=-1)
    if sink is not None:
        l = l + jnp.exp(sk - m)
    o = jnp.einsum('nbhgqk,nbkhd->nbqhgd', p, vw.astype(jnp.float32))
    o = o / jnp.moveaxis(l, -1, 2)[..., None]
    lse = jnp.moveaxis(m + jnp.log(l), -1, 2)
    o = o.reshape(n, lp, hkv, g, dh)[:, :L].astype(q.dtype)
    lse = lse.reshape(n, lp, hkv, g)[:, :L]
    return o, lse

def to_strided(t, dil):
    b, s = t.shape[:2]
    rest = t.shape[2:]
    t = t.reshape(b, s // dil, dil, *rest)
    return jnp.moveaxis(t, 2, 1).reshape(b * dil, s // dil, *rest)

def from_strided(t, b, dil):
    l = t.shape[1]
    rest = t.shape[2:]
    t = t.reshape(b, dil, l, *rest)
    return jnp.moveaxis(t, 1, 2).reshape(b, l * dil, *rest)

def windowed_gqa(h, w_in, w_out, sink):
    b, s, _ = h.shape
    gq = A_Q_HEADS // A_KV_HEADS
    dq, dk = A_Q_HEADS * HEAD_DIM, A_KV_HEADS * HEAD_DIM
    qkv = h @ w_in
    q = qkv[..., :dq].reshape(b, s, A_KV_HEADS, gq, HEAD_DIM)
    k = qkv[..., dq:dq + dk].reshape(b, s, A_KV_HEADS, HEAD_DIM)
    v = qkv[..., dq + dk:].reshape(b, s, A_KV_HEADS, HEAD_DIM)
    slopes = alibi_slopes(A_Q_HEADS).reshape(A_KV_HEADS, gq)
    o, _ = banded_attention(q, k, v, A_HALF_WINDOW, slopes, 1, sink.reshape(A_KV_HEADS, gq))
    return o.reshape(b, s, A_OUT) @ w_out

def dilated_attention(h, w_in, w_out):
    b, s, _ = h.shape
    ng = len(B_GROUPS)
    gq = B_Q_HEADS // B_KV_HEADS
    dq, dk = ng * B_Q_HEADS * HEAD_DIM, ng * B_KV_HEADS * HEAD_DIM
    qkv = h @ w_in
    q = qkv[..., :dq].reshape(b, s, ng, B_KV_HEADS, gq, HEAD_DIM)
    k = qkv[..., dq:dq + dk].reshape(b, s, ng, B_KV_HEADS, HEAD_DIM)
    v = qkv[..., dq + dk:].reshape(b, s, ng, B_KV_HEADS, HEAD_DIM)
    slopes = alibi_slopes(ng * B_Q_HEADS).reshape(ng, B_KV_HEADS, gq)
    outs, lses = [], []
    for gi, (window, dil) in enumerate(B_GROUPS):
        half = window // (2 * dil)
        o, lse = banded_attention(to_strided(q[:, :, gi], dil), to_strided(k[:, :, gi], dil),
                                  to_strided(v[:, :, gi], dil), half, slopes[gi], dil)
        outs.append(from_strided(o, b, dil))
        lses.append(from_strided(lse, b, dil))
    alpha = jax.nn.softmax(jnp.stack(lses), axis=0)
    o = jnp.einsum('nbshg,nbshgd->bshgd', alpha,
                   jnp.stack(outs).astype(jnp.float32)).astype(h.dtype)
    return o.reshape(b, s, B_OUT) @ w_out

def swiglu_2(h, w_in, w_out):
    gu = h @ w_in
    gate, up = jnp.split(gu, 2, axis=-1)
    return (jax.nn.silu(gate) * up) @ w_out

def second_inputs(seed: int = 0) -> dict:
    key = jax.random.key(seed)
    ks = jax.random.split(key, 16)
    D = D_MODEL
    nrm = lambda k, shape, scale: jax.random.normal(k, shape, jnp.float32) * scale
    return {
        "x": nrm(ks[0], (BATCH, SEQ, D), 1.0),
        "c": nrm(ks[1], (BATCH, D), 1.0),
        "ada_w": nrm(ks[2], (DEPTH, D, 6 * D), 0.5 * D ** -0.5),
        "ada_b": nrm(ks[3], (DEPTH, 6 * D), 0.1),
        "norm_mix": 1.0 + nrm(ks[4], (DEPTH, D), 0.05),
        "norm_ffn": 1.0 + nrm(ks[5], (DEPTH, D), 0.05),
        "ffn_w_in": nrm(ks[6], (DEPTH, D, 2 * D_FF_2), D ** -0.5),
        "ffn_w_out": nrm(ks[7], (DEPTH, D_FF_2, D), D_FF_2 ** -0.5),
        "a_w_in": nrm(ks[8], (N_A_LAYERS, D, A_QKV), D ** -0.5),
        "a_w_out": nrm(ks[9], (N_A_LAYERS, A_OUT, D), A_OUT ** -0.5),
        "a_sink": nrm(ks[10], (N_A_LAYERS, A_Q_HEADS), 0.5),
        "b_w_in": nrm(ks[11], (N_B_LAYERS, D, B_QKV), D ** -0.5),
        "b_w_out": nrm(ks[12], (N_B_LAYERS, B_OUT, D), B_OUT ** -0.5),
        "final_norm": 1.0 + nrm(ks[13], (D,), 0.05),
    }

def second_block(x, c, ada_w, ada_b, norm_mix, norm_ffn, ffn_w_in, ffn_w_out,
              a_w_in, a_w_out, a_sink, b_w_in, b_w_out, final_norm):
    cond = jax.nn.silu(c)
    for i in range(DEPTH):
        mod = (cond @ ada_w[i] + ada_b[i])[:, None, :]
        sh1, sc1, g1, sh2, sc2, g2 = jnp.split(mod, 6, axis=-1)
        h = rmsnorm_2(x, norm_mix[i]) * (1 + sc1) + sh1
        j = i // N_MIXERS
        if i % N_MIXERS == 0:
            y = windowed_gqa(h, a_w_in[j], a_w_out[j], a_sink[j])
        else:
            y = dilated_attention(h, b_w_in[j], b_w_out[j])
        x = x + g1 * y
        h = rmsnorm_2(x, norm_ffn[i]) * (1 + sc2) + sh2
        x = x + g2 * swiglu_2(h, ffn_w_in[i], ffn_w_out[i])
    return rmsnorm_2(x, final_norm)


def setup_inputs(seed=0):
    out = dict(first_inputs(seed))
    for name, value in second_inputs(seed + 1).items():
        if name != "x":
            out[name + "_2"] = value
    return out


def reference(
    x, c, ctx, c_ctx, w_ada, b_ada, w_in, w_four, q_norm, k_norm, hg_lb_logits, hg_norm, w_out,
    w_gate, w_up, w_down, final_norm, c_2, ada_w_2, ada_b_2, norm_mix_2, norm_ffn_2, ffn_w_in_2,
    ffn_w_out_2, a_w_in_2, a_w_out_2, a_sink_2, b_w_in_2, b_w_out_2, final_norm_2,
):
    x = first_block(
        x, c, ctx, c_ctx, w_ada, b_ada, w_in, w_four, q_norm, k_norm, hg_lb_logits, hg_norm,
        w_out, w_gate, w_up, w_down, final_norm,
    )
    return second_block(
        x, c_2, ada_w_2, ada_b_2, norm_mix_2, norm_ffn_2, ffn_w_in_2, ffn_w_out_2, a_w_in_2,
        a_w_out_2, a_sink_2, b_w_in_2, b_w_out_2, final_norm_2,
    )


_drawn_inputs = setup_inputs


def setup_inputs(seed=0):
    import zlib

    import numpy as np

    out = dict(_drawn_inputs(seed))
    spreads = {}
    factors = {'q_norm': 8.0,
     'k_norm': 8.0,
     'hg_norm': 7.557,
     'final_norm': 2.717,
     'norm_mix_2': 4.686,
     'a_sink_2': 64.0,
     'norm_ffn_2': 3.371}
    for name, (base, spread) in spreads.items():
        noise = np.random.default_rng([zlib.crc32(name.encode()), seed]).standard_normal(out[name].shape)
        drawn = base * np.exp(spread * noise) if base else spread * noise
        out[name] = jnp.asarray(drawn.astype(out[name].dtype))
    for name, factor in factors.items():
        out[name] = (out[name] * factor).astype(out[name].dtype)
    return out
```

```python
from contextlib import ExitStack

import numpy as np

import concourse.bass as bass
from concourse import mybir

P = 128
F32 = mybir.dt.float32
BF16 = mybir.dt.bfloat16
ALU = mybir.AluOpType
ACT = mybir.ActivationFunctionType
AX = mybir.AxisListType

D = 1024
KD = D // P
N = 256
DH = 64
FF = 2816
NF = FF // P
EPS = 1e-6
PROJ = [2304, 2304, 1536, 2304]
OFF_Q, OFF_K, OFF_V, OFF_Z, OFF_I, OFF_HQ, OFF_G = 256, 768, 896, 1024, 1536, 1792, 2048
LEVELS = 7
WSLOTS = 3
SLOT = KD * 512
NBANKS = 6
X_TILES, C_TILES = (0, 1), (2, 3)
ADA = 12
GROUPS_B = ((128, 1), (512, 4), (2048, 16))


def level_matrices():
    i = np.arange(P)
    sums, tails, masks = [], [], []
    for h in (1 << j for j in range(LEVELS)):
        mid = (i // (2 * h)) * 2 * h + h
        second = (i % (2 * h)) >= h
        r, c = i[:, None], i[None, :]
        fwd = second[None, :] & (r >= mid[None, :]) & (r <= c)
        back = ~second[None, :] & (r > c) & (r < mid[None, :])
        sums.append((fwd | back).astype(np.float32))
        same = (i[:, None] // (2 * h)) == (i[None, :] // (2 * h))
        masks.append((same & ~second[:, None] & second[None, :]).astype(np.float32))
    sums.append((i[:, None] <= i[None, :]).astype(np.float32))
    masks.append(np.eye(P, dtype=np.float32))
    tails = (i[:, None] > i[None, :]).astype(np.float32)
    sums, masks = np.stack(sums, 1), np.stack(masks, 1)
    both = [np.stack([a, a[::-1, ..., ::-1]], 1) for a in (sums, tails, masks)]
    return [np.ascontiguousarray(a.reshape(P, 2, -1)) for a in both]


def rope_tables():
    half = DH // 2
    freqs = (10000.0 ** (-np.arange(0, half, 2, dtype=np.float32) / np.float32(half))).astype(np.float32)
    pos = np.arange(N)
    ang = [(p[:, None].astype(np.float32) * freqs).astype(np.float32) for p in (pos // 64, pos % 64)]
    cos = np.concatenate([np.cos(a) for a in (ang[0], ang[0], ang[1], ang[1])], 1).astype(np.float32)
    sin = np.concatenate([-np.sin(ang[0]), np.sin(ang[0]), -np.sin(ang[1]), np.sin(ang[1])], 1).astype(np.float32)
    return [np.ascontiguousarray(a.reshape(2, P, DH).transpose(1, 0, 2)) for a in (cos, sin)]


def fourier_tables():
    t = 2 * np.pi * (np.outer(np.arange(N), np.arange(N)) % N) / N
    cs = np.concatenate([np.cos(t), np.sin(t)], 1).astype(np.float32).reshape(2, P, 2 * N).transpose(1, 0, 2)
    t = 2 * np.pi * (np.outer(np.arange(DH), np.arange(DH)) % DH) / DH
    cols = [np.kron(np.eye(2), f / 128.0).astype(np.float32) for f in (np.cos(t), -np.sin(t))]
    return np.ascontiguousarray(cs), np.ascontiguousarray(np.stack(cols, 1))


def distance_tables():
    t, s = np.arange(N)[:, None], np.arange(N)[None, :]
    away = np.abs(t - s)
    seen = [away <= P] + [((t - s) % dil == 0) & (away <= window // 2) for window, dil in GROUPS_B]
    out = np.stack([np.where(ok, -away, -1e30) for ok in seen]).astype(np.float32)
    return np.ascontiguousarray(out.reshape(4, 2, P, N).transpose(2, 0, 1, 3))


def slopes(n):
    return [float(x) for x in (2.0 ** (-8.0 * np.arange(1, n + 1) / n)).astype(np.float32)]


def tables():
    sums, tails, masks = level_matrices()
    cos, sin = rope_tables()
    cs, cols = fourier_tables()
    return {"t_sums": sums, "t_tails": tails, "t_masks": masks, "t_cos": cos, "t_sin": sin, "t_cs": cs,
            "t_cols": cols, "t_dist": distance_tables(), "t_ident": np.eye(P, dtype=np.float32)}


def tiles_of(layer, stage):
    if stage == "mix":
        return (0, 1, 2, 3) if layer < 2 else (0, 1)
    return (0, 1, 2, 3) if layer == 0 else (0, 1)


def conds_of(layer, chunk=0):
    if layer >= 2:
        return (2,)
    return (0, 1) if layer == 0 or chunk < 4 else (0,)


def cond_of_tile(t):
    return 0 if t < 2 else 1


def col_groups(layer):
    return [(a, min(a + 512, PROJ[layer])) for a in range(0, PROJ[layer], 512)]


def cols_of(layer, t, a, b):
    if layer == 1 and t >= 2:
        a, b = max(a, OFF_K), min(b, OFF_HQ)
    return (a, b) if a < b else None


def proj_jobs(layer):
    return [(j, t) for j, (a, b) in enumerate(col_groups(layer)) for t in tiles_of(layer, "mix") if cols_of(layer, t, a, b)]


def load_plan():
    out = []
    for l in range(4):
        out += [("win", l, j) for j in range(len(col_groups(l)))]
        out += [("wo", l, h) for h in range(2)]
        out += [("gu", l, f) for f in range(NF // 2)]
        out += [("dn", l, h, c) for h in range(2) for c in range(3)]
    return out


def attention_units(l):
    out = []
    if l < 2:
        for t in tiles_of(l, "ffn"):
            s = (0, 1, 2, 3) if t < 2 else (2, 3)
            for h in range(8):
                kv = h // 4
                out.append(dict(t=t, h=h, og=(t, 0), oc=h, keys=[(h // 2, kv, s[0] * P, len(s) * P, 0)], half=h % 2,
                                vals=[(i, OFF_V + DH * kv) for i in s], bias=None, size=len(s) * P))
    elif l == 2:
        for t in X_TILES:
            for h in range(16):
                out.append(dict(t=t, h=h, og=(t, h // 8), oc=h % 8, keys=[(h // 2, h // 4, 0, N, 0)], half=h % 2,
                                vals=[(i, 1280 + DH * (h // 4)) for i in X_TILES], bias=[(0, slopes(16)[h])], size=N))
    else:
        for t in X_TILES:
            for h in range(8):
                kv = h // 4
                out.append(dict(t=t, h=h, og=(t, 0), oc=h, half=h % 2, size=3 * N,
                                keys=[((8 * g + h) // 2, 2 * g + kv, 0, N, g * N) for g in range(3)],
                                vals=[(i, 1920 + DH * (2 * g + kv)) for g in range(3) for i in X_TILES],
                                bias=[(1 + g, slopes(24)[8 * g + h]) for g in range(3)]))
    return out


def out_groups(l):
    return list(dict.fromkeys(u["og"] for u in attention_units(l)))


OUT_COL = [OFF_Q, OFF_Q, 0, 0]
HEADS_Q = [8, 8, 16, 24]
HEADS_K = [2, 2, 4, 6]


def mix_banks(l):
    if l < 2:
        return [(2, [OFF_Q + P * i for i in range(4)]), (6, [OFF_G, OFF_G + P])]
    return [(4 * b, [P * (4 * b + i) for i in range(4)]) for b in range(2 if l == 2 else 1)]


KO = [8, 8, 8, 4]


def scan_steps(l):
    order = ((2, 3, 0, 1), (3, 2, 1, 0))
    return [(2 * i + d, order[d][i], d, l == 0 or order[d][i] < 2) for i in range(4) for d in range(2)]


class Counts:

    def __init__(self, nc, ctx, first=None):
        self.nc, self.ctx, self.first = nc, ctx, first
        self.sems, self.count, self.at = {}, {}, {}
        self.banks, self.tenants = {}, []

    def sem(self, name):
        if name not in self.sems:
            self.sems[name] = self.ctx.enter_context(self.nc.semaphore(name))
        return self.sems[name]

    def made(self, name, *key, by=1):
        self.count[name] = self.count.get(name, 0) + by
        self.at[(name, *key)] = self.count[name]
        return self.sem(name), by

    def upto(self, name, *key):
        return self.sem(name), self.first.at[(name, *key)] if self.first else 1

    def drained(self, *key):
        if not self.first:
            return self.sem("drained_act"), 1
        if key[0] == "sc" and key[1] < 2:
            return self.upto("probs", *key[1:3])
        name = "drained_act" if ("drained_act", *key) in self.first.at else "drained_dve"
        return self.upto(name, *key)


def block_kernel(nc, io, first=None):
    ctx = ExitStack()
    with ctx:
        count = Counts(nc, ctx, first)
        made, upto, drained = count.made, count.upto, count.drained

        def sb(name, shape, dt=F32):
            return ctx.enter_context(nc.sbuf_tensor(name, shape, dt))

        X = sb("X", [P, 4, D])
        HT = sb("HT", [P, KD, 512])
        A1 = sb("A1", [P, NF * 512])
        A2 = sb("A2", [P, 11264])
        ring = sb("ring", [P, WSLOTS, SLOT])
        tb_sums = sb("tb_sums", [P, 2048])
        tb_tails = sb("tb_tails", [P, 2, P])
        tb_masks = sb("tb_masks", [P, 2, 8 * P], BF16)
        tb_cs = sb("tb_cs", [P, 2, 2 * N])
        tb_cols = sb("tb_cols", [P, 2, P])
        tb_cos = sb("tb_cos", [P, 2, DH])
        tb_sin = sb("tb_sin", [P, 2, DH])
        ident = sb("ident", [P, P])
        ones = sb("ones", [P, P])
        lb = sb("lb", [P, 2, 256])
        oml = sb("oml", [P, 2, 256])
        grow = sb("grow", [P, 2, D])
        cond = sb("cond", [P, 3, 8])
        condt = sb("condt", [P, 2, 24])
        modc = sb("modc", [P, 2, 48, 2])
        scl = sb("scl", [P, 2, 8])
        gcol = sb("gcol", [P, 4, 8])
        ms = sb("ms", [P, 16])
        lnm = sb("lnm", [P, 16])
        rs = sb("rs", [P, 16])
        nw = sb("nw", [P, 16])
        nmax = sb("nmax", [P, 2, 16])
        lsum = sb("lsum", [P, 2, 16])
        sinkn = sb("sinkn", [P, 16])
        sinke = sb("sinke", [P, 2, 16])
        rinv = sb("rinv", [P, 8])

        U = A1[:, 0:9216].rearrange("p (t c) -> p t c", t=4)
        XN = A1[:, 9216:11264].rearrange("p (b c) -> p b c", b=2)
        AT = A1[:, :].rearrange("p (f n) -> p f n", f=NF)
        W4 = A1[:, 9216:9728].rearrange("p (k c) -> p k c", k=2)
        G10 = A1[:, 9728:10368].rearrange("p (h c) -> p h c", h=10)
        GROW3 = A1[:, 10368:10560].rearrange("p (h c) -> p h c", h=3)
        DIAG = A1[:, 10560:11072].rearrange("p (h c) -> p h c", h=4)

        def cut(start, n):
            return A2[:, start:start + n]

        AW = [cut(4608 * b, 4608) for b in range(2)]
        ACC = cut(9216, 2048).rearrange("p (b i c) -> p b i c", b=2, i=2)
        FA = cut(6656, 1024).rearrange("p (d c) -> p d c", d=2)
        FY = cut(7680, 512).rearrange("p (d c) -> p d c", d=2)
        LOGIT = cut(8192, 1024).rearrange("p (d l c) -> p d l c", d=2, l=2)
        QT = [cut(0, 3072).rearrange("p (k c) -> p k c", c=512 if l < 2 else 256) for l in range(4)]
        KT = [cut(3072, 1536).rearrange("p (k c) -> p k c", c=512 if l < 2 else 256) for l in range(4)]
        SB = cut(4608, 1536).rearrange("p (b c) -> p b c", b=2)
        PB = cut(6144, 1536).rearrange("p (b c) -> p b c", b=2)
        PT = cut(7680, 1536).rearrange("p (b c) -> p b c", b=2)
        KDUP = cut(9216, 768)
        QN, QM = cut(9984, 640), cut(10624, 640)
        QR = cut(4608, 640)
        HW = cut(0, 2048).rearrange("p (b c) -> p b c", b=2)
        QW, KW = cut(2048, 1024), cut(3072, 896)
        AM = cut(3968, 2048).rearrange("p (b c) -> p b c", b=2)
        QT2 = cut(6016, 1024).rearrange("p (t k c) -> p t k c", t=4, k=2)
        KT2 = cut(7040, 256).rearrange("p (k c) -> p k c", k=2)
        HK = cut(7296, 512).rearrange("p (b c) -> p b c", b=2)
        LF = cut(7808, 512).rearrange("p (b c) -> p b c", b=2)
        HE, HS = cut(8320, 256), cut(8576, 256)
        SF = cut(8832, 258)
        KS = cut(9092, 256)
        ST = cut(9348, 512).rearrange("p (d k c) -> p d k c", d=2, k=2)
        OS = cut(9860, 1024).rearrange("p (t c) -> p t c", t=4)
        SUMS = tb_sums[:, :].rearrange("p (d c) -> p d c", d=2)
        DIST = tb_sums[:, :].rearrange("p (g t c) -> p g t c", g=4, t=2)

        bank = [ctx.enter_context(nc.psum_tensor(f"bank{b}", [P, 512], F32)) for b in range(NBANKS)]
        obank = [ctx.enter_context(nc.psum_tensor(f"obank{b}", [P, 512], F32)) for b in range(2)]

        def psum(*key):
            return bank[(first or count).banks.get(key, 0)]

        loads = load_plan()
        slot_of = {key: n % WSLOTS for n, key in enumerate(loads)}

        def slot(key):
            return ring[:, slot_of[key], :]

        def load_ready(key):
            return upto(f"weights{slot_of[key]}", key)

        def last_use(key):
            kind, l = key[:2]
            if kind == "win":
                t = [t for j, t in proj_jobs(l) if j == key[2]][-1]
                return upto("product", "u", l, key[2], t)
            if kind == "wo":
                return upto("product", "x1", l, key[2], tiles_of(l, "ffn")[-1])
            if kind == "gu":
                return upto("product", "up", l, 2 * key[2] + 1)
            if key[3] < 2:
                return upto("down_part", *key[1:])
            return upto("product", "x2", l, key[2], tiles_of(l, "ffn")[-1])

        ada_chunks = [(l, j) for l in range(4) for j in range(ADA)]

        def ada_beside(l, f):
            if l == 3:
                return []
            return [(l + 1, f)] + ([(l + 1, ADA - 1)] if f == NF // 2 - 1 else [])

        def ada_w(l):
            w = io["w_ada"][l] if l < 2 else io["ada_w_2"][l - 2]
            b = io["b_ada"][l] if l < 2 else io["ada_b_2"][l - 2]
            return w, b

        block = ctx.enter_context(nc.Block())

        @block.sync
        def _(sp):
            for name, dst, src in (
                ("cond_in", cond[:, 0, :], io["c"][0].rearrange("(p k) -> p k", k=8)),
                ("cond_in", cond[:, 1, :], io["c_ctx"].rearrange("(p k) -> p k", k=8)),
                ("cond_in", cond[:, 2, :], io["c_2"][0].rearrange("(p k) -> p k", k=8)),
                ("ident_in", ident[:, :], io["t_ident"]),
                ("x_in", X[:, 0:2, :], io["x"][0].rearrange("(t p) d -> p t d", p=P)),
                ("x_in", X[:, 2:4, :], io["ctx"][0].rearrange("(t p) d -> p t d", p=P)),
                ("tables_in", tb_sums[:, :], io["t_sums"].rearrange("p d c -> p (d c)")),
                ("tables_in", tb_tails[:, :, :], io["t_tails"]),
                ("tables_in", tb_masks[:, :, :], io["t_masks"]),
                ("tables_in", tb_cs[:, :, :], io["t_cs"]),
                ("tables_in", tb_cols[:, :, :], io["t_cols"]),
                ("tables_in", tb_cos[:, :, :], io["t_cos"]),
                ("tables_in", tb_sin[:, :, :], io["t_sin"]),
            ):
                sp.dma_start(dst, src).then_inc(*made(name, by=16))

            def rows(w, a, n):
                return w[a * P:(a + n) * P, :].rearrange("(k p) c -> p k c", p=P)

            for n, key in enumerate(loads):
                kind, l = key[:2]
                if n >= WSLOTS:
                    sp.wait_ge(*last_use(loads[n - WSLOTS]))
                to = slot(key)
                sem = f"weights{slot_of[key]}"
                if kind == "win":
                    w = (io["w_in"][l] if l < 2 else io["a_w_in_2"][0] if l == 2 else io["b_w_in_2"][0])
                    a, b = col_groups(l)[key[2]]
                    sp.dma_start(to[:, 0:KD * (b - a)].rearrange("p (k c) -> p k c", k=KD),
                                 rows(w, 0, KD)[:, :, a:b]).then_inc(*made(sem, key, by=16))
                elif kind == "wo":
                    w = (io["w_out"][l] if l < 2 else io["a_w_out_2"][0] if l == 2 else io["b_w_out_2"][0])
                    sp.dma_start(to[:, 0:KO[l] * 512].rearrange("p (k c) -> p k c", k=KO[l]),
                                 rows(w, 0, KO[l])[:, :, 512 * key[2]:512 * key[2] + 512]).then_inc(*made(sem, key, by=16))
                elif kind == "gu":
                    dst = to.rearrange("p (g k c) -> p g k c", g=2, k=KD)
                    if l < 2:
                        g, u = io["w_gate"][l], io["w_up"][l]
                    else:
                        g, u = io["ffn_w_in_2"][l - 2][:, 0:FF], io["ffn_w_in_2"][l - 2][:, FF:2 * FF]
                    for i, w in enumerate((g, u)):
                        sp.dma_start(dst[:, i], rows(w, 0, KD)[:, :, 256 * key[2]:256 * key[2] + 256]) \
                            .then_inc(*made(sem, key, by=16))
                else:
                    w = io["w_down"][l] if l < 2 else io["ffn_w_out_2"][l - 2]
                    h, c = key[2:]
                    n_f = min(8, NF - 8 * c)
                    sp.dma_start(to[:, 0:n_f * 512].rearrange("p (k c) -> p k c", k=n_f),
                                 rows(w, 8 * c, n_f)[:, :, 512 * h:512 * h + 512]).then_inc(*made(sem, key, by=16))
            sp.wait_ge(*upto("final", 3))
            sp.dma_start(io["out"][0].rearrange("(t p) d -> p t d", p=P), X[:, 0:2, :]).then_inc(*made("out_written", by=16))
            sp.wait_ge(*upto("out_written"))

        @block.gpsimd
        def _(pool):
            nc.gpsimd.memset(ones[:, :], 1.0).then_inc(*made("ones_set"))

            with nc.allow_non_contiguous_dma(reason="eight gains to a partition"):
                for i in range(2):
                    for k, g in enumerate(("norm_mix_2", "norm_ffn_2")):
                        pool.dma_start(gcol[:, 2 * i + k, :], io[g][i].rearrange("(k p) -> p k", p=P)) \
                            .then_inc(*made("gains2_in", by=16))

            def ada_load(l, j):
                n = ada_chunks.index((l, j))
                if n >= 2:
                    pool.wait_ge(*upto("product", "mod", *ada_chunks[n - 2]))
                w, b = ada_w(l)
                dst = AW[n % 2]
                pool.dma_start(dst[:, 0:4096].rearrange("p (k c) -> p k c", k=8),
                               w.rearrange("(p k) c -> p k c", k=8)[:, :, 512 * j:512 * j + 512]) \
                    .then_inc(*made(f"ada_weights{n % 2}", l, j, by=16))
                pool.dma_start(dst[0:1, 4096:4608], b[512 * j:512 * j + 512].rearrange("(a c) -> a c", a=1)) \
                    .then_inc(*made(f"ada_weights{n % 2}", l, j, by=16))

            for j in range(ADA):
                ada_load(0, j)
            for l in range(4):
                pool.wait_ge(*upto("product", "h", l, "mix", tiles_of(l, "mix")[-1], 1))
                if l < 2:
                    pool.dma_start(W4, io["w_four"][l].rearrange("(k p) c -> p k c", p=P)).then_inc(*made("gains_in", l, by=16))
                    for i, g in enumerate((io["q_norm"][l], io["k_norm"][l], io["hg_norm"][l])):
                        pool.dma_start(GROW3[:, i, :], g.partition_broadcast(P)).then_inc(*made("gains_in", l, by=16))
                    if l == 1:
                        for d in range(2):
                            pool.dma_start(LOGIT[:, d], io["hg_lb_logits"][d].partition_broadcast(P)) \
                                .then_inc(*made("logits_in", by=16))
                if l == 1:
                    pool.wait_ge(*upto("product", "m", 1, 1, 0))
                    pool.dma_start(tb_sums[:, :], io["t_dist"].rearrange("p g t c -> p (g t c)")).then_inc(*made("dist_in", by=16))
                    pool.dma_start(sinkn[:, :], io["a_sink_2"][0].partition_broadcast(P)).then_inc(*made("dist_in", by=16))
                pool.wait_ge(*upto("product", "x1", l, 1, tiles_of(l, "ffn")[-1]))
                if l < 3:
                    for j in range(ADA):
                        ada_load(l + 1, j)
                if l in (1, 3):
                    pool.wait_ge(*drained("x2", l, 1, 1))
                    g = io["final_norm"] if l == 1 else io["final_norm_2"]
                    pool.dma_start(grow[:, 0, :], g.partition_broadcast(P)).then_inc(*made("final_gain_in", l, by=16))

        @block.tensor
        def _(pe):
            tenants = []

            def open_bank(*key):
                b = len(tenants) % NBANKS
                if len(tenants) >= NBANKS:
                    pe.wait_ge(*drained(*tenants[-NBANKS]))
                tenants.append(key)
                count.banks[key] = b
                return bank[b]

            def mm(out, lhsT, rhs, start, stop):
                return nc.tensor.matmul(out, lhsT, rhs, start=start, stop=stop, skip_group_check=True)

            def turn(out, in_):
                k = in_.shape[0]
                return nc.tensor.transpose(out, in_, ident[0:k, 0:k])

            def modulation(l, j):
                n = ada_chunks.index((l, j))
                pe.wait_ge(*upto(f"ada_weights{n % 2}", l, j))
                pe.wait_ge(*upto("ada_sum", l, j))
                if n == 0:
                    pe.wait_ge(*upto("ones_set"))
                ps = open_bank("mod", l, j)
                for i in range(len(conds_of(l, j))):
                    for c in range(4):
                        o = ps[:, 2 * c + i:2 * c + i + 1]
                        mm(o, ACC[:, n % 2, i, P * c:P * c + P], ones[:, 0:1], True, False)
                        last = mm(o, AW[n % 2][0:1, 4096 + P * c:4096 + P * c + P], ones[0:1, 0:1], False, True)
                last.then_inc(*made("product", "mod", l, j))

            def norm_turn(l, st):
                for t in tiles_of(l, st):
                    pe.wait_ge(*upto("normed", l, st, t))
                    for b in range(2):
                        ps = open_bank("h", l, st, t, b)
                        for i in range(4):
                            last = turn(ps[:, P * i:P * i + P], XN[:, t % 2, P * (4 * b + i):P * (4 * b + i) + P])
                        last.then_inc(*made("product", "h", l, st, t, b))

            def h_ready(l, st):
                for t in tiles_of(l, st):
                    for b in range(2):
                        pe.wait_ge(*drained("h", l, st, t, b))

            def project(l):
                h_ready(l, "mix")
                seen = set()
                for j, t in proj_jobs(l):
                    key = ("win", l, j)
                    if j not in seen:
                        pe.wait_ge(*load_ready(key))
                        seen.add(j)
                    a0, b0 = col_groups(l)[j]
                    a, b = cols_of(l, t, a0, b0)
                    w = slot(key)[:, 0:KD * (b0 - a0)].rearrange("p (k c) -> p k c", k=KD)
                    ps = open_bank("u", l, j, t)
                    for k in range(KD):
                        last = mm(ps[:, 0:b - a], HT[:, k, P * t:P * t + P], w[:, k, a - a0:b - a0], k == 0, k == KD - 1)
                    last.then_inc(*made("product", "u", l, j, t))

            def need_u(l, t, a, b):
                for j, (a0, b0) in enumerate(col_groups(l)):
                    if a < b0 and a0 < b:
                        pe.wait_ge(*drained("u", l, j, t))

            def fourier(l, g):
                tt = (X_TILES, C_TILES)[g]
                for t in tt:
                    need_u(l, t, 0, 256)
                if l == 0 and g == 0:
                    pe.wait_ge(*upto("tables_in"))
                for d in range(2):
                    ps = open_bank("fa", l, g, d)
                    for k in range(2):
                        last = mm(ps[:, :], U[:, tt[k], P * d:P * d + P], tb_cs[:, k, :], k == 0, k == 1)
                    last.then_inc(*made("product", "fa", l, g, d))
                ps = open_bank("fy", l, g)
                for d in range(2):
                    pe.wait_ge(*drained("fa", l, g, d))
                    for k in range(2):
                        last = mm(ps[:, N * d:N * d + N], tb_cols[:, k, :], FA[:, d, N * k:N * k + N], k == 0, k == 1)
                last.then_inc(*made("product", "fy", l, g))
                pe.wait_ge(*upto("gains_in", l))
                pe.wait_ge(*drained("fy", l, g))
                ps = open_bank("ff", l, g)
                for c in range(2):
                    for k in range(2):
                        last = mm(ps[:, N * c:N * c + N], W4[:, k, P * c:P * c + P], FY[:, k, :], k == 0, k == 1)
                last.then_inc(*made("product", "ff", l, g))

            def head_turns(l):
                for t in tiles_of(l, "mix"):
                    pe.wait_ge(*upto("heads_ready", l, t))
                    if l >= 2:
                        need_u(l, t, 0, DH * HEADS_Q[l])
                    nq = HEADS_Q[l] // 2 if (l != 1 or t < 2) else 0
                    src = QN_of(l, t)
                    for b in range(0, nq, 4):
                        ps = open_bank("qT", l, t, b)
                        for i in range(4):
                            last = turn(ps[:, P * i:P * i + P], src[:, P * (b + i):P * (b + i) + P])
                        last.then_inc(*made("product", "qT", l, t, b))
                    for b in range(0, HEADS_K[l], 4):
                        ps = open_bank("kT", l, t, b)
                        for i in range(min(4, HEADS_K[l] - b)):
                            last = turn(ps[:, P * i:P * i + P], KDUP[:, P * (b + i):P * (b + i) + P])
                        last.then_inc(*made("product", "kT", l, t, b))

            def attention(l):
                units = attention_units(l)
                for t in tiles_of(l, "mix"):
                    for b in range(0, HEADS_Q[l] // 2 if (l != 1 or t < 2) else 0, 4):
                        pe.wait_ge(*drained("qT", l, t, b))
                    for b in range(0, HEADS_K[l], 4):
                        pe.wait_ge(*drained("kT", l, t, b))
                    need_u(l, t, *{2: (1280, 1536), 3: (1920, 2304)}.get(l, (OFF_V, OFF_Z)))

                def scores(n):
                    u = units[n]
                    r = slice(DH * u["half"], DH * u["half"] + DH)
                    ps = None
                    for i, (q, kv, s0, sn, at) in enumerate(u["keys"]):
                        if at % 512 == 0:
                            ps = open_bank("sc", l, n, at // 512)
                        last = mm(ps[:, at % 512:at % 512 + sn], QT[l][r, q, P * u["t"]:P * u["t"] + P],
                                  KT[l][r, kv, s0:s0 + sn], True, True)
                        if at % 512 + sn == 512 or i == len(u["keys"]) - 1:
                            last.then_inc(*made("product", "sc", l, n, at // 512))

                def turns(n):
                    u = units[n]
                    pe.wait_ge(*upto("probs", l, n))
                    for i in range(u["size"] // P):
                        if i % 4 == 0:
                            ps = open_bank("pt", l, n, i // 4)
                        last = turn(ps[:, P * (i % 4):P * (i % 4) + P], PB[:, n % 2, P * i:P * i + P])
                        if i % 4 == 3 or i == u["size"] // P - 1:
                            last.then_inc(*made("product", "pt", l, n, i // 4))

                groups = out_groups(l)

                def values(n):
                    u = units[n]
                    g = groups.index(u["og"])
                    for b in range((u["size"] + 511) // 512):
                        pe.wait_ge(*drained("pt", l, n, b))
                    if u["oc"] == 0 and g >= 2:
                        pe.wait_ge(*upto("attended", l, g - 2))
                    for i, (s, c) in enumerate(u["vals"]):
                        last = mm(obank[g % 2][:, DH * u["oc"]:DH * u["oc"] + DH], PT[:, n % 2, P * i:P * i + P],
                                  U[:, s, c:c + DH], i == 0, i == len(u["vals"]) - 1)
                    last.then_inc(*made("valued", l, n))

                for n in range(len(units) + 2):
                    if n < len(units):
                        scores(n)
                    if 1 <= n <= len(units):
                        turns(n - 1)
                    if n >= 2:
                        values(n - 2)

            def recurrence(l):
                for s, t, d, has_out in scan_steps(l):
                    pe.wait_ge(*upto("gates", l, s))
                    pe.wait_ge(*upto("decays", l, s))
                    need_u(l, t, OFF_I, OFF_HQ)
                    lf, kk = LF[:, s % 2], HK[:, s % 2]
                    if has_out:
                        if (s, t) in ((4, 0), (5, 1)) or (l == 0 and s < 2):
                            need_u(l, t, OFF_HQ, OFF_G)
                            ps = open_bank("qt2", l, t)
                            for p in range(2):
                                last = turn(ps[:, P * p:P * p + P], U[:, t, OFF_HQ + P * p:OFF_HQ + P * p + P])
                            last.then_inc(*made("product", "qt2", l, t))
                        ps = open_bank("kt2", l, s)
                        for p in range(2):
                            last = turn(ps[:, P * p:P * p + P], kk[:, P * p:P * p + P])
                        last.then_inc(*made("product", "kt2", l, s))
                        for p in range(2):
                            for b in range(2):
                                ps = open_bank("e", l, s, p, b)
                                mm(ps[:, :], lf[:, P * p:P * p + P], SUMS[:, d, 512 * b:512 * b + 512], True, True) \
                                    .then_inc(*made("product", "e", l, s, p, b))
                        if s >= 2 and ((l == 0) or s >= 6):
                            pe.wait_ge(*upto("scanned", l, s - 2))
                        for p in range(2):
                            pe.wait_ge(*upto("weighed", l, s, p))
                            for hh in range(2):
                                r = slice(DH * hh, DH * hh + DH)
                                for b in range(2):
                                    ps = open_bank("a", l, s, p, hh, b)
                                    for i in range(4):
                                        j = 4 * b + i
                                        q = QT2[r, t, p, :] if j == LEVELS else QW[r, P * j:P * j + P]
                                        k = KT2[r, p, :] if j == LEVELS else KW[r, P * j:P * j + P]
                                        last = mm(ps[:, P * i:P * i + P], k, q, True, True)
                                    last.then_inc(*made("product", "a", l, s, p, hh, b))
                            o = obank[s % 2]
                            if s >= 2:
                                pe.wait_ge(*drained("su", l, s - 2))
                                mm(o[:, P * p:P * p + P], QW[:, LEVELS * P:LEVELS * P + P], ST[:, d, p, :], True, False) \
                                    .then_inc(*made("carried", l, s, p))
                            for hh in range(2):
                                pe.wait_ge(*drained("a", l, s, p, hh, 0))
                                pe.wait_ge(*drained("a", l, s, p, hh, 1))
                                c = P * p + DH * hh
                                for j in range(8):
                                    last = mm(o[:, c:c + DH], AM[:, hh, P * j:P * j + P],
                                              U[:, t, OFF_I + c:OFF_I + c + DH], s < 2 and j == 0, j == 7)
                                last.then_inc(*made("read_out", l, s, p, hh))
                    if s < 6:
                        ps = open_bank("sf", l, s)
                        mm(ps[:, 0:256], tb_tails[:, d, :], lf, True, True)
                        for p in range(2):
                            last = mm(ps[:, 256 + p:257 + p], lf[:, P * p:P * p + P], ones[:, 0:1], True, True)
                        last.then_inc(*made("product", "sf", l, s))
                        pe.wait_ge(*upto("tailed", l, s))
                        ps = open_bank("su", l, s)
                        for p in range(2):
                            last = mm(ps[:, P * p:P * p + P], KS[:, P * p:P * p + P], U[:, t, OFF_I + P * p:OFF_I + P * p + P], True, True)
                        last.then_inc(*made("product", "su", l, s))

            def mixed_turns(l):
                for t in tiles_of(l, "ffn"):
                    if l < 2:
                        pe.wait_ge(*upto("mixed", l, t))
                    for g, og in enumerate(out_groups(l)):
                        if og[0] == t:
                            pe.wait_ge(*upto("attended", l, g))
                    for b, (k0, cols) in enumerate(mix_banks(l)):
                        ps = open_bank("m", l, t, b)
                        for i, c in enumerate(cols):
                            last = turn(ps[:, P * i:P * i + P], U[:, t, c:c + P])
                        last.then_inc(*made("product", "m", l, t, b))

            def gate_rows(l, st):
                for i in range(2 if l == 0 else 1):
                    for h in range(2):
                        pe.wait_ge(*upto("diagonal", l, st, i, h))
                        ps = open_bank("g", l, st, i, h)
                        mm(ps[:, :], ones[:, :], DIAG, True, True).then_inc(*made("product", "g", l, st, i, h))

            def project_out(l):
                for t in tiles_of(l, "ffn"):
                    for b in range(len(mix_banks(l))):
                        pe.wait_ge(*drained("m", l, t, b))
                if l < 2:
                    for g in range(2 if l == 0 else 1):
                        pe.wait_ge(*drained("ff", l, g))
                for h in range(2):
                    pe.wait_ge(*load_ready(("wo", l, h)))
                    w = slot(("wo", l, h))[:, 0:KO[l] * 512].rearrange("p (k c) -> p k c", k=KO[l])
                    for t in tiles_of(l, "ffn"):
                        ps = open_bank("x1", l, h, t)
                        for k in range(KO[l]):
                            last = mm(ps[:, :], HT[:, k, P * t:P * t + P], w[:, k, :], k == 0, k == KO[l] - 1)
                        last.then_inc(*made("product", "x1", l, h, t))

            def feed_forward(l):
                n = P * len(tiles_of(l, "ffn"))
                h_ready(l, "ffn")
                for fp in range(NF // 2):
                    key = ("gu", l, fp)
                    pe.wait_ge(*load_ready(key))
                    w = slot(key).rearrange("p (g k c) -> p g k c", g=2, k=KD)
                    for i in range(2):
                        f = 2 * fp + i
                        for g, name in enumerate(("gate", "up")):
                            ps = open_bank(name, l, f)
                            for k in range(KD):
                                last = mm(ps[:, 0:n], w[:, g, k, P * i:P * i + P], HT[:, k, 0:n], k == 0, k == KD - 1)
                            last.then_inc(*made("product", name, l, f))
                    if fp >= 1:
                        for c in ada_beside(l, fp - 1):
                            modulation(*c)
                for c in ada_beside(l, NF // 2 - 1):
                    modulation(*c)
                for h in range(2):
                    ps = {t: open_bank("x2", l, h, t) for t in tiles_of(l, "ffn")}
                    for c in range(3):
                        key = ("dn", l, h, c)
                        n_f = min(8, NF - 8 * c)
                        pe.wait_ge(*load_ready(key))
                        w = slot(key)[:, 0:n_f * 512].rearrange("p (k c) -> p k c", k=n_f)
                        if h == 0:
                            pe.wait_ge(*drained("up", l, 8 * c + n_f - 1))
                        for t in tiles_of(l, "ffn"):
                            for k in range(n_f):
                                f = 8 * c + k
                                last = mm(ps[t][:, :], AT[:, f, P * t:P * t + P], w[:, k, :], f == 0, f == NF - 1)
                            if c == 2:
                                last.then_inc(*made("product", "x2", l, h, t))
                        if c < 2:
                            last.then_inc(*made("down_part", *key[1:]))

            def QN_of(l, t):
                return QN if l < 2 else U[:, t, :]

            pe.wait_ge(*upto("ident_in"))
            for j in range(ADA):
                modulation(0, j)
            for l in range(4):
                norm_turn(l, "mix")
                project(l)
                if l < 2:
                    for g in range(2 if l == 0 else 1):
                        fourier(l, g)
                head_turns(l)
                attention(l)
                if l < 2:
                    recurrence(l)
                mixed_turns(l)
                gate_rows(l, "mix")
                project_out(l)
                gate_rows(l, "ffn")
                norm_turn(l, "ffn")
                feed_forward(l)

        @block.scalar
        def _(act):
            def put(key, out, in_, func=ACT.Copy, **kw):
                return nc.scalar.activation(out, in_, func, **kw)

            def take(*key):
                act.wait_ge(*upto("product", *key))
                return psum(*key)

            def inverse_root(*key, n):
                act.wait_ge(*upto("mean_square", *key))
                nc.scalar.activation(lnm[:, 0:n], ms[:, 0:n], ACT.Ln).then_inc(*made("log_taken", *key))
                act.wait_ge(*made_now("log_taken"))
                nc.scalar.activation(rs[:, 0:n], lnm[:, 0:n], ACT.Exp, scale=-0.5).then_inc(*made("root_guess", *key))

            def made_now(name):
                return count.sem(name), count.count[name]

            def modulation(l, j):
                ps = take("mod", l, j)
                nc_ = len(conds_of(l, j))
                nc.scalar.activation(modc[:, l % 2, 4 * j:4 * j + 4, 0:nc_],
                                     ps[:, 0:8].rearrange("p (c i) -> p c i", i=2)[:, :, 0:nc_], ACT.Copy) \
                    .then_inc(*made("drained_act", "mod", l, j))

            def squares(l, st, tiles):
                for n, t in enumerate(tiles):
                    if st == "mix" and l == 0:
                        act.wait_ge(*upto("x_in"))
                    elif st == "mix" and l == 2:
                        act.wait_ge(*upto("final", 1))
                    elif st == "ffn":
                        act.wait_ge(*drained("x1", l, 1, t))
                    else:
                        m = l if st == "final" else l - 1
                        act.wait_ge(*drained("x2", m, 1, tiles_of(m, "ffn")[-1]))
                    if n >= 2:
                        act.wait_ge(*upto("squared", l, st, tiles[n - 2]))
                    nc.scalar.activation(XN[:, t % 2, :], X[:, t, :], ACT.Square, accum_out=lsum[:, 0, t:t + 1]) \
                        .then_inc(*made("squared", l, st, t))
                inverse_root(l, st, n=len(tiles))

            def norm_take(l, st):
                act.wait_ge(*upto("scales", l, st))
                base = 0 if st == "mix" else 24
                for t in tiles_of(l, st):
                    i = cond_of_tile(t) if l < 2 else 0
                    for b in range(2):
                        ps = take("h", l, st, t, b)
                        for c in range(4):
                            k = 4 * b + c
                            last = nc.scalar.activation(HT[:, k, P * t:P * t + P], ps[:, P * c:P * c + P], ACT.Identity,
                                                        scale=scl[:, i, k:k + 1], bias=modc[:, l % 2, base + k, i:i + 1])
                        last.then_inc(*made("drained_act", "h", l, st, t, b))

            def project(l):
                for n, (j, t) in enumerate(proj_jobs(l)):
                    if n % 2 == 0:
                        ps = take("u", l, j, t)
                        a, b = cols_of(l, t, *col_groups(l)[j])
                        nc.scalar.activation(U[:, t, a:b], ps[:, 0:b - a], ACT.Copy).then_inc(*made("drained_act", "u", l, j, t))

            def fourier(l, g):
                for d in range(2):
                    ps = take("fa", l, g, d)
                    nc.scalar.activation(FA[:, d, :], ps[:, :], ACT.Copy).then_inc(*made("drained_act", "fa", l, g, d))
                ps = take("ff", l, g)
                nc.scalar.activation(HT[:, 0:2, N * g:N * g + N], ps[:, :].rearrange("p (c n) -> p c n", c=2), ACT.Copy) \
                    .then_inc(*made("drained_act", "ff", l, g))

            def head_turns(l):
                for t in tiles_of(l, "mix"):
                    if l < 2:
                        inverse_root(l, "heads", t, n=10 if (l == 0 or t < 2) else 2)
                    nq = HEADS_Q[l] // 2 if (l != 1 or t < 2) else 0
                    for b in range(0, nq, 4):
                        ps = take("qT", l, t, b)
                        nc.scalar.activation(QT[l][:, b:b + 4, P * t:P * t + P], ps[:, :].rearrange("p (k c) -> p k c", k=4),
                                             ACT.Copy, scale=1.0 if l < 2 else 0.125) \
                            .then_inc(*made("drained_act", "qT", l, t, b))
                    for b in range(0, HEADS_K[l], 4):
                        n = min(4, HEADS_K[l] - b)
                        ps = take("kT", l, t, b)
                        nc.scalar.activation(KT[l][:, b:b + n, P * t:P * t + P],
                                             ps[:, 0:P * n].rearrange("p (k c) -> p k c", k=n), ACT.Copy) \
                            .then_inc(*made("drained_act", "kT", l, t, b))

            def attention(l):
                units = attention_units(l)
                groups = out_groups(l)

                def probs(n):
                    u = units[n]
                    g = groups.index(u["og"])
                    act.wait_ge(*upto("maximum", l, n))
                    if n >= 2:
                        for b in range((units[n - 2]["size"] + 511) // 512):
                            act.wait_ge(*upto("product", "pt", l, n - 2, b))
                    src = SB[:, n % 2, 0:u["size"]] if u["bias"] else psum("sc", l, n, 0)[:, 0:u["size"]]
                    col = u["oc"]
                    if u["oc"] == 0 and g >= 2:
                        act.wait_ge(*upto("attended", l, g - 2))
                    nc.scalar.activation(PB[:, n % 2, 0:u["size"]], src, ACT.Exp, bias=nmax[:, g % 2, col:col + 1],
                                         accum_out=lsum[:, g % 2, col:col + 1]) \
                        .then_inc(*made("probs", l, n))
                    if l == 2:
                        h = u["h"]
                        nc.scalar.activation(sinke[:, g % 2, col:col + 1], sinkn[:, h:h + 1], ACT.Exp, scale=-1.0,
                                             bias=nmax[:, g % 2, col:col + 1]).then_inc(*made("sink_term", l, n))

                def take_turned(n):
                    u = units[n]
                    for b in range((u["size"] + 511) // 512):
                        if (n + b) % 2 == 0 or u["size"] == 512:
                            w = min(512, u["size"] - 512 * b)
                            ps = take("pt", l, n, b)
                            if n >= 2:
                                act.wait_ge(*upto("valued", l, n - 2))
                            nc.scalar.activation(PT[:, n % 2, 512 * b:512 * b + w], ps[:, 0:w], ACT.Copy) \
                                .then_inc(*made("drained_act", "pt", l, n, b))

                for n in range(len(units) + 1):
                    if n < len(units):
                        probs(n)
                    if n >= 1:
                        take_turned(n - 1)

            def recurrence(l):
                steps = scan_steps(l)

                def gates(n):
                    s, t, d, has_out = steps[n]
                    act.wait_ge(*upto("gate_in", l, s))
                    nc.scalar.activation(HE, HS, ACT.Exp, scale=-1.0).then_inc(*made("gate_exp", l, s))
                    act.wait_ge(*upto("gates", l, s))
                    nc.scalar.activation(LF[:, s % 2], HS, ACT.Ln).then_inc(*made("decays", l, s))

                gates(0)
                for n, (s, t, d, has_out) in enumerate(steps):
                    if n + 1 < len(steps):
                        gates(n + 1)
                    if has_out:
                        if (s, t) in ((4, 0), (5, 1)) or (l == 0 and s < 2):
                            ps = take("qt2", l, t)
                            nc.scalar.activation(QT2[:, t], ps[:, 0:256].rearrange("p (k c) -> p k c", k=2), ACT.Copy) \
                                .then_inc(*made("drained_act", "qt2", l, t))
                        ps = take("kt2", l, s)
                        nc.scalar.activation(KT2, ps[:, 0:256].rearrange("p (k c) -> p k c", k=2), ACT.Copy) \
                            .then_inc(*made("drained_act", "kt2", l, s))
                        for p in range(2):
                            for b in range(2):
                                ps = take("e", l, s, p, b)
                                nc.scalar.activation(HW[:, p, 512 * b:512 * b + 512], ps[:, :], ACT.Exp) \
                                    .then_inc(*made("drained_act", "e", l, s, p, b))
                    if s < 6:
                        ps = take("sf", l, s)
                        if s:
                            act.wait_ge(*drained("su", l, s - 1))
                        nc.scalar.activation(SF, ps[:, 0:258], ACT.Exp).then_inc(*made("drained_act", "sf", l, s))
                for t in tiles_of(l, "ffn"):
                    inverse_root(l, "scan", t, n=4)
                    act.wait_ge(*upto("gain_done", l, t))
                    act.wait_ge(*drained("u", l, 4, t))
                    nc.scalar.activation(HE, U[:, t, OFF_G:OFF_G + 256], ACT.Exp, scale=-1.0).then_inc(*made("silu_exp", l, t))

            def mixed_turns(l):
                for t in tiles_of(l, "ffn"):
                    for b, (k0, cols) in enumerate(mix_banks(l)):
                        n = len(cols)
                        ps = take("m", l, t, b)
                        nc.scalar.activation(HT[:, k0:k0 + n, P * t:P * t + P],
                                             ps[:, 0:P * n].rearrange("p (k c) -> p k c", k=n), ACT.Copy) \
                            .then_inc(*made("drained_act", "m", l, t, b))

            def gate_rows(l, st):
                for i in range(2 if l == 0 else 1):
                    for h in range(2):
                        ps = take("g", l, st, i, h)
                        if st == "ffn":
                            act.wait_ge(*drained("x1", l, 1, tiles_of(l, "ffn")[-1]))
                        nc.scalar.activation(grow[:, i, 512 * h:512 * h + 512], ps[:, :], ACT.Copy) \
                            .then_inc(*made("drained_act", "g", l, st, i, h))

            def feed_forward(l):
                n = P * len(tiles_of(l, "ffn"))
                for fp in range(NF // 2):
                    for f in (2 * fp, 2 * fp + 1):
                        ps = take("gate", l, f)
                        nc.scalar.activation(AT[:, f, 0:n], ps[:, 0:n], ACT.Silu).then_inc(*made("drained_act", "gate", l, f))
                    if fp >= 1:
                        for c in ada_beside(l, fp - 1):
                            modulation(*c)
                for c in ada_beside(l, NF // 2 - 1):
                    modulation(*c)

            act.wait_ge(*upto("cond_in"))
            nc.scalar.activation(condt[:, 0, :], cond[:, :, :].rearrange("p i k -> p (i k)"), ACT.Exp, scale=-1.0) \
                .then_inc(*made("cond_exp"))
            for j in range(ADA):
                modulation(0, j)
            for l in range(4):
                squares(l, "mix", tiles_of(l, "mix"))
                norm_take(l, "mix")
                project(l)
                if l < 2:
                    if l == 1:
                        act.wait_ge(*upto("logits_less"))
                        nc.scalar.activation(LOGIT, LOGIT, ACT.Exp).then_inc(*made("logits_exp"))
                    for g in range(2 if l == 0 else 1):
                        fourier(l, g)
                head_turns(l)
                attention(l)
                if l < 2:
                    recurrence(l)
                mixed_turns(l)
                gate_rows(l, "mix")
                gate_rows(l, "ffn")
                squares(l, "ffn", tiles_of(l, "ffn"))
                norm_take(l, "ffn")
                feed_forward(l)
                if l in (1, 3):
                    squares(l, "final", X_TILES)

        @block.vector
        def _(dve):
            V = nc.vector

            def link(ins):
                ins.then_inc(*made("dve_link"))
                dve.wait_ge(count.sem("dve_link"), count.count["dve_link"])

            def take(*key):
                dve.wait_ge(*upto("product", *key))
                return psum(*key)

            def ada_sum(l, j):
                n = ada_chunks.index((l, j))
                dve.wait_ge(*upto(f"ada_weights{n % 2}", l, j))
                if n >= 2:
                    dve.wait_ge(*upto("product", "mod", *ada_chunks[n - 2]))
                w = AW[n % 2][:, 0:4096].rearrange("p (k c) -> p k c", k=8)
                cs = conds_of(l, j)
                for i in range(len(cs)):
                    last = V.tensor_scalar(ACC[:, n % 2, i, :], w[:, 0, :], cond[:, cs[i], 0:1], None, ALU.mult)
                    if i < len(cs) - 1:
                        continue
                link(last)
                for k in range(1, 8):
                    for i in range(len(cs)):
                        a = ACC[:, n % 2, i, :]
                        last = V.scalar_tensor_tensor(out=a, in0=w[:, k, :], scalar=cond[:, cs[i], k:k + 1], in1=a,
                                                      op0=ALU.mult, op1=ALU.add)
                    if k < 7:
                        link(last)
                last.then_inc(*made("ada_sum", l, j))

            def refine(*key, n):
                dve.wait_ge(*upto("root_guess", *key))
                link(V.tensor_tensor(nw[:, 0:n], rs[:, 0:n], rs[:, 0:n], ALU.mult))
                link(V.tensor_tensor(nw[:, 0:n], nw[:, 0:n], ms[:, 0:n], ALU.mult))
                link(V.tensor_scalar(nw[:, 0:n], nw[:, 0:n], -0.5, 1.5, ALU.mult, ALU.add))
                link(V.tensor_tensor(rs[:, 0:n], rs[:, 0:n], nw[:, 0:n], ALU.mult))

            def row_norms(l, st, tiles):
                for t in tiles:
                    dve.wait_ge(*upto("squared", l, st, t))
                n = len(tiles)
                V.tensor_scalar(ms[:, 0:n], lsum[:, 0, 0:n], 1.0 / D, EPS, ALU.mult, ALU.add) \
                    .then_inc(*made("mean_square", l, st))
                refine(l, st, n=n)

            def scales(l, st):
                base = 8 if st == "mix" else 32
                n = len(conds_of(l, 2 if st == "mix" else 8))
                for j in range(ADA):
                    dve.wait_ge(*drained("mod", l, j))
                src = modc[:, l % 2, base:base + 8, 0:n].rearrange("p k i -> p i k")
                if l < 2:
                    V.tensor_scalar(scl[:, 0:n, :], src, 1.0, None, ALU.add).then_inc(*made("scales", l, st))
                else:
                    dve.wait_ge(*upto("gains2_in"))
                    link(V.tensor_scalar(scl[:, 0:n, :], src, 1.0, None, ALU.add))
                    V.tensor_tensor(scl[:, 0, :], scl[:, 0, :], gcol[:, 2 * (l - 2) + (st == "ffn"), :], ALU.mult) \
                        .then_inc(*made("scales", l, st))

            def norm(l, st):
                tiles = tiles_of(l, st)
                if st == "ffn":
                    dve.wait_ge(*drained("h", l, "mix", tiles_of(l, "mix")[-1], 1))
                elif l:
                    dve.wait_ge(*drained("h", l - 1, "ffn", tiles_of(l - 1, "ffn")[-1], 1))
                scales(l, st)
                row_norms(l, st, tiles)
                for n, t in enumerate(tiles):
                    if n >= 2:
                        dve.wait_ge(*upto("product", "h", l, st, tiles[n - 2], 1))
                    V.tensor_scalar(XN[:, t % 2, :], X[:, t, :], rs[:, t:t + 1], None, ALU.mult) \
                        .then_inc(*made("normed", l, st, t))

            def project(l):
                for n, (j, t) in enumerate(proj_jobs(l)):
                    if n % 2 == 1:
                        ps = take("u", l, j, t)
                        a, b = cols_of(l, t, *col_groups(l)[j])
                        V.tensor_copy(U[:, t, a:b], ps[:, 0:b - a]).then_inc(*made("drained_dve", "u", l, j, t))

            def need_u(l, t, a, b):
                for j, (a0, b0) in enumerate(col_groups(l)):
                    if a < b0 and a0 < b:
                        dve.wait_ge(*drained("u", l, j, t))

            def fourier(l, g):
                ps = take("fy", l, g)
                V.tensor_copy(FY, ps[:, :].rearrange("p (d n) -> p d n", d=2)).then_inc(*made("drained_dve", "fy", l, g))

            def gains(l):
                dve.wait_ge(*upto("gains_in", l))
                V.tensor_scalar(G10[:, 0:8, :], GROW3[:, 0, :].unsqueeze(1).broadcast_to([P, 8, DH]), 0.125, None, ALU.mult)
                link(V.tensor_copy(G10[:, 8:10, :], GROW3[:, 1, :].unsqueeze(1).broadcast_to([P, 2, DH])))
                if l == 0:
                    dve.wait_ge(*upto("tables_in"))
                    V.memset(lb[:, :, :], 0.0)
                    link(V.memset(oml[:, :, :], 1.0))
                    return
                dve.wait_ge(*upto("logits_in"))
                link(V.tensor_tensor(lb[:, :, :], LOGIT[:, :, 0, :], LOGIT[:, :, 1, :], ALU.max))
                V.tensor_tensor(LOGIT, LOGIT, lb[:, :, :].unsqueeze(2).broadcast_to([P, 2, 2, 256]), ALU.subtract) \
                    .then_inc(*made("logits_less"))
                dve.wait_ge(*upto("logits_exp"))
                link(V.tensor_tensor(oml[:, :, :], LOGIT[:, :, 0, :], LOGIT[:, :, 1, :], ALU.add))
                link(V.reciprocal(oml[:, :, :], oml[:, :, :]))
                link(V.tensor_tensor(lb[:, :, :], LOGIT[:, :, 1, :], oml[:, :, :], ALU.mult))
                link(V.tensor_scalar(oml[:, :, :], lb[:, :, :], -1.0, 1.0, ALU.mult, ALU.add))

            def heads(l):
                tiles = tiles_of(l, "mix")
                for n, t in enumerate(tiles):
                    if l >= 2:
                        nk, c = HEADS_K[l], DH * HEADS_Q[l]
                        need_u(l, t, c, c + DH * nk)
                        if n:
                            dve.wait_ge(*upto("product", "kT", l, tiles[n - 1], 4 * ((nk - 1) // 4)))
                        V.tensor_copy(KDUP[:, 0:P * nk].rearrange("p (k a c) -> p k a c", k=nk, a=2),
                                      U[:, t, c:c + DH * nk].rearrange("p (k c) -> p k c", k=nk)
                                      .unsqueeze(2).broadcast_to([P, nk, 2, DH])).then_inc(*made("heads_ready", l, t))
                        continue
                    has_q = l == 0 or t < 2
                    nh, c = (10, OFF_Q) if has_q else (2, OFF_K)
                    g0 = 10 - nh
                    need_u(l, t, c, OFF_V)
                    if n:
                        dve.wait_ge(*upto("product", "kT", l, tiles[n - 1], 0))
                    u = U[:, t, c:c + DH * nh].rearrange("p (h c) -> p h c", h=nh)
                    qn = QN[:, 0:DH * nh].rearrange("p (h c) -> p h c", h=nh)
                    qm = QM[:, 0:DH * nh].rearrange("p (h c) -> p h c", h=nh)
                    link(V.tensor_tensor(qn, u, u, ALU.mult))
                    link(V.tensor_reduce(nw[:, 0:nh], qn, AX.X, ALU.add))
                    V.tensor_scalar(ms[:, 0:nh], nw[:, 0:nh], 1.0 / DH, EPS, ALU.mult, ALU.add) \
                        .then_inc(*made("mean_square", l, "heads", t))
                    refine(l, "heads", t, n=nh)
                    link(V.tensor_tensor(qn, u, rs[:, 0:nh].unsqueeze(2).broadcast_to([P, nh, DH]), ALU.mult))
                    link(V.tensor_tensor(qn, qn, G10[:, g0:10, :], ALU.mult))
                    if t < 2:
                        v = QN.rearrange("p (h a s c) -> p h a s c", h=10, a=2, s=2)
                        w = QR.rearrange("p (h a s c) -> p h a s c", h=10, a=2, s=2)
                        sn = tb_sin[:, t, :].rearrange("p (a s c) -> p a s c", a=2, s=2)
                        for s in range(2):
                            V.tensor_tensor(w[:, :, :, s, :], v[:, :, :, 1 - s, :],
                                            sn[:, :, s, :].unsqueeze(1).broadcast_to([P, 10, 2, 16]), ALU.mult)
                        link(V.tensor_tensor(qm, qn, tb_cos[:, t, :].unsqueeze(1).broadcast_to([P, 10, DH]), ALU.mult))
                        link(V.tensor_tensor(qn, qm, QR.rearrange("p (h c) -> p h c", h=10), ALU.add))
                    V.tensor_copy(KDUP[:, 0:256].rearrange("p (k a c) -> p k a c", k=2, a=2),
                                  qn[:, nh - 2:nh, :].unsqueeze(2).broadcast_to([P, 2, 2, DH])) \
                        .then_inc(*made("heads_ready", l, t))

            def attention(l):
                units = attention_units(l)
                groups = out_groups(l)
                if l == 2:
                    dve.wait_ge(*upto("dist_in"))
                    link(V.tensor_scalar(sinkn[:, :], sinkn[:, :], -1.0, None, ALU.mult))

                def maximum(n):
                    u = units[n]
                    g, col = groups.index(u["og"]), u["oc"]
                    nm = nmax[:, g % 2, col:col + 1]
                    for b in range((u["size"] + 511) // 512):
                        take("sc", l, n, b)
                    if n >= 2:
                        dve.wait_ge(*upto("probs", l, n - 2))
                    if u["oc"] == 0 and g >= 2:
                        dve.wait_ge(*upto("attended", l, g - 2))
                    if u["bias"] is None:
                        V.tensor_reduce(nm, psum("sc", l, n, 0)[:, 0:u["size"]], AX.X, ALU.max, negate=True) \
                            .then_inc(*made("maximum", l, n))
                        return
                    for i, (g_, slope) in enumerate(u["bias"]):
                        at = u["keys"][i][4]
                        last = V.scalar_tensor_tensor(out=SB[:, n % 2, at:at + N], in0=DIST[:, g_, u["t"], :], scalar=slope,
                                                      in1=psum("sc", l, n, at // 512)[:, at % 512:at % 512 + N],
                                                      op0=ALU.mult, op1=ALU.add)
                        if at % 512 == 256 or i == len(u["bias"]) - 1:
                            last.then_inc(*made("drained_dve", "sc", l, n, at // 512))
                    dve.wait_ge(*count_now("drained_dve"))
                    last = V.tensor_reduce(nm, SB[:, n % 2, 0:u["size"]], AX.X, ALU.max, negate=True)
                    if l == 2:
                        link(last)
                        last = V.tensor_tensor(nm, nm, sinkn[:, u["h"]:u["h"] + 1], ALU.min)
                    last.then_inc(*made("maximum", l, n))

                def take_turned(n):
                    u = units[n]
                    for b in range((u["size"] + 511) // 512):
                        if not ((n + b) % 2 == 0 or u["size"] == 512):
                            w = min(512, u["size"] - 512 * b)
                            ps = take("pt", l, n, b)
                            if n >= 2:
                                dve.wait_ge(*upto("valued", l, n - 2))
                            V.tensor_copy(PT[:, n % 2, 512 * b:512 * b + w], ps[:, 0:w]).then_inc(*made("drained_dve", "pt", l, n, b))

                def normalise(n):
                    u = units[n]
                    g = groups.index(u["og"])
                    dve.wait_ge(*upto("valued", l, n))
                    if l == 2:
                        dve.wait_ge(*upto("sink_term", l, n))
                        link(V.tensor_tensor(lsum[:, g % 2, 0:8], lsum[:, g % 2, 0:8], sinke[:, g % 2, 0:8], ALU.add))
                    link(V.reciprocal(rinv[:, :], lsum[:, g % 2, 0:8]))
                    c = OUT_COL[l] + 512 * u["og"][1]
                    V.tensor_tensor(U[:, u["t"], c:c + 512].rearrange("p (h c) -> p h c", h=8),
                                    obank[g % 2][:, :].rearrange("p (h c) -> p h c", h=8),
                                    rinv[:, :].unsqueeze(2).broadcast_to([P, 8, DH]), ALU.mult) \
                        .then_inc(*made("attended", l, g))

                for n in range(len(units) + 3):
                    if n < len(units):
                        maximum(n)
                    if 1 <= n <= len(units):
                        take_turned(n - 1)
                    if n >= 3 and units[n - 3]["oc"] == 7:
                        normalise(n - 3)

            def count_now(name):
                return count.sem(name), count.count[name]

            def recurrence(l):
                steps = scan_steps(l)
                link(V.memset(ST, 0.0))

                def gates(n):
                    s, t, d, has_out = steps[n]
                    need_u(l, t, OFF_Z + 256 * d, OFF_Z + 256 * d + 256)
                    kk = HK[:, s % 2]
                    if n:
                        dve.wait_ge(*upto("decays", l, s - 1))
                    V.tensor_scalar(HS, U[:, t, OFF_Z + 256 * d:OFF_Z + 256 * d + 256], -80.0, None, ALU.max) \
                        .then_inc(*made("gate_in", l, s))
                    dve.wait_ge(*upto("gate_exp", l, s))
                    link(V.tensor_scalar(HS, HE, 1.0, None, ALU.add))
                    link(V.reciprocal(HS, HS))
                    if l:
                        link(V.tensor_tensor(HS, HS, oml[:, d, :], ALU.mult))
                    last = V.tensor_tensor(kk, HS, HE, ALU.mult)
                    if l:
                        link(last)
                        last = V.tensor_tensor(HS, HS, lb[:, d, :], ALU.add)
                    last.then_inc(*made("gates", l, s))

                gates(0)
                for n, (s, t, d, has_out) in enumerate(steps):
                    kk = HK[:, s % 2]
                    if n + 1 < len(steps):
                        gates(n + 1)
                    if has_out:
                        dve.wait_ge(*drained("qt2", l, t))
                        dve.wait_ge(*drained("kt2", l, s))
                        for p in range(2):
                            for b in range(2):
                                dve.wait_ge(*drained("e", l, s, p, b))
                            if p == 1 and s >= 2:
                                dve.wait_ge(*upto("carried", l, s, 0))
                            if p == 1:
                                dve.wait_ge(*upto("product", "a", l, s, 0, 1, 1))
                            w = HW[:, p, :].rearrange("p (j c) -> p j c", j=8)
                            V.tensor_tensor(QW.rearrange("p (j c) -> p j c", j=8), w,
                                            QT2[:, t, p, :].unsqueeze(1).broadcast_to([P, 8, P]), ALU.mult)
                            V.tensor_tensor(KW.rearrange("p (j c) -> p j c", j=7), w[:, 0:7, :],
                                            KT2[:, p, :].unsqueeze(1).broadcast_to([P, 7, P]), ALU.mult) \
                                .then_inc(*made("weighed", l, s, p))
                            for hh in range(2):
                                if p == 1:
                                    dve.wait_ge(*upto("read_out", l, s, 0, hh))
                                for b in range(2):
                                    ps = take("a", l, s, p, hh, b)
                                    V.tensor_tensor(AM[:, hh, 512 * b:512 * b + 512], ps[:, :],
                                                    tb_masks[:, d, 512 * b:512 * b + 512], ALU.mult) \
                                        .then_inc(*made("drained_dve", "a", l, s, p, hh, b))
                        dve.wait_ge(*upto("read_out", l, s, 1, 1))
                        o = obank[s % 2][:, 0:256]
                        visited = any(t2 == t and s2 < s and o2 for s2, t2, _, o2 in steps)
                        if visited:
                            for s2, t2, _, o2 in steps:
                                if t2 == t and s2 < s:
                                    dve.wait_ge(*upto("scanned", l, s2))
                            V.tensor_tensor(OS[:, t, :], o, OS[:, t, :], ALU.add).then_inc(*made("scanned", l, s))
                        else:
                            V.tensor_copy(OS[:, t, :], o).then_inc(*made("scanned", l, s))
                    if s < 6:
                        dve.wait_ge(*drained("sf", l, s))
                        V.tensor_tensor(KS, kk, SF[:, 0:256], ALU.mult).then_inc(*made("tailed", l, s))
                        ps = take("su", l, s)
                        for p in range(2):
                            for hh in range(2):
                                r = slice(DH * hh, DH * hh + DH)
                                a = ST[r, d, p, DH * hh:DH * hh + DH]
                                last = V.scalar_tensor_tensor(out=a, in0=a, scalar=SF[r, 256 + p:257 + p],
                                                              in1=ps[r, P * p + DH * hh:P * p + DH * hh + DH],
                                                              op0=ALU.mult, op1=ALU.add)
                        last.then_inc(*made("drained_dve", "su", l, s))
                for t in tiles_of(l, "ffn"):
                    o4 = OS[:, t, :].rearrange("p (h c) -> p h c", h=4)
                    for s, t2, _, o2 in steps:
                        if t2 == t and o2:
                            dve.wait_ge(*upto("scanned", l, s))
                    hs4 = HS.rearrange("p (h c) -> p h c", h=4)
                    link(V.tensor_tensor(hs4, o4, o4, ALU.mult))
                    link(V.tensor_reduce(nw[:, 0:4], hs4, AX.X, ALU.add))
                    V.tensor_scalar(ms[:, 0:4], nw[:, 0:4], 1.0 / DH, EPS, ALU.mult, ALU.add) \
                        .then_inc(*made("mean_square", l, "scan", t))
                    refine(l, "scan", t, n=4)
                    link(V.tensor_tensor(hs4, o4, rs[:, 0:4].unsqueeze(2).broadcast_to([P, 4, DH]), ALU.mult))
                    V.tensor_tensor(hs4, hs4, GROW3[:, 2, :].unsqueeze(1).broadcast_to([P, 4, DH]), ALU.mult) \
                        .then_inc(*made("gain_done", l, t))
                    dve.wait_ge(*upto("gain_done", l, t))
                    dve.wait_ge(*upto("silu_exp", l, t))
                    need_u(l, t, OFF_G, OFF_G + 256)
                    g = U[:, t, OFF_G:OFF_G + 256]
                    link(V.tensor_scalar(HE, HE, 1.0, None, ALU.add))
                    link(V.reciprocal(HE, HE))
                    link(V.tensor_tensor(HE, HE, g, ALU.mult))
                    V.tensor_tensor(g, HE, HS, ALU.mult).then_inc(*made("mixed", l, t))
                    dve.wait_ge(*upto("mixed", l, t))

            def gate_rows(l, st):
                base = 16 if st == "mix" else 40
                for i in range(2 if l == 0 else 1):
                    for h in range(2):
                        if h or i:
                            dve.wait_ge(*upto("product", "g", l, st, i if h else i - 1, 1 - h))
                        elif st == "ffn":
                            dve.wait_ge(*upto("product", "g", l, "mix", 1 if l == 0 else 0, 1))
                        for c in range(4):
                            k = base + 4 * h + c
                            last = V.tensor_scalar(DIAG[:, c, :], ident[:, :], modc[:, l % 2, k, i:i + 1], None, ALU.mult)
                        last.then_inc(*made("diagonal", l, st, i, h))

            def add_up(name, l):
                st = "mix" if name == "x1" else "ffn"
                for h in range(2):
                    for t in tiles_of(l, "ffn"):
                        i = cond_of_tile(t) if l < 2 else 0
                        dve.wait_ge(*drained("g", l, st, i, h))
                        ps = take(name, l, h, t)
                        link(V.tensor_tensor(ps[:, :], ps[:, :], grow[:, i, 512 * h:512 * h + 512], ALU.mult))
                        x = X[:, t, 512 * h:512 * h + 512]
                        V.tensor_tensor(x, ps[:, :], x, ALU.add).then_inc(*made("drained_dve", name, l, h, t))

            def feed_forward(l):
                n = P * len(tiles_of(l, "ffn"))
                for fp in range(NF // 2):
                    for f in (2 * fp, 2 * fp + 1):
                        ps = take("up", l, f)
                        dve.wait_ge(*drained("gate", l, f))
                        V.tensor_tensor(AT[:, f, 0:n], ps[:, 0:n], AT[:, f, 0:n], ALU.mult) \
                            .then_inc(*made("drained_dve", "up", l, f))
                    for c in ada_beside(l, fp):
                        ada_sum(*c)

            dve.wait_ge(*upto("ident_in"))
            dve.wait_ge(*upto("cond_exp"))
            flat = cond[:, :, :].rearrange("p i k -> p (i k)")
            link(V.tensor_scalar(condt[:, 0, :], condt[:, 0, :], 1.0, None, ALU.add))
            link(V.reciprocal(condt[:, 1, :], condt[:, 0, :]))
            link(V.tensor_tensor(flat, flat, condt[:, 1, :], ALU.mult))
            for j in range(ADA):
                ada_sum(0, j)
            for l in range(4):
                norm(l, "mix")
                project(l)
                if l < 2:
                    gains(l)
                    for g in range(2 if l == 0 else 1):
                        fourier(l, g)
                heads(l)
                attention(l)
                if l < 2:
                    recurrence(l)
                gate_rows(l, "mix")
                add_up("x1", l)
                gate_rows(l, "ffn")
                norm(l, "ffn")
                feed_forward(l)
                add_up("x2", l)
                if l in (1, 3):
                    row_norms(l, "final", X_TILES)
                    dve.wait_ge(*upto("final_gain_in", l))
                    for t in X_TILES:
                        last = V.scalar_tensor_tensor(out=X[:, t, :], in0=X[:, t, :], scalar=rs[:, t:t + 1],
                                                      in1=grow[:, 0, :], op0=ALU.mult, op1=ALU.mult)
                    last.then_inc(*made("final", l))

        return count


_INS = ["x", "c", "ctx", "c_ctx", "w_ada", "b_ada", "w_in", "w_four", "q_norm", "k_norm", "hg_lb_logits", "hg_norm",
        "w_out", "w_gate", "w_up", "w_down", "final_norm", "c_2", "ada_w_2", "ada_b_2", "norm_mix_2", "norm_ffn_2",
        "ffn_w_in_2", "ffn_w_out_2", "a_w_in_2", "a_w_out_2", "a_sink_2", "b_w_in_2", "b_w_out_2", "final_norm_2"]


def kernel(**inputs):
    import ml_dtypes
    import concourse.bacc as bacc
    from concourse.bass_utils import run_bass_kernel_spmd as run

    consts = tables()
    consts["t_masks"] = consts["t_masks"].astype(ml_dtypes.bfloat16)
    arrays = {f"in_{n}": np.ascontiguousarray(inputs[n]) for n in _INS}
    arrays.update({f"in_{n}": a for n, a in consts.items()})
    counts = None
    for _ in range(2):
        nc = bacc.Bacc("TRN2", target_bir_lowering=False, num_devices=1)
        io = {n[3:]: nc.dram_tensor(n, a.shape, mybir.dt.from_np(a.dtype), kind="ExternalInput").ap()
              for n, a in arrays.items()}
        io["out"] = nc.dram_tensor("out_0", (1, N, D), F32, kind="ExternalOutput").ap()
        counts = block_kernel(nc, io, counts)
    r = run(nc, [arrays], core_ids=[0])
    return r.results[0]["out_0"]
```

```python
from contextlib import ExitStack

import numpy as np

import concourse.bass as bass
from concourse import mybir

P = 128
F32 = mybir.dt.float32
F32R = mybir.dt.float32r
U8 = mybir.dt.uint8
ALU = mybir.AluOpType
ACT = mybir.ActivationFunctionType
AX = mybir.AxisListType

D = 1024
KD = D // P
N = 256
DH = 64
FF = 2816
NF = FF // P
EPS = 1e-6
PROJ = [2304, 2304, 1536, 2304]
OFF_Q, OFF_K, OFF_V, OFF_Z, OFF_I, OFF_HQ, OFF_G = 256, 768, 896, 1024, 1536, 1792, 2048
LEVELS = 7
RAW = 4
HIGH = 3
SLOT = KD * 256
NBANKS = 6
X_TILES, C_TILES = (0, 1), (2, 3)
ADA = 24
GROUPS_B = ((128, 1), (512, 4), (2048, 16))


def level_matrices():
    i = np.arange(P)
    sums, tails, masks = [], [], []
    for h in (1 << j for j in range(LEVELS)):
        mid = (i // (2 * h)) * 2 * h + h
        second = (i % (2 * h)) >= h
        r, c = i[:, None], i[None, :]
        fwd = second[None, :] & (r >= mid[None, :]) & (r <= c)
        back = ~second[None, :] & (r > c) & (r < mid[None, :])
        sums.append((fwd | back).astype(np.float32))
        same = (i[:, None] // (2 * h)) == (i[None, :] // (2 * h))
        masks.append((same & ~second[:, None] & second[None, :]).astype(np.float32))
    sums.append((i[:, None] <= i[None, :]).astype(np.float32))
    masks.insert(0, np.eye(P, dtype=np.float32))
    tails = (i[:, None] > i[None, :]).astype(np.float32)
    sums, masks = np.stack(sums, 1), np.stack(masks, 1)
    both = [np.stack([a, a[::-1, ..., ::-1]], 1) for a in (sums, tails, masks)]
    return [np.ascontiguousarray(a.reshape(P, 2, -1)) for a in both]


def rope_tables():
    half = DH // 2
    freqs = (10000.0 ** (-np.arange(0, half, 2, dtype=np.float32) / np.float32(half))).astype(np.float32)
    pos = np.arange(N)
    ang = [(p[:, None].astype(np.float32) * freqs).astype(np.float32) for p in (pos // 64, pos % 64)]
    cos = np.concatenate([np.cos(a) for a in (ang[0], ang[0], ang[1], ang[1])], 1).astype(np.float32)
    sin = np.concatenate([-np.sin(ang[0]), np.sin(ang[0]), -np.sin(ang[1]), np.sin(ang[1])], 1).astype(np.float32)
    return [np.ascontiguousarray(a.reshape(2, P, DH).transpose(1, 0, 2)) for a in (cos, sin)]


def fourier_tables():
    t = 2 * np.pi * (np.outer(np.arange(N), np.arange(N)) % N) / N
    cs = np.concatenate([np.cos(t), np.sin(t)], 1).astype(np.float32).reshape(2, P, 2 * N).transpose(1, 0, 2)
    t = 2 * np.pi * (np.outer(np.arange(DH), np.arange(DH)) % DH) / DH
    cols = [np.kron(np.eye(2), f / 128.0).astype(np.float32) for f in (np.cos(t), -np.sin(t))]
    return np.ascontiguousarray(cs), np.ascontiguousarray(np.stack(cols, 1))


def distance_tables():
    t, s = np.arange(N)[:, None], np.arange(N)[None, :]
    away = np.abs(t - s)
    seen = [away <= P] + [((t - s) % dil == 0) & (away <= window // 2) for window, dil in GROUPS_B]
    out = np.stack([np.where(ok, -away, -1e30) for ok in seen]).astype(np.float32)
    return np.ascontiguousarray(out.reshape(4, 2, P, N).transpose(2, 0, 1, 3))


def slopes(n):
    return [float(x) for x in (2.0 ** (-8.0 * np.arange(1, n + 1) / n)).astype(np.float32)]


def tables():
    sums, tails, masks = level_matrices()
    cos, sin = rope_tables()
    cs, cols = fourier_tables()
    return {"t_sums": sums, "t_tails": tails, "t_masks": masks, "t_cos": cos, "t_sin": sin, "t_cs": cs,
            "t_cols": cols, "t_dist": distance_tables(), "t_ident": np.eye(P, dtype=np.float32)}


def tiles_of(layer, stage):
    if stage == "mix":
        return (0, 1, 2, 3) if layer < 2 else (0, 1)
    return (0, 1, 2, 3) if layer == 0 else (0, 1)


def conds_of(layer, chunk=0):
    if layer >= 2:
        return (2,)
    return (0, 1) if layer == 0 or chunk < 8 else (0,)


def cond_of_tile(t):
    return 0 if t < 2 else 1


def col_groups(layer):
    return [(a, a + 256) for a in range(0, PROJ[layer], 256)]


def cols_of(layer, t, a, b):
    if layer == 1 and t >= 2:
        a, b = max(a, OFF_K), min(b, OFF_HQ)
    return (a, b) if a < b else None


def proj_jobs(layer):
    return [(j, t) for j, (a, b) in enumerate(col_groups(layer)) for t in tiles_of(layer, "mix") if cols_of(layer, t, a, b)]


def halves(l):
    return 2 if l == 0 else 1


def hidden_tiles(l, half):
    n = NF // halves(l)
    return range(n * half, n * half + n)


def down_chunks(l, half):
    f = hidden_tiles(l, half)
    return [f[i:i + 4] for i in range(0, len(f), 4)]


def out_loads(l):
    return [(8, 256)] * 4 if l < 3 else [(4, 512)] * 2


def load_plan():
    out = []
    for l in range(4):
        out += [("win", l, j) for j in range(len(col_groups(l)))]
        out += [("wo", l, j) for j in range(len(out_loads(l)))]
        for half in range(halves(l)):
            out += [("gu", l, f) for f in hidden_tiles(l, half)]
            out += [("dn", l, half, h, c) for h in range(2) for c in range(len(down_chunks(l, half)))]
    return out


def ada_plan():
    out = {}
    for j in range(8):
        out[("win", 0, j)] = [(0, 8 + 2 * j), (0, 9 + 2 * j)]
    for l in range(3):
        todo = [(l + 1, j) for j in range(ADA)]
        for key in load_plan():
            if key[1] == l and (key[0] == "dn" or (key[0] == "gu" and (key[2] % 2 == 1 or key[2] == 0))) and todo:
                out[key] = [todo.pop(0)]
        assert not todo
    return out


def attention_units(l):
    out = []
    if l < 2:
        for t in tiles_of(l, "ffn"):
            s = (0, 1, 2, 3) if t < 2 else (2, 3)
            for h in range(8):
                kv = h // 4
                out.append(dict(t=t, h=h, og=(t, 0), oc=h, keys=[(h // 2, kv, s[0] * P, len(s) * P, 0)], half=h % 2,
                                vals=[(i, OFF_V + DH * kv) for i in s], bias=None, size=len(s) * P))
    elif l == 2:
        for t in X_TILES:
            for h in range(16):
                out.append(dict(t=t, h=h, og=(t, h // 8), oc=h % 8, keys=[(h // 2, h // 4, 0, N, 0)], half=h % 2,
                                vals=[(i, 1280 + DH * (h // 4)) for i in X_TILES], bias=[(0, slopes(16)[h])], size=N))
    else:
        for t in X_TILES:
            for h in range(8):
                kv = h // 4
                out.append(dict(t=t, h=h, og=(t, 0), oc=h, half=h % 2, size=3 * N,
                                keys=[((8 * g + h) // 2, 2 * g + kv, 0, N, g * N) for g in range(3)],
                                vals=[(i, 1920 + DH * (2 * g + kv)) for g in range(3) for i in X_TILES],
                                bias=[(1 + g, slopes(24)[8 * g + h]) for g in range(3)]))
    return out


def out_groups(l):
    return list(dict.fromkeys(u["og"] for u in attention_units(l)))


OUT_COL = [OFF_Q, OFF_Q, 0, 0]
HEADS_Q = [8, 8, 16, 24]
HEADS_K = [2, 2, 4, 6]


def mix_banks(l):
    if l < 2:
        return [(2, [OFF_Q + P * i for i in range(4)]), (6, [OFF_G, OFF_G + P])]
    return [(4 * b, [P * (4 * b + i) for i in range(4)]) for b in range(2 if l == 2 else 1)]


KO = [8, 8, 8, 4]


def scan_steps(l):
    order = ((2, 3, 0, 1), (3, 2, 1, 0))
    return [(2 * i + d, order[d][i], d, l == 0 or order[d][i] < 2) for i in range(4) for d in range(2)]


def first_visit(l, s, t):
    return s == min(s2 for s2, t2, _, out in scan_steps(l) if t2 == t and out)


def half_buffer(l, s, p, q):
    n = sum(out for s2, _, _, out in scan_steps(l) if s2 < s)
    return (4 * n + 2 * p + q) % 3


def half_buffer_last(l, s, p, q):
    steps = [s2 for s2, _, _, out in scan_steps(l) if out]
    n = 4 * steps.index(s) + 2 * p + q - 3
    return None if n < 0 else (steps[n // 4], (n % 4) // 2, n % 2)


class Counts:

    def __init__(self, nc, ctx, first=None):
        self.nc, self.ctx, self.first = nc, ctx, first
        self.sems, self.count, self.at = {}, {}, {}
        self.banks, self.tenants = {}, []

    def sem(self, name):
        if name not in self.sems:
            self.sems[name] = self.ctx.enter_context(self.nc.semaphore(name))
        return self.sems[name]

    def made(self, name, *key, by=1):
        self.count[name] = self.count.get(name, 0) + by
        self.at[(name, *key)] = self.count[name]
        return self.sem(name), by

    def upto(self, name, *key):
        return self.sem(name), self.first.at[(name, *key)] if self.first else 1

    def drained(self, *key):
        if not self.first:
            return self.sem("drained_act"), 1
        if key[0] == "sc" and key[1] < 2:
            return self.upto("probs", *key[1:3])
        name = "drained_act" if ("drained_act", *key) in self.first.at else "drained_dve"
        return self.upto(name, *key)


def block_kernel(nc, io, first=None):
    ctx = ExitStack()
    with ctx:
        count = Counts(nc, ctx, first)
        made, upto, drained = count.made, count.upto, count.drained

        base = [-(-nc.sbuf_base // 32) * 32]

        def place(name, offset, shape, dt=F32):
            return nc.alloc_sbuf_tensor_at(name, shape, dt, offset=offset)

        def sb(name, shape, dt=F32):
            offset = base[0]
            n = int(np.prod(shape[1:])) * (1 if dt == U8 else 4)
            base[0] += -(-n // 32) * 32
            return place(name, offset, shape, dt)

        X = sb("X", [P, 4, D])
        HTH = sb("HTH", [P, KD, 512], F32R)
        a1 = base[0]
        A1 = sb("A1", [P, NF * 512])
        a2 = base[0]
        A2 = sb("A2", [P, 11264])
        HTL = place("HTL", a2, [P, KD, 512], F32R)
        hidden = {}
        for n_half in (2, 1):
            shape = [P, NF // n_half, 256 * n_half]
            hidden[n_half] = (place(f"hidden_high{n_half}", a1, shape, F32R),
                              place(f"hidden_low{n_half}", a1 + NF * 256 * 4, shape, F32R))
        LFH = place("LFH", a2 + 4 * 11008, [P, 256], F32R)
        LFL = place("LFL", a1 + 4 * 10560, [P, 256], F32R)
        raw_at = base[0]
        raw = sb("raw", [P, RAW, SLOT])
        wlow = place("wlow", raw_at, [P, RAW, SLOT], F32R)
        whigh = sb("whigh", [P, HIGH, SLOT], F32R)
        dist_at = base[0]
        SUMS = sb("SUMS", [P, 2, 8 * P], F32R)
        DIST = place("DIST", dist_at, [P, 4, 2, N])
        TAILS = sb("TAILS", [P, 2, P], F32R)
        tb_masks = sb("tb_masks", [P, 2, 8, P], U8)
        tb_cols = sb("tb_cols", [P, 2, P])
        tb_cos = sb("tb_cos", [P, 2, DH])
        tb_sin = sb("tb_sin", [P, 2, DH])
        ident = sb("ident", [P, P])
        ones = sb("ones", [P, P])
        lb = sb("lb", [P, 2, 256])
        grow = sb("grow", [P, 2, D])
        cond = sb("cond", [P, 3, 8])
        condt = sb("condt", [P, 2, 24])
        modc = sb("modc", [P, 2, 48, 2])
        scl = sb("scl", [P, 2, 8])
        gcol = sb("gcol", [P, 4, 8])
        ms = sb("ms", [P, 16])
        lnm = sb("lnm", [P, 16])
        rs = sb("rs", [P, 16])
        nw = sb("nw", [P, 16])
        nmax = sb("nmax", [P, 2, 16])
        lsum = sb("lsum", [P, 2, 16])
        sinkn = sb("sinkn", [P, 16])
        sinke = sb("sinke", [P, 2, 16])
        rinv = sb("rinv", [P, 8])
        TOT = sb("TOT", [P, 2, 2])

        U = A1[:, 0:9216].rearrange("p (t c) -> p t c", t=4)
        XN = A1[:, 9216:11264].rearrange("p (b c) -> p b c", b=2)
        W4 = A1[:, 9216:9728].rearrange("p (k c) -> p k c", k=2)
        G10 = A1[:, 9728:10368].rearrange("p (h c) -> p h c", h=10)
        GROW3 = A1[:, 10368:10560].rearrange("p (h c) -> p h c", h=3)
        DIAG = A1[:, 10560:11072].rearrange("p (h c) -> p h c", h=4)

        def cut(start, n):
            return A2[:, start:start + n]

        STAGE = cut(0, 4352)
        G = cut(4096, 1024).rearrange("p (b c) -> p b c", b=2)
        AW = [cut(5632 + 2304 * b, 2304) for b in range(2)]
        ACC = cut(10240, 1024).rearrange("p (b i c) -> p b i c", b=2, i=2)
        TCS = cut(4608, 1024).rearrange("p (k c) -> p k c", k=2)
        FA = cut(6656, 1024).rearrange("p (d c) -> p d c", d=2)
        LOGIT = cut(8192, 1024).rearrange("p (d l c) -> p d l c", d=2, l=2)
        QT = [cut(0, 3072).rearrange("p (k c) -> p k c", c=512 if l < 2 else 256) for l in range(4)]
        KT = [cut(3072, 1536).rearrange("p (k c) -> p k c", c=512 if l < 2 else 256) for l in range(4)]
        SB = cut(4608, 1536).rearrange("p (b c) -> p b c", b=2)
        PB = cut(6144, 1536).rearrange("p (b c) -> p b c", b=2)
        PT = cut(7680, 1536).rearrange("p (b c) -> p b c", b=2)
        KDUP = cut(9216, 768)
        QN, QM = cut(9984, 640), cut(10624, 640)
        QR = cut(4608, 640)
        HW = cut(0, 2304).rearrange("p (b j c) -> p b j c", b=2, j=9)
        QW = cut(2304, 3072).rearrange("p (b j h c) -> p b j h c", b=3, j=4, h=2)
        KW = cut(5376, 2048).rearrange("p (b j c) -> p b j c", b=2, j=8)
        AS = cut(7424, 1024).rearrange("p (d h c) -> p d h c", d=2, h=4)
        QP = cut(8448, 256).rearrange("p (b c) -> p b c", b=2)
        KT2 = cut(8704, 256).rearrange("p (k c) -> p k c", k=2)
        LF, HE, HS, SF = cut(8960, 256), cut(9216, 256), cut(9472, 256), cut(9728, 256)
        ST = cut(9984, 512).rearrange("p (d k c) -> p d k c", d=2, k=2)
        KS, HK = cut(10496, 256), cut(10752, 256)

        def scanned_sum(t):
            return U[:, t, OFF_K:OFF_K + 256]

        def qt2(t):
            return U[:, t, OFF_HQ:OFF_HQ + 256].rearrange("p (k c) -> p k c", k=2)

        bank = [ctx.enter_context(nc.psum_tensor(f"bank{b}", [P, 512], F32)) for b in range(NBANKS + 2)]
        obank = bank[NBANKS:]

        def psum(*key):
            return bank[(first or count).banks.get(key, 0)]

        loads = load_plan()
        index = {key: n for n, key in enumerate(loads)}
        ada_by = ada_plan()

        def load_size(key):
            kind, l = key[:2]
            if kind == "dn":
                return 512 * len(down_chunks(l, key[2])[key[4]])
            return SLOT

        def raw_slot(key):
            return raw[:, index[key] % RAW, 0:load_size(key)]

        def parts(key):
            n = index[key]
            return whigh[:, n % HIGH, 0:load_size(key)], wlow[:, n % RAW, 0:load_size(key)]

        def last_use(key):
            kind, l = key[:2]
            if kind == "win":
                t = [t for j, t in proj_jobs(l) if j == key[2]][-1]
                return upto("product", "u", l, key[2], t)
            if kind == "wo":
                return upto("product", "x1", l, key[2], tiles_of(l, "ffn")[-1])
            if kind == "gu":
                return upto("product", "up", l, key[2])
            if key[4] < len(down_chunks(l, key[2])) - 1:
                return upto("down_part", *key[1:])
            return upto("product", "x2", l, key[2], key[3], tiles_of(l, "ffn")[-1])

        def stage_done(l, st):
            if st == "mix":
                return ("x1", l, len(out_loads(l)) - 1, tiles_of(l, "ffn")[-1])
            return ("x2", l, halves(l) - 1, 1, tiles_of(l, "ffn")[-1])

        ada_chunks = [(l, j) for l in range(4) for j in range(ADA)]

        def ada_w(l):
            w = io["w_ada"][l] if l < 2 else io["ada_w_2"][l - 2]
            b = io["b_ada"][l] if l < 2 else io["ada_b_2"][l - 2]
            return w, b

        block = ctx.enter_context(nc.Block())

        @block.sync
        def _(sp):
            for name, dst, src in (
                ("cond_in", cond[:, 0, :], io["c"][0].rearrange("(p k) -> p k", k=8)),
                ("cond_in", cond[:, 1, :], io["c_ctx"].rearrange("(p k) -> p k", k=8)),
                ("cond_in", cond[:, 2, :], io["c_2"][0].rearrange("(p k) -> p k", k=8)),
                ("ident_in", ident[:, :], io["t_ident"]),
                ("x_in", X[:, 0:2, :], io["x"][0].rearrange("(t p) d -> p t d", p=P)),
                ("x_in", X[:, 2:4, :], io["ctx"][0].rearrange("(t p) d -> p t d", p=P)),
                ("stage_in", STAGE[:, 0:2048], io["t_sums"].rearrange("p d c -> p (d c)")),
                ("stage_in", STAGE[:, 2048:2304], io["t_tails"].rearrange("p d c -> p (d c)")),
                ("stage_in", STAGE[:, 2304:4352], io["t_masks"].rearrange("p d c -> p (d c)")),
                ("tables_in", tb_cols[:, :, :], io["t_cols"]),
                ("tables_in", tb_cos[:, :, :], io["t_cos"]),
                ("tables_in", tb_sin[:, :, :], io["t_sin"]),
            ):
                sp.dma_start(dst, src).then_inc(*made(name, by=16))

            def rows(w, a, n):
                return w[a * P:(a + n) * P, :].rearrange("(k p) c -> p k c", p=P)

            for n, key in enumerate(loads):
                kind, l = key[:2]
                if n >= RAW:
                    sp.wait_ge(*last_use(loads[n - RAW]))
                to = raw_slot(key)
                sem = f"weights{n % RAW}"
                if kind == "win":
                    w = (io["w_in"][l] if l < 2 else io["a_w_in_2"][0] if l == 2 else io["b_w_in_2"][0])
                    a, b = col_groups(l)[key[2]]
                    sp.dma_start(to.rearrange("p (k c) -> p k c", k=KD), rows(w, 0, KD)[:, :, a:b]) \
                        .then_inc(*made(sem, key, by=16))
                elif kind == "wo":
                    w = (io["w_out"][l] if l < 2 else io["a_w_out_2"][0] if l == 2 else io["b_w_out_2"][0])
                    k, c = out_loads(l)[key[2]]
                    sp.dma_start(to.rearrange("p (k c) -> p k c", k=k), rows(w, 0, k)[:, :, c * key[2]:c * key[2] + c]) \
                        .then_inc(*made(sem, key, by=16))
                elif kind == "gu":
                    dst = to.rearrange("p (g k c) -> p g k c", g=2, k=KD)
                    if l < 2:
                        g, u = io["w_gate"][l], io["w_up"][l]
                    else:
                        g, u = io["ffn_w_in_2"][l - 2][:, 0:FF], io["ffn_w_in_2"][l - 2][:, FF:2 * FF]
                    for i, w in enumerate((g, u)):
                        sp.dma_start(dst[:, i], rows(w, 0, KD)[:, :, P * key[2]:P * key[2] + P]) \
                            .then_inc(*made(sem, key, by=16))
                else:
                    w = io["w_down"][l] if l < 2 else io["ffn_w_out_2"][l - 2]
                    f = down_chunks(l, key[2])[key[4]]
                    h = key[3]
                    sp.dma_start(to.rearrange("p (k c) -> p k c", k=len(f)),
                                 rows(w, f[0], len(f))[:, :, 512 * h:512 * h + 512]).then_inc(*made(sem, key, by=16))
            sp.wait_ge(*upto("final", 3))
            sp.dma_start(io["out"][0].rearrange("(t p) d -> p t d", p=P), X[:, 0:2, :]).then_inc(*made("out_written", by=16))
            sp.wait_ge(*upto("out_written"))

        @block.gpsimd
        def _(pool):
            nc.gpsimd.memset(ones[:, :], 1.0).then_inc(*made("ones_set"))

            with nc.allow_non_contiguous_dma(reason="eight gains to a partition"):
                for i in range(2):
                    for k, g in enumerate(("norm_mix_2", "norm_ffn_2")):
                        pool.dma_start(gcol[:, 2 * i + k, :], io[g][i].rearrange("(k p) -> p k", p=P)) \
                            .then_inc(*made("gains2_in", by=16))

            def ada_load(l, j):
                n = ada_chunks.index((l, j))
                if n >= 2:
                    pool.wait_ge(*upto("product", "mod", *ada_chunks[n - 2]))
                w, b = ada_w(l)
                dst = AW[n % 2]
                pool.dma_start(dst[:, 0:2048].rearrange("p (k c) -> p k c", k=8),
                               w.rearrange("(p k) c -> p k c", k=8)[:, :, 256 * j:256 * j + 256]) \
                    .then_inc(*made(f"ada_weights{n % 2}", l, j, by=16))
                pool.dma_start(dst[0:1, 2048:2304], b[256 * j:256 * j + 256].rearrange("(a c) -> a c", a=1)) \
                    .then_inc(*made(f"ada_weights{n % 2}", l, j, by=16))

            for j in range(ADA):
                ada_load(0, j)
            for l in range(4):
                pool.wait_ge(*upto("product", "h", l, "mix", tiles_of(l, "mix")[-1], 1))
                if l < 2:
                    pool.wait_ge(*upto("norm_low", l, "mix", tiles_of(l, "mix")[-1], 1))
                    pool.dma_start(TCS, io["t_cs"]).then_inc(*made("gains_in", l, by=16))
                    pool.dma_start(W4, io["w_four"][l].rearrange("(k p) c -> p k c", p=P)).then_inc(*made("gains_in", l, by=16))
                    for i, g in enumerate((io["q_norm"][l], io["k_norm"][l], io["hg_norm"][l])):
                        pool.dma_start(GROW3[:, i, :], g.partition_broadcast(P)).then_inc(*made("gains_in", l, by=16))
                    if l == 1:
                        for d in range(2):
                            pool.dma_start(LOGIT[:, d], io["hg_lb_logits"][d].partition_broadcast(P)) \
                                .then_inc(*made("logits_in", by=16))
                if l == 1:
                    pool.wait_ge(*upto("product", "m", 1, 1, 0))
                    pool.dma_start(DIST[:, :, :, :], io["t_dist"]).then_inc(*made("dist_in", by=16))
                    pool.dma_start(sinkn[:, :], io["a_sink_2"][0].partition_broadcast(P)).then_inc(*made("dist_in", by=16))
                pool.wait_ge(*upto("product", *stage_done(l, "mix")))
                if l < 3:
                    for j in range(ADA):
                        ada_load(l + 1, j)
                if l in (1, 3):
                    pool.wait_ge(*drained(*stage_done(l, "ffn")))
                    g = io["final_norm"] if l == 1 else io["final_norm_2"]
                    pool.dma_start(grow[:, 0, :], g.partition_broadcast(P)).then_inc(*made("final_gain_in", l, by=16))

        @block.tensor
        def _(pe):
            tenants = []

            def open_bank(*key):
                b = len(tenants) % NBANKS
                if len(tenants) >= NBANKS:
                    pe.wait_ge(*drained(*tenants[-NBANKS]))
                tenants.append(key)
                count.banks[key] = b
                return bank[b]

            def mm(out, lhsT, rhs, start, stop):
                return nc.tensor.matmul(out, lhsT, rhs, start=start, stop=stop, skip_group_check=True)

            def mm3(out, left, right, first, last):
                (lh, ll), (rh, rl) = left, right
                mm(out, lh, rh, first, False)
                mm(out, lh, rl, False, False)
                return mm(out, ll, rh, False, last)

            def need_parts(key):
                pe.wait_ge(*upto("split_low", key))

            def turn(out, in_):
                k = in_.shape[0]
                return nc.tensor.transpose(out, in_, ident[0:k, 0:k])

            def modulation(l, j):
                n = ada_chunks.index((l, j))
                pe.wait_ge(*upto(f"ada_weights{n % 2}", l, j))
                pe.wait_ge(*upto("ada_sum", l, j))
                if n == 0:
                    pe.wait_ge(*upto("ones_set"))
                ps = open_bank("mod", l, j)
                for i in range(len(conds_of(l, j))):
                    for c in range(2):
                        o = ps[:, 2 * c + i:2 * c + i + 1]
                        mm(o, ACC[:, n % 2, i, P * c:P * c + P], ones[:, 0:1], True, False)
                        last = mm(o, AW[n % 2][0:1, 2048 + P * c:2048 + P * c + P], ones[0:1, 0:1], False, True)
                last.then_inc(*made("product", "mod", l, j))

            def norm_turn(l, st):
                for t in tiles_of(l, st):
                    pe.wait_ge(*upto("normed", l, st, t))
                    for b in range(2):
                        ps = open_bank("h", l, st, t, b)
                        for i in range(4):
                            last = turn(ps[:, P * i:P * i + P], XN[:, t % 2, P * (4 * b + i):P * (4 * b + i) + P])
                        last.then_inc(*made("product", "h", l, st, t, b))

            def h_ready(l, st):
                for t in tiles_of(l, st):
                    for b in range(2):
                        pe.wait_ge(*upto("norm_low", l, st, t, b))

            waiting = []

            def beside(key):
                for c in waiting:
                    modulation(*c)
                waiting[:] = ada_by.get(key, [])

            def project(l):
                h_ready(l, "mix")
                for j, (a, b) in enumerate(col_groups(l)):
                    key = ("win", l, j)
                    need_parts(key)
                    wh, wl = (w.rearrange("p (k c) -> p k c", k=KD) for w in parts(key))
                    for t in [t for j2, t in proj_jobs(l) if j2 == j]:
                        ps = open_bank("u", l, j, t)
                        r = slice(P * t, P * t + P)
                        for k in range(KD):
                            last = mm3(ps[:, 0:256], (HTH[:, k, r], HTL[:, k, r]), (wh[:, k, :], wl[:, k, :]), k == 0, k == KD - 1)
                        last.then_inc(*made("product", "u", l, j, t))
                    beside(key)
                beside(None)

            def need_u(l, t, a, b):
                for j, (a0, b0) in enumerate(col_groups(l)):
                    if a < b0 and a0 < b:
                        pe.wait_ge(*drained("u", l, j, t))

            def fourier(l, g):
                tt = (X_TILES, C_TILES)[g]
                for t in tt:
                    need_u(l, t, 0, 256)
                if g == 0:
                    pe.wait_ge(*upto("tables_in"))
                    pe.wait_ge(*upto("gains_in", l))
                for d in range(2):
                    ps = open_bank("fa", l, g, d)
                    for k in range(2):
                        last = mm(ps[:, :], U[:, tt[k], P * d:P * d + P], TCS[:, k, :], k == 0, k == 1)
                    last.then_inc(*made("product", "fa", l, g, d))
                ps = open_bank("fy", l, g)
                for d in range(2):
                    pe.wait_ge(*drained("fa", l, g, d))
                    for k in range(2):
                        last = mm(ps[:, N * d:N * d + N], tb_cols[:, k, :], FA[:, d, N * k:N * k + N], k == 0, k == 1)
                last.then_inc(*made("product", "fy", l, g))

            def fourier_out(l, g):
                pe.wait_ge(*drained("fy", l, g))
                ps = open_bank("ff", l, g)
                for c in range(2):
                    for k in range(2):
                        last = mm(ps[:, N * c:N * c + N], W4[:, k, P * c:P * c + P], U[:, 2 * g + k, 0:256], k == 0, k == 1)
                last.then_inc(*made("product", "ff", l, g))

            def head_turns(l):
                for t in tiles_of(l, "mix"):
                    pe.wait_ge(*upto("heads_ready", l, t))
                    if l >= 2:
                        need_u(l, t, 0, DH * HEADS_Q[l])
                    nq = HEADS_Q[l] // 2 if (l != 1 or t < 2) else 0
                    src = QN_of(l, t)
                    for b in range(0, nq, 4):
                        ps = open_bank("qT", l, t, b)
                        for i in range(4):
                            last = turn(ps[:, P * i:P * i + P], src[:, P * (b + i):P * (b + i) + P])
                        last.then_inc(*made("product", "qT", l, t, b))
                    for b in range(0, HEADS_K[l], 4):
                        ps = open_bank("kT", l, t, b)
                        for i in range(min(4, HEADS_K[l] - b)):
                            last = turn(ps[:, P * i:P * i + P], KDUP[:, P * (b + i):P * (b + i) + P])
                        last.then_inc(*made("product", "kT", l, t, b))

            def attention(l):
                units = attention_units(l)
                for t in tiles_of(l, "mix"):
                    for b in range(0, HEADS_Q[l] // 2 if (l != 1 or t < 2) else 0, 4):
                        pe.wait_ge(*drained("qT", l, t, b))
                    for b in range(0, HEADS_K[l], 4):
                        pe.wait_ge(*drained("kT", l, t, b))
                    need_u(l, t, *{2: (1280, 1536), 3: (1920, 2304)}.get(l, (OFF_V, OFF_Z)))

                def scores(n):
                    u = units[n]
                    r = slice(DH * u["half"], DH * u["half"] + DH)
                    ps = None
                    for i, (q, kv, s0, sn, at) in enumerate(u["keys"]):
                        if at % 512 == 0:
                            ps = open_bank("sc", l, n, at // 512)
                        last = mm(ps[:, at % 512:at % 512 + sn], QT[l][r, q, P * u["t"]:P * u["t"] + P],
                                  KT[l][r, kv, s0:s0 + sn], True, True)
                        if at % 512 + sn == 512 or i == len(u["keys"]) - 1:
                            last.then_inc(*made("product", "sc", l, n, at // 512))

                def turns(n):
                    u = units[n]
                    pe.wait_ge(*upto("probs", l, n))
                    for i in range(u["size"] // P):
                        if i % 4 == 0:
                            ps = open_bank("pt", l, n, i // 4)
                        last = turn(ps[:, P * (i % 4):P * (i % 4) + P], PB[:, n % 2, P * i:P * i + P])
                        if i % 4 == 3 or i == u["size"] // P - 1:
                            last.then_inc(*made("product", "pt", l, n, i // 4))

                groups = out_groups(l)

                def values(n):
                    u = units[n]
                    g = groups.index(u["og"])
                    for b in range((u["size"] + 511) // 512):
                        pe.wait_ge(*drained("pt", l, n, b))
                    if u["oc"] == 0 and g >= 2:
                        pe.wait_ge(*upto("attended", l, g - 2))
                    for i, (s, c) in enumerate(u["vals"]):
                        last = mm(obank[g % 2][:, DH * u["oc"]:DH * u["oc"] + DH], PT[:, n % 2, P * i:P * i + P],
                                  U[:, s, c:c + DH], i == 0, i == len(u["vals"]) - 1)
                    last.then_inc(*made("valued", l, n))

                for n in range(len(units) + 2):
                    if n < len(units):
                        scores(n)
                    if 1 <= n <= len(units):
                        turns(n - 1)
                    if n >= 2:
                        values(n - 2)

            def recurrence(l):
                steps = scan_steps(l)

                def prepare(s, t, d, has_out):
                    pe.wait_ge(*upto("gates", l, s))
                    pe.wait_ge(*upto("decays_low", l, s))
                    if s == 0 and l == 0:
                        pe.wait_ge(*upto("sums_set"))
                    if has_out:
                        if first_visit(l, s, t):
                            need_u(l, t, OFF_HQ, OFF_G)
                            ps = open_bank("qt2", l, t)
                            for p in range(2):
                                last = turn(ps[:, P * p:P * p + P], U[:, t, OFF_HQ + P * p:OFF_HQ + P * p + P])
                            last.then_inc(*made("product", "qt2", l, t))
                        ps = open_bank("kt2", l, s)
                        for p in range(2):
                            last = turn(ps[:, P * p:P * p + P], HK[:, P * p:P * p + P])
                        last.then_inc(*made("product", "kt2", l, s))
                        for p in range(2):
                            for b in range(2):
                                ps = open_bank("e", l, s, p, b)
                                r = slice(P * p, P * p + P)
                                mm(ps[:, :], LFH[:, r], SUMS[:, d, 512 * b:512 * b + 512], True, False)
                                mm(ps[:, :], LFL[:, r], SUMS[:, d, 512 * b:512 * b + 512], False, True) \
                                    .then_inc(*made("product", "e", l, s, p, b))
                    if s < 6:
                        ps = open_bank("sf", l, s)
                        mm(ps[:, 0:256], TAILS[:, d, :], LFH[:, :], True, False)
                        mm(ps[:, 0:256], TAILS[:, d, :], LFL[:, :], False, True)
                        for p in range(2):
                            last = mm(ps[:, 256 + p:257 + p], LF[:, P * p:P * p + P], ones[:, 0:1], True, True)
                        last.then_inc(*made("product", "sf", l, s))

                prepare(*steps[0])
                for n, (s, t, d, has_out) in enumerate(steps):
                    need_u(l, t, OFF_I, OFF_HQ)
                    if has_out:
                        for p in range(2):
                            for q in range(2):
                                pe.wait_ge(*upto("weighed", l, s, p, q))
                                hb = half_buffer(l, s, p, q)
                                for b in range(2):
                                    ps = open_bank("a", l, s, p, q, b)
                                    for i in range(2):
                                        j = 2 * b + i
                                        last = mm(ps[:, 256 * i:256 * i + 256], KW[:, p, 4 * q + j, :],
                                                  QW[:, hb, j].rearrange("p h c -> p (h c)"), True, True)
                                    last.then_inc(*made("product", "a", l, s, p, q, b))
                    if n + 1 < len(steps):
                        prepare(*steps[n + 1])
                    if has_out:
                        o = obank[s % 2]
                        if s >= 2 and (l == 0 or s >= 6):
                            pe.wait_ge(*upto("scanned", l, s - 2))
                        for p in range(2):
                            if s >= 2:
                                pe.wait_ge(*drained("su", l, s - 2))
                                mm(o[:, P * p:P * p + P], QP[:, p, :], ST[:, d, p, :], True, False)
                            pe.wait_ge(*drained("a", l, s, p, 1, 1))
                            for h in (2 * p, 2 * p + 1):
                                last = mm(o[:, DH * h:DH * h + DH], AS[:, d, h, :], U[:, t, OFF_I + DH * h:OFF_I + DH * h + DH],
                                          s < 2, True)
                        last.then_inc(*made("read_out", l, s))
                    if s < 6:
                        pe.wait_ge(*upto("tailed", l, s))
                        ps = open_bank("su", l, s)
                        for p in range(2):
                            last = mm(ps[:, P * p:P * p + P], KS[:, P * p:P * p + P], U[:, t, OFF_I + P * p:OFF_I + P * p + P], True, True)
                        last.then_inc(*made("product", "su", l, s))

            def mixed_turns(l):
                for t in tiles_of(l, "ffn"):
                    if l < 2:
                        pe.wait_ge(*upto("mixed", l, t))
                    for g, og in enumerate(out_groups(l)):
                        if og[0] == t:
                            pe.wait_ge(*upto("attended", l, g))
                    for b, (k0, cols) in enumerate(mix_banks(l)):
                        ps = open_bank("m", l, t, b)
                        for i, c in enumerate(cols):
                            last = turn(ps[:, P * i:P * i + P], U[:, t, c:c + P])
                        last.then_inc(*made("product", "m", l, t, b))

            def gate_rows(l, st):
                for i in range(2 if l == 0 else 1):
                    for h in range(2):
                        pe.wait_ge(*upto("diagonal", l, st, i, h))
                        ps = open_bank("g", l, st, i, h)
                        mm(ps[:, :], ones[:, :], DIAG, True, True).then_inc(*made("product", "g", l, st, i, h))

            def project_out(l):
                for t in tiles_of(l, "ffn"):
                    for b in range(len(mix_banks(l))):
                        pe.wait_ge(*drained("m", l, t, b))
                if l < 2:
                    for g in range(2 if l == 0 else 1):
                        pe.wait_ge(*drained("ff", l, g))
                for j, (nk, nc_) in enumerate(out_loads(l)):
                    key = ("wo", l, j)
                    need_parts(key)
                    wh, wl = (w.rearrange("p (k c) -> p k c", k=nk) for w in parts(key))
                    for t in tiles_of(l, "ffn"):
                        ps = open_bank("x1", l, j, t)
                        r = slice(P * t, P * t + P)
                        for k in range(nk):
                            last = mm3(ps[:, 0:nc_], (HTH[:, k, r], HTL[:, k, r]), (wh[:, k, :], wl[:, k, :]), k == 0, k == nk - 1)
                        last.then_inc(*made("product", "x1", l, j, t))

            def open_down(l, half, h, t):
                if l == 0:
                    return open_bank("x2", l, half, h, t)
                if h:
                    pe.wait_ge(*drained("x2", l, half, 0, t))
                count.banks[("x2", l, half, h, t)] = NBANKS + t
                return obank[t]

            def feed_forward(l):
                n = P * len(tiles_of(l, "ffn"))
                ath, atl = hidden[halves(l)]
                h_ready(l, "ffn")
                for half in range(halves(l)):
                    fs = hidden_tiles(l, half)
                    for f in fs:
                        key = ("gu", l, f)
                        need_parts(key)
                        wh, wl = (w.rearrange("p (g k c) -> p g k c", g=2, k=KD) for w in parts(key))
                        for g, name in enumerate(("gate", "up")):
                            ps = open_bank(name, l, f)
                            for k in range(KD):
                                last = mm3(ps[:, 0:n], (wh[:, g, k, :], wl[:, g, k, :]), (HTH[:, k, 0:n], HTL[:, k, 0:n]),
                                           k == 0, k == KD - 1)
                            last.then_inc(*made("product", name, l, f))
                        beside(key)
                    chunks = down_chunks(l, half)
                    for h in range(2):
                        ps = {t: open_down(l, half, h, t) for t in tiles_of(l, "ffn")}
                        for c, f4 in enumerate(chunks):
                            key = ("dn", l, half, h, c)
                            need_parts(key)
                            wh, wl = (w.rearrange("p (k c) -> p k c", k=len(f4)) for w in parts(key))
                            if h == 0:
                                pe.wait_ge(*upto("hidden", l, f4[-1]))
                            for t in tiles_of(l, "ffn"):
                                r = slice(P * t, P * t + P)
                                for k, f in enumerate(f4):
                                    last = mm3(ps[t][:, :], (ath[:, f - fs[0], r], atl[:, f - fs[0], r]), (wh[:, k, :], wl[:, k, :]),
                                               f == fs[0], f == fs[-1])
                                if c == len(chunks) - 1:
                                    last.then_inc(*made("product", "x2", l, half, h, t))
                            if c < len(chunks) - 1:
                                last.then_inc(*made("down_part", *key[1:]))
                            beside(key)
                beside(None)

            def QN_of(l, t):
                return QN if l < 2 else U[:, t, :]

            pe.wait_ge(*upto("ident_in"))
            for j in range(8):
                modulation(0, j)
            for l in range(4):
                norm_turn(l, "mix")
                project(l)
                if l < 2:
                    for g in range(2 if l == 0 else 1):
                        fourier(l, g)
                head_turns(l)
                attention(l)
                if l < 2:
                    recurrence(l)
                    for g in range(2 if l == 0 else 1):
                        fourier_out(l, g)
                mixed_turns(l)
                gate_rows(l, "mix")
                project_out(l)
                gate_rows(l, "ffn")
                norm_turn(l, "ffn")
                feed_forward(l)

        @block.scalar
        def _(act):
            def put(key, out, in_, func=ACT.Copy, **kw):
                return nc.scalar.activation(out, in_, func, **kw)

            def take(*key):
                act.wait_ge(*upto("product", *key))
                return psum(*key)

            def inverse_root(*key, n):
                act.wait_ge(*upto("mean_square", *key))
                nc.scalar.activation(lnm[:, 0:n], ms[:, 0:n], ACT.Ln).then_inc(*made("log_taken", *key))
                act.wait_ge(*made_now("log_taken"))
                nc.scalar.activation(rs[:, 0:n], lnm[:, 0:n], ACT.Exp, scale=-0.5).then_inc(*made("root_guess", *key))

            def made_now(name):
                return count.sem(name), count.count[name]

            def split(n):
                if n < len(loads):
                    act.wait_ge(*upto(f"weights{n % RAW}", loads[n]))
                    if n >= HIGH:
                        act.wait_ge(*last_use(loads[n - HIGH]))
                    nc.scalar.activation(parts(loads[n])[0], raw_slot(loads[n]), ACT.Copy).then_inc(*made("split_high", loads[n]))

            waiting = []

            def beside(key):
                for c in waiting:
                    modulation(*c)
                waiting[:] = ada_by.get(key, [])

            def modulation(l, j):
                ps = take("mod", l, j)
                nc_ = len(conds_of(l, j))
                nc.scalar.activation(modc[:, l % 2, 2 * j:2 * j + 2, 0:nc_],
                                     ps[:, 0:4].rearrange("p (c i) -> p c i", i=2)[:, :, 0:nc_], ACT.Copy) \
                    .then_inc(*made("drained_act", "mod", l, j))

            def squares(l, st, tiles):
                for n, t in enumerate(tiles):
                    if st == "mix" and l == 0:
                        act.wait_ge(*upto("x_in"))
                    elif st == "mix" and l == 2:
                        act.wait_ge(*upto("final", 1))
                    elif st == "ffn":
                        act.wait_ge(*drained(*stage_done(l, "mix")))
                    else:
                        m = l if st == "final" else l - 1
                        act.wait_ge(*drained(*stage_done(m, "ffn")))
                    if n >= 2:
                        act.wait_ge(*upto("squared", l, st, tiles[n - 2]))
                    nc.scalar.activation(XN[:, t % 2, :], X[:, t, :], ACT.Square, accum_out=lsum[:, 0, t:t + 1]) \
                        .then_inc(*made("squared", l, st, t))
                inverse_root(l, st, n=len(tiles))

            def norm_take(l, st):
                act.wait_ge(*upto("scales", l, st))
                base = 0 if st == "mix" else 24
                for t in tiles_of(l, st):
                    i = cond_of_tile(t) if l < 2 else 0
                    if last_norm[0]:
                        act.wait_ge(*upto("norm_low", *last_norm[0], 0))
                    ps = take("h", l, st, t, 0)
                    for k in range(4):
                        last = nc.scalar.activation(G[:, 0, P * k:P * k + P], ps[:, P * k:P * k + P], ACT.Identity,
                                                    scale=scl[:, i, k:k + 1], bias=modc[:, l % 2, base + k, i:i + 1])
                    last.then_inc(*made("drained_act", "h", l, st, t, 0))
                    for b in range(2):
                        act.wait_ge(*drained("h", l, st, t, b))
                        nc.scalar.activation(HTH[:, 4 * b:4 * b + 4, P * t:P * t + P],
                                             G[:, b, :].rearrange("p (k c) -> p k c", k=4), ACT.Copy) \
                            .then_inc(*made("norm_high", l, st, t, b))
                    last_norm[0] = (l, st, t)

            last_norm = [None]

            def project(l):
                for j in range(len(col_groups(l))):
                    for t in [t for j2, t in proj_jobs(l) if j2 == j]:
                        ps = take("u", l, j, t)
                        a, b = col_groups(l)[j]
                        nc.scalar.activation(U[:, t, a:b], ps[:, 0:b - a], ACT.Copy).then_inc(*made("drained_act", "u", l, j, t))
                    split(index[("win", l, j)] + HIGH)
                    beside(("win", l, j))
                beside(None)

            def fourier(l, g):
                for d in range(2):
                    ps = take("fa", l, g, d)
                    nc.scalar.activation(FA[:, d, :], ps[:, :], ACT.Copy).then_inc(*made("drained_act", "fa", l, g, d))

            def fourier_out(l, g):
                ps = take("ff", l, g)
                nc.scalar.activation(HTH[:, 0:2, N * g:N * g + N], ps[:, :].rearrange("p (c n) -> p c n", c=2), ACT.Copy) \
                    .then_inc(*made("mixed_high", "ff", l, g))

            def head_turns(l):
                for t in tiles_of(l, "mix"):
                    if l < 2:
                        inverse_root(l, "heads", t, n=10 if (l == 0 or t < 2) else 2)
                    nq = HEADS_Q[l] // 2 if (l != 1 or t < 2) else 0
                    for b in range(0, nq, 4):
                        ps = take("qT", l, t, b)
                        nc.scalar.activation(QT[l][:, b:b + 4, P * t:P * t + P], ps[:, :].rearrange("p (k c) -> p k c", k=4),
                                             ACT.Copy, scale=1.0 if l < 2 else 0.125) \
                            .then_inc(*made("drained_act", "qT", l, t, b))
                    for b in range(0, HEADS_K[l], 4):
                        n = min(4, HEADS_K[l] - b)
                        ps = take("kT", l, t, b)
                        nc.scalar.activation(KT[l][:, b:b + n, P * t:P * t + P],
                                             ps[:, 0:P * n].rearrange("p (k c) -> p k c", k=n), ACT.Copy) \
                            .then_inc(*made("drained_act", "kT", l, t, b))

            def attention(l):
                units = attention_units(l)
                groups = out_groups(l)

                def probs(n):
                    u = units[n]
                    g = groups.index(u["og"])
                    act.wait_ge(*upto("maximum", l, n))
                    if n >= 2:
                        for b in range((units[n - 2]["size"] + 511) // 512):
                            act.wait_ge(*upto("product", "pt", l, n - 2, b))
                    src = SB[:, n % 2, 0:u["size"]] if u["bias"] else psum("sc", l, n, 0)[:, 0:u["size"]]
                    col = u["oc"]
                    if u["oc"] == 0 and g >= 2:
                        act.wait_ge(*upto("attended", l, g - 2))
                    nc.scalar.activation(PB[:, n % 2, 0:u["size"]], src, ACT.Exp, bias=nmax[:, g % 2, col:col + 1],
                                         accum_out=lsum[:, g % 2, col:col + 1]) \
                        .then_inc(*made("probs", l, n))
                    if l == 2:
                        h = u["h"]
                        nc.scalar.activation(sinke[:, g % 2, col:col + 1], sinkn[:, h:h + 1], ACT.Exp, scale=-1.0,
                                             bias=nmax[:, g % 2, col:col + 1]).then_inc(*made("sink_term", l, n))

                def take_turned(n):
                    u = units[n]
                    for b in range((u["size"] + 511) // 512):
                        if (n + b) % 2 == 0 or u["size"] == 512:
                            w = min(512, u["size"] - 512 * b)
                            ps = take("pt", l, n, b)
                            if n >= 2:
                                act.wait_ge(*upto("valued", l, n - 2))
                            nc.scalar.activation(PT[:, n % 2, 512 * b:512 * b + w], ps[:, 0:w], ACT.Copy) \
                                .then_inc(*made("drained_act", "pt", l, n, b))

                for n in range(len(units) + 1):
                    if n < len(units):
                        probs(n)
                    if n >= 1:
                        take_turned(n - 1)

            def recurrence(l):
                steps = scan_steps(l)

                def gates(n):
                    s, t, d, has_out = steps[n]
                    act.wait_ge(*upto("gate_in", l, s))
                    nc.scalar.activation(HE, HS, ACT.Exp, scale=-1.0).then_inc(*made("gate_exp", l, s))
                    act.wait_ge(*upto("gates", l, s))
                    if n:
                        s2 = steps[n - 1][0]
                        act.wait_ge(*(upto("product", "sf", l, s2) if s2 < 6 else upto("product", "e", l, s2, 1, 1)))
                    nc.scalar.activation(LF, HS, ACT.Ln).then_inc(*made("decays", l, s))
                    act.wait_ge(*upto("decays", l, s))
                    nc.scalar.activation(LFH[:, :], LF, ACT.Copy).then_inc(*made("decays_high", l, s))

                gates(0)
                for n, (s, t, d, has_out) in enumerate(steps):
                    if has_out:
                        if first_visit(l, s, t):
                            ps = take("qt2", l, t)
                            nc.scalar.activation(qt2(t), ps[:, 0:256].rearrange("p (k c) -> p k c", k=2), ACT.Copy) \
                                .then_inc(*made("drained_act", "qt2", l, t))
                        ps = take("kt2", l, s)
                        nc.scalar.activation(KT2, ps[:, 0:256].rearrange("p (k c) -> p k c", k=2), ACT.Copy) \
                            .then_inc(*made("drained_act", "kt2", l, s))
                        for p in range(2):
                            for b in range(2):
                                ps = take("e", l, s, p, b)
                                nc.scalar.activation(HW[:, p, 1 + 4 * b:5 + 4 * b, :],
                                                     ps[:, :].rearrange("p (j c) -> p j c", j=4), ACT.Exp) \
                                    .then_inc(*made("drained_act", "e", l, s, p, b))
                    if s < 6:
                        ps = take("sf", l, s)
                        nc.scalar.activation(SF, ps[:, 0:256], ACT.Exp)
                        nc.scalar.activation(TOT[:, s % 2, :], ps[:, 256:258], ACT.Exp).then_inc(*made("drained_act", "sf", l, s))
                    if n + 1 < len(steps):
                        gates(n + 1)
                for t in tiles_of(l, "ffn"):
                    inverse_root(l, "scan", t, n=4)
                    act.wait_ge(*upto("gain_done", l, t))
                    act.wait_ge(*drained("u", l, OFF_G // 256, t))
                    nc.scalar.activation(HE, U[:, t, OFF_G:OFF_G + 256], ACT.Exp, scale=-1.0).then_inc(*made("silu_exp", l, t))

            def mixed_turns(l):
                for t in tiles_of(l, "ffn"):
                    for b, (k0, cols) in enumerate(mix_banks(l)):
                        n = len(cols)
                        ps = take("m", l, t, b)
                        nc.scalar.activation(HTH[:, k0:k0 + n, P * t:P * t + P],
                                             ps[:, 0:P * n].rearrange("p (k c) -> p k c", k=n), ACT.Copy) \
                            .then_inc(*made("mixed_high", "m", l, t, b))

            def gate_rows(l, st):
                for i in range(2 if l == 0 else 1):
                    for h in range(2):
                        ps = take("g", l, st, i, h)
                        if st == "ffn":
                            act.wait_ge(*drained(*stage_done(l, "mix")))
                        nc.scalar.activation(grow[:, i, 512 * h:512 * h + 512], ps[:, :], ACT.Copy) \
                            .then_inc(*made("drained_act", "g", l, st, i, h))

            def project_out(l):
                for j in range(len(out_loads(l))):
                    split(index[("wo", l, j)] + HIGH)

            def feed_forward(l):
                n = P * len(tiles_of(l, "ffn"))
                ath, atl = hidden[halves(l)]
                for half in range(halves(l)):
                    fs = hidden_tiles(l, half)

                    def high(f):
                        act.wait_ge(*drained("up", l, f))
                        if f == fs[0] and half:
                            act.wait_ge(*last_use(("dn", l, 0, 1, len(down_chunks(l, 0)) - 1)))
                        nc.scalar.activation(ath[:, f - fs[0], 0:n], G[:, f % 2, 0:n], ACT.Copy).then_inc(*made("hidden_high", l, f))

                    for f in fs:
                        ps = take("gate", l, f)
                        if f >= 2:
                            act.wait_ge(*upto("hidden", l, f - 2))
                        nc.scalar.activation(G[:, f % 2, 0:n], ps[:, 0:n], ACT.Silu).then_inc(*made("drained_act", "gate", l, f))
                        if f > fs[0]:
                            high(f - 1)
                        split(index[("gu", l, f)] + HIGH)
                        beside(("gu", l, f))
                    high(fs[-1])
                    for h in range(2):
                        for c in range(len(down_chunks(l, half))):
                            key = ("dn", l, half, h, c)
                            split(index[key] + HIGH)
                            beside(key)
                beside(None)

            act.wait_ge(*upto("stage_in"))
            nc.scalar.activation(SUMS[:, :, :].rearrange("p d c -> p (d c)"), STAGE[:, 0:2048], ACT.Copy)
            nc.scalar.activation(tb_masks[:, :, :, :].rearrange("p d j c -> p (d j c)"), STAGE[:, 2304:4352], ACT.Copy)
            nc.scalar.activation(TAILS[:, :, :].rearrange("p d c -> p (d c)"), STAGE[:, 2048:2304], ACT.Copy) \
                .then_inc(*made("sums_set"))
            act.wait_ge(*upto("cond_in"))
            nc.scalar.activation(condt[:, 0, :], cond[:, :, :].rearrange("p i k -> p (i k)"), ACT.Exp, scale=-1.0) \
                .then_inc(*made("cond_exp"))
            for n in range(HIGH):
                split(n)
            for j in range(8):
                modulation(0, j)
            for l in range(4):
                squares(l, "mix", tiles_of(l, "mix"))
                norm_take(l, "mix")
                project(l)
                if l < 2:
                    if l == 1:
                        act.wait_ge(*upto("logits_less"))
                        nc.scalar.activation(LOGIT, LOGIT, ACT.Exp).then_inc(*made("logits_exp"))
                    for g in range(2 if l == 0 else 1):
                        fourier(l, g)
                head_turns(l)
                attention(l)
                if l < 2:
                    recurrence(l)
                    for g in range(2 if l == 0 else 1):
                        fourier_out(l, g)
                mixed_turns(l)
                gate_rows(l, "mix")
                project_out(l)
                gate_rows(l, "ffn")
                squares(l, "ffn", tiles_of(l, "ffn"))
                norm_take(l, "ffn")
                feed_forward(l)
                if l in (1, 3):
                    squares(l, "final", X_TILES)

        @block.vector
        def _(dve):
            V = nc.vector

            def link(ins):
                ins.then_inc(*made("dve_link"))
                dve.wait_ge(count.sem("dve_link"), count.count["dve_link"])

            def take(*key):
                dve.wait_ge(*upto("product", *key))
                return psum(*key)

            def as_float(ap):
                return ap.bitcast(F32)

            def split(n):
                if n < len(loads):
                    dve.wait_ge(*upto("split_high", loads[n]))
                    high, low = parts(loads[n])
                    V.tensor_tensor(low, raw_slot(loads[n]), as_float(high), ALU.subtract).then_inc(*made("split_low", loads[n]))

            def ada_sum(l, j):
                n = ada_chunks.index((l, j))
                dve.wait_ge(*upto(f"ada_weights{n % 2}", l, j))
                if n >= 2:
                    dve.wait_ge(*upto("product", "mod", *ada_chunks[n - 2]))
                w = AW[n % 2][:, 0:2048].rearrange("p (k c) -> p k c", k=8)
                cs = conds_of(l, j)
                for i in range(len(cs)):
                    last = V.tensor_scalar(ACC[:, n % 2, i, :], w[:, 0, :], cond[:, cs[i], 0:1], None, ALU.mult)
                    if i < len(cs) - 1:
                        continue
                link(last)
                for k in range(1, 8):
                    for i in range(len(cs)):
                        a = ACC[:, n % 2, i, :]
                        last = V.scalar_tensor_tensor(out=a, in0=w[:, k, :], scalar=cond[:, cs[i], k:k + 1], in1=a,
                                                      op0=ALU.mult, op1=ALU.add)
                    if k < 7:
                        link(last)
                last.then_inc(*made("ada_sum", l, j))

            def refine(*key, n):
                dve.wait_ge(*upto("root_guess", *key))
                link(V.tensor_tensor(nw[:, 0:n], rs[:, 0:n], rs[:, 0:n], ALU.mult))
                link(V.tensor_tensor(nw[:, 0:n], nw[:, 0:n], ms[:, 0:n], ALU.mult))
                link(V.tensor_scalar(nw[:, 0:n], nw[:, 0:n], -0.5, 1.5, ALU.mult, ALU.add))
                link(V.tensor_tensor(rs[:, 0:n], rs[:, 0:n], nw[:, 0:n], ALU.mult))

            def row_norms(l, st, tiles):
                for t in tiles:
                    dve.wait_ge(*upto("squared", l, st, t))
                n = len(tiles)
                V.tensor_scalar(ms[:, 0:n], lsum[:, 0, 0:n], 1.0 / D, EPS, ALU.mult, ALU.add) \
                    .then_inc(*made("mean_square", l, st))
                refine(l, st, n=n)

            def scales(l, st):
                base = 8 if st == "mix" else 32
                n = len(conds_of(l, 0 if st == "mix" else 16))
                for j in range(8) if st == "mix" else range(8, ADA):
                    dve.wait_ge(*drained("mod", l, j))
                src = modc[:, l % 2, base:base + 8, 0:n].rearrange("p k i -> p i k")
                if l < 2:
                    V.tensor_scalar(scl[:, 0:n, :], src, 1.0, None, ALU.add).then_inc(*made("scales", l, st))
                else:
                    dve.wait_ge(*upto("gains2_in"))
                    link(V.tensor_scalar(scl[:, 0:n, :], src, 1.0, None, ALU.add))
                    V.tensor_tensor(scl[:, 0, :], scl[:, 0, :], gcol[:, 2 * (l - 2) + (st == "ffn"), :], ALU.mult) \
                        .then_inc(*made("scales", l, st))

            last_norm = [None]

            def norm(l, st):
                tiles = tiles_of(l, st)
                if st == "ffn":
                    dve.wait_ge(*drained("h", l, "mix", tiles_of(l, "mix")[-1], 1))
                elif l:
                    dve.wait_ge(*drained("h", l - 1, "ffn", tiles_of(l - 1, "ffn")[-1], 1))
                scales(l, st)
                row_norms(l, st, tiles)
                for n, t in enumerate(tiles):
                    if n >= 2:
                        dve.wait_ge(*upto("product", "h", l, st, tiles[n - 2], 1))
                    V.tensor_scalar(XN[:, t % 2, :], X[:, t, :], rs[:, t:t + 1], None, ALU.mult) \
                        .then_inc(*made("normed", l, st, t))
                    if n:
                        norm_take(l, st, tiles[n - 1])
                norm_take(l, st, tiles[-1])

            def norm_take(l, st, t):
                base = 0 if st == "mix" else 24
                i = cond_of_tile(t) if l < 2 else 0
                ps = take("h", l, st, t, 1)
                if last_norm[0]:
                    dve.wait_ge(*upto("norm_low", *last_norm[0], 1))
                last_norm[0] = (l, st, t)
                for k in range(4):
                    last = V.tensor_scalar(G[:, 1, P * k:P * k + P], ps[:, P * k:P * k + P], scl[:, i, 4 + k:5 + k],
                                           modc[:, l % 2, base + 4 + k, i:i + 1], ALU.mult, ALU.add)
                last.then_inc(*made("drained_dve", "h", l, st, t, 1))
                for b in range(2):
                    dve.wait_ge(*upto("norm_high", l, st, t, b))
                    r = slice(P * t, P * t + P)
                    V.tensor_tensor(HTL[:, 4 * b:4 * b + 4, r], G[:, b, :].rearrange("p (k c) -> p k c", k=4),
                                    as_float(HTH[:, 4 * b:4 * b + 4, r]), ALU.subtract).then_inc(*made("norm_low", l, st, t, b))

            def project(l):
                for j in range(len(col_groups(l))):
                    split(index[("win", l, j)] + HIGH)
                    for c in ada_by.get(("win", l, j), []):
                        ada_sum(*c)

            def project_out(l):
                for j, (_, n) in enumerate(out_loads(l)):
                    for t in tiles_of(l, "ffn"):
                        i = cond_of_tile(t) if l < 2 else 0
                        dve.wait_ge(*drained("g", l, "mix", i, n * j // 512))
                        ps = take("x1", l, j, t)
                        link(V.tensor_tensor(ps[:, 0:n], ps[:, 0:n], grow[:, i, n * j:n * j + n], ALU.mult))
                        x = X[:, t, n * j:n * j + n]
                        V.tensor_tensor(x, ps[:, 0:n], x, ALU.add).then_inc(*made("drained_dve", "x1", l, j, t))
                    split(index[("wo", l, j)] + HIGH)

            def need_u(l, t, a, b):
                for j, (a0, b0) in enumerate(col_groups(l)):
                    if a < b0 and a0 < b:
                        dve.wait_ge(*drained("u", l, j, t))

            def fourier(l, g):
                ps = take("fy", l, g)
                V.tensor_copy(U[:, 2 * g:2 * g + 2, 0:256], ps[:, :].rearrange("p (d n) -> p d n", d=2)) \
                    .then_inc(*made("drained_dve", "fy", l, g))

            def fourier_out(l, g):
                dve.wait_ge(*upto("mixed_high", "ff", l, g))
                V.tensor_tensor(HTL[:, 0:2, N * g:N * g + N], psum("ff", l, g)[:, :].rearrange("p (c n) -> p c n", c=2),
                                as_float(HTH[:, 0:2, N * g:N * g + N]), ALU.subtract).then_inc(*made("drained_dve", "ff", l, g))

            def mixed_turns(l):
                for t in tiles_of(l, "ffn"):
                    for b, (k0, cols) in enumerate(mix_banks(l)):
                        n = len(cols)
                        dve.wait_ge(*upto("mixed_high", "m", l, t, b))
                        r = slice(P * t, P * t + P)
                        V.tensor_tensor(HTL[:, k0:k0 + n, r], psum("m", l, t, b)[:, 0:P * n].rearrange("p (k c) -> p k c", k=n),
                                        as_float(HTH[:, k0:k0 + n, r]), ALU.subtract).then_inc(*made("drained_dve", "m", l, t, b))

            def gains(l):
                dve.wait_ge(*upto("gains_in", l))
                V.tensor_scalar(G10[:, 0:8, :], GROW3[:, 0, :].unsqueeze(1).broadcast_to([P, 8, DH]), 0.125, None, ALU.mult)
                link(V.tensor_copy(G10[:, 8:10, :], GROW3[:, 1, :].unsqueeze(1).broadcast_to([P, 2, DH])))
                if l == 0:
                    dve.wait_ge(*upto("tables_in"))
                    return
                dve.wait_ge(*upto("logits_in"))
                link(V.tensor_tensor(lb[:, :, :], LOGIT[:, :, 0, :], LOGIT[:, :, 1, :], ALU.max))
                V.tensor_tensor(LOGIT, LOGIT, lb[:, :, :].unsqueeze(2).broadcast_to([P, 2, 2, 256]), ALU.subtract) \
                    .then_inc(*made("logits_less"))
                dve.wait_ge(*upto("logits_exp"))
                link(V.tensor_tensor(lb[:, :, :], LOGIT[:, :, 0, :], LOGIT[:, :, 1, :], ALU.add))
                link(V.reciprocal(lb[:, :, :], lb[:, :, :]))
                link(V.tensor_tensor(lb[:, :, :], LOGIT[:, :, 1, :], lb[:, :, :], ALU.mult))

            def heads(l):
                tiles = tiles_of(l, "mix")
                for n, t in enumerate(tiles):
                    if l >= 2:
                        nk, c = HEADS_K[l], DH * HEADS_Q[l]
                        need_u(l, t, c, c + DH * nk)
                        if n:
                            dve.wait_ge(*upto("product", "kT", l, tiles[n - 1], 4 * ((nk - 1) // 4)))
                        V.tensor_copy(KDUP[:, 0:P * nk].rearrange("p (k a c) -> p k a c", k=nk, a=2),
                                      U[:, t, c:c + DH * nk].rearrange("p (k c) -> p k c", k=nk)
                                      .unsqueeze(2).broadcast_to([P, nk, 2, DH])).then_inc(*made("heads_ready", l, t))
                        continue
                    has_q = l == 0 or t < 2
                    nh, c = (10, OFF_Q) if has_q else (2, OFF_K)
                    g0 = 10 - nh
                    need_u(l, t, c, OFF_V)
                    if n:
                        dve.wait_ge(*upto("product", "kT", l, tiles[n - 1], 0))
                    u = U[:, t, c:c + DH * nh].rearrange("p (h c) -> p h c", h=nh)
                    qn = QN[:, 0:DH * nh].rearrange("p (h c) -> p h c", h=nh)
                    qm = QM[:, 0:DH * nh].rearrange("p (h c) -> p h c", h=nh)
                    link(V.tensor_tensor(qn, u, u, ALU.mult))
                    link(V.tensor_reduce(nw[:, 0:nh], qn, AX.X, ALU.add))
                    V.tensor_scalar(ms[:, 0:nh], nw[:, 0:nh], 1.0 / DH, EPS, ALU.mult, ALU.add) \
                        .then_inc(*made("mean_square", l, "heads", t))
                    refine(l, "heads", t, n=nh)
                    link(V.tensor_tensor(qn, u, rs[:, 0:nh].unsqueeze(2).broadcast_to([P, nh, DH]), ALU.mult))
                    link(V.tensor_tensor(qn, qn, G10[:, g0:10, :], ALU.mult))
                    if t < 2:
                        v = QN.rearrange("p (h a s c) -> p h a s c", h=10, a=2, s=2)
                        w = QR.rearrange("p (h a s c) -> p h a s c", h=10, a=2, s=2)
                        sn = tb_sin[:, t, :].rearrange("p (a s c) -> p a s c", a=2, s=2)
                        for s in range(2):
                            V.tensor_tensor(w[:, :, :, s, :], v[:, :, :, 1 - s, :],
                                            sn[:, :, s, :].unsqueeze(1).broadcast_to([P, 10, 2, 16]), ALU.mult)
                        link(V.tensor_tensor(qm, qn, tb_cos[:, t, :].unsqueeze(1).broadcast_to([P, 10, DH]), ALU.mult))
                        link(V.tensor_tensor(qn, qm, QR.rearrange("p (h c) -> p h c", h=10), ALU.add))
                    V.tensor_copy(KDUP[:, 0:256].rearrange("p (k a c) -> p k a c", k=2, a=2),
                                  qn[:, nh - 2:nh, :].unsqueeze(2).broadcast_to([P, 2, 2, DH])) \
                        .then_inc(*made("heads_ready", l, t))

            def attention(l):
                units = attention_units(l)
                groups = out_groups(l)
                if l == 2:
                    dve.wait_ge(*upto("dist_in"))
                    link(V.tensor_scalar(sinkn[:, :], sinkn[:, :], -1.0, None, ALU.mult))

                def maximum(n):
                    u = units[n]
                    g, col = groups.index(u["og"]), u["oc"]
                    nm = nmax[:, g % 2, col:col + 1]
                    for b in range((u["size"] + 511) // 512):
                        take("sc", l, n, b)
                    if n >= 2:
                        dve.wait_ge(*upto("probs", l, n - 2))
                    if u["oc"] == 0 and g >= 2:
                        dve.wait_ge(*upto("attended", l, g - 2))
                    if u["bias"] is None:
                        V.tensor_reduce(nm, psum("sc", l, n, 0)[:, 0:u["size"]], AX.X, ALU.max, negate=True) \
                            .then_inc(*made("maximum", l, n))
                        return
                    for i, (g_, slope) in enumerate(u["bias"]):
                        at = u["keys"][i][4]
                        last = V.scalar_tensor_tensor(out=SB[:, n % 2, at:at + N], in0=DIST[:, g_, u["t"], :], scalar=slope,
                                                      in1=psum("sc", l, n, at // 512)[:, at % 512:at % 512 + N],
                                                      op0=ALU.mult, op1=ALU.add)
                        if at % 512 == 256 or i == len(u["bias"]) - 1:
                            last.then_inc(*made("drained_dve", "sc", l, n, at // 512))
                    dve.wait_ge(*count_now("drained_dve"))
                    last = V.tensor_reduce(nm, SB[:, n % 2, 0:u["size"]], AX.X, ALU.max, negate=True)
                    if l == 2:
                        link(last)
                        last = V.tensor_tensor(nm, nm, sinkn[:, u["h"]:u["h"] + 1], ALU.min)
                    last.then_inc(*made("maximum", l, n))

                def take_turned(n):
                    u = units[n]
                    for b in range((u["size"] + 511) // 512):
                        if not ((n + b) % 2 == 0 or u["size"] == 512):
                            w = min(512, u["size"] - 512 * b)
                            ps = take("pt", l, n, b)
                            if n >= 2:
                                dve.wait_ge(*upto("valued", l, n - 2))
                            V.tensor_copy(PT[:, n % 2, 512 * b:512 * b + w], ps[:, 0:w]).then_inc(*made("drained_dve", "pt", l, n, b))

                def normalise(n):
                    u = units[n]
                    g = groups.index(u["og"])
                    dve.wait_ge(*upto("valued", l, n))
                    if l == 2:
                        dve.wait_ge(*upto("sink_term", l, n))
                        link(V.tensor_tensor(lsum[:, g % 2, 0:8], lsum[:, g % 2, 0:8], sinke[:, g % 2, 0:8], ALU.add))
                    link(V.reciprocal(rinv[:, :], lsum[:, g % 2, 0:8]))
                    c = OUT_COL[l] + 512 * u["og"][1]
                    V.tensor_tensor(U[:, u["t"], c:c + 512].rearrange("p (h c) -> p h c", h=8),
                                    obank[g % 2][:, :].rearrange("p (h c) -> p h c", h=8),
                                    rinv[:, :].unsqueeze(2).broadcast_to([P, 8, DH]), ALU.mult) \
                        .then_inc(*made("attended", l, g))

                for n in range(len(units) + 3):
                    if n < len(units):
                        maximum(n)
                    if 1 <= n <= len(units):
                        take_turned(n - 1)
                    if n >= 3 and units[n - 3]["oc"] == 7:
                        normalise(n - 3)

            def count_now(name):
                return count.sem(name), count.count[name]

            def recurrence(l):
                steps = scan_steps(l)
                V.memset(ST, 0.0)
                V.memset(AS, 0.0)
                V.memset(QW, 0.0)
                link(V.memset(HW[:, :, 0, :], 1.0))

                def gates(n):
                    s, t, d, has_out = steps[n]
                    need_u(l, t, OFF_Z + 256 * d, OFF_Z + 256 * d + 256)
                    if n:
                        dve.wait_ge(*upto("decays", l, steps[n - 1][0]))
                        if steps[n - 1][3]:
                            dve.wait_ge(*upto("product", "kt2", l, steps[n - 1][0]))
                    V.tensor_scalar(HS, U[:, t, OFF_Z + 256 * d:OFF_Z + 256 * d + 256], -80.0, None, ALU.max) \
                        .then_inc(*made("gate_in", l, s))
                    dve.wait_ge(*upto("gate_exp", l, s))
                    link(V.tensor_scalar(HS, HE, 1.0, None, ALU.add))
                    link(V.reciprocal(HS, HS))
                    if l:
                        link(V.tensor_tensor(HK, HS, lb[:, d, :], ALU.mult))
                        link(V.tensor_tensor(HS, HS, HK, ALU.subtract))
                    last = V.tensor_tensor(HK, HS, HE, ALU.mult)
                    if l:
                        link(last)
                        last = V.tensor_tensor(HS, HS, lb[:, d, :], ALU.add)
                    last.then_inc(*made("gates", l, s))

                def low(n):
                    s = steps[n][0]
                    dve.wait_ge(*upto("decays_high", l, s))
                    V.tensor_tensor(LFL[:, :], LF, as_float(LFH[:, :]), ALU.subtract).then_inc(*made("decays_low", l, s))

                gates(0)
                low(0)
                for n, (s, t, d, has_out) in enumerate(steps):
                    if s < 6:
                        dve.wait_ge(*drained("sf", l, s))
                        if n:
                            dve.wait_ge(*upto("product", "su", l, s - 1))
                        V.tensor_tensor(KS, HK, SF, ALU.mult).then_inc(*made("tailed", l, s))
                        dve.wait_ge(*upto("tailed", l, s))
                    if has_out:
                        dve.wait_ge(*drained("qt2", l, t))
                        dve.wait_ge(*drained("kt2", l, s))
                        for p in range(2):
                            for q in range(2):
                                dve.wait_ge(*drained("e", l, s, p, q))
                                if q == 0:
                                    V.tensor_tensor(KW[:, p, 0:4, :], HW[:, p, 0:4, :],
                                                    KT2[:, p, :].unsqueeze(1).broadcast_to([P, 4, P]), ALU.mult)
                                else:
                                    V.tensor_tensor(KW[:, p, 4:8, :], HW[:, p, 4:8, :],
                                                    KT2[:, p, :].unsqueeze(1).broadcast_to([P, 4, P]), ALU.mult)
                                    V.tensor_tensor(QP[:, p, :], HW[:, p, 8, :], qt2(t)[:, p, :], ALU.mult)
                                user = half_buffer_last(l, s, p, q)
                                if user:
                                    dve.wait_ge(*upto("product", "a", l, *user, 1))
                                hb = half_buffer(l, s, p, q)
                                for hh in range(2):
                                    r = slice(DH * hh, DH * hh + DH)
                                    last = V.tensor_tensor(QW[r, hb, :, hh, :], HW[r, p, 4 * q:4 * q + 4, :],
                                                           qt2(t)[r, p, :].unsqueeze(1).broadcast_to([DH, 4, P]), ALU.mult)
                                last.then_inc(*made("weighed", l, s, p, q))
                    if n + 1 < len(steps):
                        gates(n + 1)
                        low(n + 1)
                    if has_out:
                        for p in range(2):
                            for q in range(2):
                                for b in range(2):
                                    ps = take("a", l, s, p, q, b)
                                    for i in range(2):
                                        j = 4 * q + 2 * b + i
                                        if i:
                                            link(last)
                                        elif q or b:
                                            dve.wait_ge(*count_now("drained_dve"))
                                        last = V.copy_predicated(AS[:, d, 2 * p:2 * p + 2, :],
                                                                 tb_masks[:, d, j, :].unsqueeze(1).broadcast_to([P, 2, P]),
                                                                 ps[:, 256 * i:256 * i + 256].rearrange("p (h c) -> p h c", h=2))
                                    last.then_inc(*made("drained_dve", "a", l, s, p, q, b))
                        dve.wait_ge(*upto("read_out", l, s))
                        o = obank[s % 2][:, 0:256]
                        if first_visit(l, s, t):
                            V.tensor_copy(scanned_sum(t), o).then_inc(*made("scanned", l, s))
                        else:
                            for s2, t2, _, o2 in steps:
                                if t2 == t and s2 < s and o2:
                                    dve.wait_ge(*upto("scanned", l, s2))
                            V.tensor_tensor(scanned_sum(t), o, scanned_sum(t), ALU.add).then_inc(*made("scanned", l, s))
                    if s < 6:
                        ps = take("su", l, s)
                        for p in range(2):
                            for hh in range(2):
                                r = slice(DH * hh, DH * hh + DH)
                                a = ST[r, d, p, DH * hh:DH * hh + DH]
                                last = V.scalar_tensor_tensor(out=a, in0=a, scalar=TOT[r, s % 2, p:p + 1],
                                                              in1=ps[r, P * p + DH * hh:P * p + DH * hh + DH],
                                                              op0=ALU.mult, op1=ALU.add)
                        last.then_inc(*made("drained_dve", "su", l, s))
                        dve.wait_ge(*drained("su", l, s))
                for t in tiles_of(l, "ffn"):
                    o4 = scanned_sum(t).rearrange("p (h c) -> p h c", h=4)
                    for s, t2, _, o2 in steps:
                        if t2 == t and o2:
                            dve.wait_ge(*upto("scanned", l, s))
                    hs4 = HS.rearrange("p (h c) -> p h c", h=4)
                    link(V.tensor_tensor(hs4, o4, o4, ALU.mult))
                    link(V.tensor_reduce(nw[:, 0:4], hs4, AX.X, ALU.add))
                    V.tensor_scalar(ms[:, 0:4], nw[:, 0:4], 1.0 / DH, EPS, ALU.mult, ALU.add) \
                        .then_inc(*made("mean_square", l, "scan", t))
                    refine(l, "scan", t, n=4)
                    link(V.tensor_tensor(hs4, o4, rs[:, 0:4].unsqueeze(2).broadcast_to([P, 4, DH]), ALU.mult))
                    V.tensor_tensor(hs4, hs4, GROW3[:, 2, :].unsqueeze(1).broadcast_to([P, 4, DH]), ALU.mult) \
                        .then_inc(*made("gain_done", l, t))
                    dve.wait_ge(*upto("gain_done", l, t))
                    dve.wait_ge(*upto("silu_exp", l, t))
                    need_u(l, t, OFF_G, OFF_G + 256)
                    g = U[:, t, OFF_G:OFF_G + 256]
                    link(V.tensor_scalar(HE, HE, 1.0, None, ALU.add))
                    link(V.reciprocal(HE, HE))
                    link(V.tensor_tensor(HE, HE, g, ALU.mult))
                    V.tensor_tensor(g, HE, HS, ALU.mult).then_inc(*made("mixed", l, t))
                    dve.wait_ge(*upto("mixed", l, t))

            def gate_rows(l, st):
                base = 16 if st == "mix" else 40
                for i in range(2 if l == 0 else 1):
                    for h in range(2):
                        if h or i:
                            dve.wait_ge(*upto("product", "g", l, st, i if h else i - 1, 1 - h))
                        elif st == "ffn":
                            dve.wait_ge(*upto("product", "g", l, "mix", 1 if l == 0 else 0, 1))
                        for c in range(4):
                            k = base + 4 * h + c
                            last = V.tensor_scalar(DIAG[:, c, :], ident[:, :], modc[:, l % 2, k, i:i + 1], None, ALU.mult)
                        last.then_inc(*made("diagonal", l, st, i, h))

            def feed_forward(l):
                n = P * len(tiles_of(l, "ffn"))
                ath, atl = hidden[halves(l)]
                for half in range(halves(l)):
                    fs = hidden_tiles(l, half)

                    def low(f):
                        dve.wait_ge(*upto("hidden_high", l, f))
                        V.tensor_tensor(atl[:, f - fs[0], 0:n], G[:, f % 2, 0:n], as_float(ath[:, f - fs[0], 0:n]), ALU.subtract) \
                            .then_inc(*made("hidden", l, f))

                    for f in fs:
                        ps = take("up", l, f)
                        dve.wait_ge(*drained("gate", l, f))
                        V.tensor_tensor(G[:, f % 2, 0:n], ps[:, 0:n], G[:, f % 2, 0:n], ALU.mult) \
                            .then_inc(*made("drained_dve", "up", l, f))
                        if f > fs[0]:
                            low(f - 1)
                        split(index[("gu", l, f)] + HIGH)
                        for c in ada_by.get(("gu", l, f), []):
                            ada_sum(*c)
                    low(fs[-1])
                    for h in range(2):
                        for c in range(len(down_chunks(l, half))):
                            key = ("dn", l, half, h, c)
                            split(index[key] + HIGH)
                            for a in ada_by.get(key, []):
                                ada_sum(*a)
                        for t in tiles_of(l, "ffn"):
                            i = cond_of_tile(t) if l < 2 else 0
                            dve.wait_ge(*drained("g", l, "ffn", i, h))
                            ps = take("x2", l, half, h, t)
                            link(V.tensor_tensor(ps[:, :], ps[:, :], grow[:, i, 512 * h:512 * h + 512], ALU.mult))
                            x = X[:, t, 512 * h:512 * h + 512]
                            V.tensor_tensor(x, ps[:, :], x, ALU.add).then_inc(*made("drained_dve", "x2", l, half, h, t))

            dve.wait_ge(*upto("ident_in"))
            dve.wait_ge(*upto("cond_exp"))
            flat = cond[:, :, :].rearrange("p i k -> p (i k)")
            link(V.tensor_scalar(condt[:, 0, :], condt[:, 0, :], 1.0, None, ALU.add))
            link(V.reciprocal(condt[:, 1, :], condt[:, 0, :]))
            link(V.tensor_tensor(flat, flat, condt[:, 1, :], ALU.mult))
            for j in range(8):
                ada_sum(0, j)
                if j < HIGH:
                    split(j)
            for l in range(4):
                norm(l, "mix")
                project(l)
                if l < 2:
                    gains(l)
                    for g in range(2 if l == 0 else 1):
                        fourier(l, g)
                heads(l)
                attention(l)
                if l < 2:
                    recurrence(l)
                    for g in range(2 if l == 0 else 1):
                        fourier_out(l, g)
                mixed_turns(l)
                gate_rows(l, "mix")
                project_out(l)
                gate_rows(l, "ffn")
                norm(l, "ffn")
                feed_forward(l)
                if l in (1, 3):
                    row_norms(l, "final", X_TILES)
                    dve.wait_ge(*upto("final_gain_in", l))
                    for t in X_TILES:
                        last = V.scalar_tensor_tensor(out=X[:, t, :], in0=X[:, t, :], scalar=rs[:, t:t + 1],
                                                      in1=grow[:, 0, :], op0=ALU.mult, op1=ALU.mult)
                    last.then_inc(*made("final", l))

        return count


_INS = ["x", "c", "ctx", "c_ctx", "w_ada", "b_ada", "w_in", "w_four", "q_norm", "k_norm", "hg_lb_logits", "hg_norm",
        "w_out", "w_gate", "w_up", "w_down", "final_norm", "c_2", "ada_w_2", "ada_b_2", "norm_mix_2", "norm_ffn_2",
        "ffn_w_in_2", "ffn_w_out_2", "a_w_in_2", "a_w_out_2", "a_sink_2", "b_w_in_2", "b_w_out_2", "final_norm_2"]


def kernel(**inputs):
    import concourse.bacc as bacc
    from concourse.bass_utils import run_bass_kernel_spmd as run

    consts = tables()
    arrays = {f"in_{n}": np.ascontiguousarray(inputs[n]) for n in _INS}
    arrays.update({f"in_{n}": a for n, a in consts.items()})
    counts = None
    for _ in range(2):
        nc = bacc.Bacc("TRN2", target_bir_lowering=False, num_devices=1)
        io = {n[3:]: nc.dram_tensor(n, a.shape, mybir.dt.from_np(a.dtype), kind="ExternalInput").ap()
              for n, a in arrays.items()}
        io["out"] = nc.dram_tensor("out_0", (1, N, D), F32, kind="ExternalOutput").ap()
        counts = block_kernel(nc, io, counts)
    r = run(nc, [arrays], core_ids=[0])
    return r.results[0]["out_0"]
```

```python
from contextlib import ExitStack

import numpy as np

import concourse.bass as bass
from concourse import mybir

P = 128
F32 = mybir.dt.float32
F32R = mybir.dt.float32r
U8 = mybir.dt.uint8
I32 = mybir.dt.int32
ALU = mybir.AluOpType
ACT = mybir.ActivationFunctionType
AX = mybir.AxisListType

D = 1024
KD = D // P
N = 256
DH = 64
FF = 2816
NF = FF // P
EPS = 1e-6
PROJ = [2304, 2304, 1536, 2304]
OFF_Q, OFF_K, OFF_V, OFF_Z, OFF_I, OFF_HQ, OFF_G = 256, 768, 896, 1024, 1536, 1792, 2048
LEVELS = 7
RAW = 4
HIGH = 3
SLOT = KD * 256
NBANKS = 6
X_TILES, C_TILES = (0, 1), (2, 3)
ADA = 24
GROUPS_B = ((128, 1), (512, 4), (2048, 16))


def level_matrices():
    i = np.arange(P)
    sums, tails, masks = [], [], []
    for h in (1 << j for j in range(LEVELS)):
        mid = (i // (2 * h)) * 2 * h + h
        second = (i % (2 * h)) >= h
        r, c = i[:, None], i[None, :]
        fwd = second[None, :] & (r >= mid[None, :]) & (r <= c)
        back = ~second[None, :] & (r > c) & (r < mid[None, :])
        sums.append((fwd | back).astype(np.float32))
        same = (i[:, None] // (2 * h)) == (i[None, :] // (2 * h))
        masks.append((same & ~second[:, None] & second[None, :]).astype(np.float32))
    sums.append((i[:, None] <= i[None, :]).astype(np.float32))
    masks.insert(0, np.eye(P, dtype=np.float32))
    tails = (i[:, None] > i[None, :]).astype(np.float32)
    sums, masks = np.stack(sums, 1), np.stack(masks, 1)
    both = [np.stack([a, a[::-1, ..., ::-1]], 1) for a in (sums, tails, masks)]
    return [np.ascontiguousarray(a.reshape(P, 2, -1)) for a in both]


def rope_tables():
    half = DH // 2
    freqs = (10000.0 ** (-np.arange(0, half, 2, dtype=np.float32) / np.float32(half))).astype(np.float32)
    pos = np.arange(N)
    ang = [(p[:, None].astype(np.float32) * freqs).astype(np.float32) for p in (pos // 64, pos % 64)]
    cos = np.concatenate([np.cos(a) for a in (ang[0], ang[0], ang[1], ang[1])], 1).astype(np.float32)
    sin = np.concatenate([-np.sin(ang[0]), np.sin(ang[0]), -np.sin(ang[1]), np.sin(ang[1])], 1).astype(np.float32)
    return [np.ascontiguousarray(a.reshape(2, P, DH).transpose(1, 0, 2)) for a in (cos, sin)]


def fourier_tables():
    t = 2 * np.pi * (np.outer(np.arange(N), np.arange(N)) % N) / N
    cs = np.concatenate([np.cos(t), np.sin(t)], 1).astype(np.float32).reshape(2, P, 2 * N).transpose(1, 0, 2)
    t = 2 * np.pi * (np.outer(np.arange(DH), np.arange(DH)) % DH) / DH
    cols = [np.kron(np.eye(2), f / 128.0).astype(np.float32) for f in (np.cos(t), -np.sin(t))]
    return np.ascontiguousarray(cs), np.ascontiguousarray(np.stack(cols, 1))


def distance_tables():
    t, s = np.arange(N)[:, None], np.arange(N)[None, :]
    away = np.abs(t - s)
    seen = [away <= P] + [((t - s) % dil == 0) & (away <= window // 2) for window, dil in GROUPS_B]
    out = np.stack([np.where(ok, -away, -1e30) for ok in seen]).astype(np.float32)
    return np.ascontiguousarray(out.reshape(4, 2, P, N).transpose(2, 0, 1, 3))


def slopes(n):
    return [float(x) for x in (2.0 ** (-8.0 * np.arange(1, n + 1) / n)).astype(np.float32)]


def tables():
    sums, tails, masks = level_matrices()
    cos, sin = rope_tables()
    cs, cols = fourier_tables()
    return {"t_sums": sums, "t_tails": tails, "t_masks": masks, "t_cos": cos, "t_sin": sin, "t_cs": cs,
            "t_cols": cols, "t_dist": distance_tables(), "t_ident": np.eye(P, dtype=np.float32)}


def tiles_of(layer, stage):
    if stage == "mix":
        return (0, 1, 2, 3) if layer < 2 else (0, 1)
    return (0, 1, 2, 3) if layer == 0 else (0, 1)


def conds_of(layer, chunk=0):
    if layer >= 2:
        return (2,)
    return (0, 1) if layer == 0 or chunk < 8 else (0,)


def cond_of_tile(t):
    return 0 if t < 2 else 1


def col_groups(layer):
    return [(a, a + 256) for a in range(0, PROJ[layer], 256)]


def cols_of(layer, t, a, b):
    if layer == 1 and t >= 2:
        a, b = max(a, OFF_K), min(b, OFF_HQ)
    return (a, b) if a < b else None


def proj_jobs(layer):
    return [(j, t) for j, (a, b) in enumerate(col_groups(layer)) for t in tiles_of(layer, "mix") if cols_of(layer, t, a, b)]


def halves(l):
    return 2 if l == 0 else 1


def hidden_tiles(l, half):
    n = NF // halves(l)
    return range(n * half, n * half + n)


def down_chunks(l, half):
    f = hidden_tiles(l, half)
    return [f[i:i + 4] for i in range(0, len(f), 4)]


def out_loads(l):
    return [(8, 256)] * 4 if l < 3 else [(4, 512)] * 2


def load_plan():
    out = []
    for l in range(4):
        out += [("win", l, j) for j in range(len(col_groups(l)))]
        out += [("wo", l, j) for j in range(len(out_loads(l)))]
        for half in range(halves(l)):
            out += [("gu", l, f) for f in hidden_tiles(l, half)]
            out += [("dn", l, half, h, c) for h in range(2) for c in range(len(down_chunks(l, half)))]
    return out


STARTING = 8
START_ORDER = (0, 2, 1, 4, 3, 6, 5, 7)


def ada_plan():
    chunks = [(l, j) for l in range(4) for j in range(ADA)]
    out = {("start",): [chunks.pop(0) for _ in range(STARTING)]}

    def give(spots):
        for spot in spots:
            out.setdefault(spot, []).append(chunks.pop(0))

    def attention(l, n):
        return [(l, "attention", ROUNDS * i) for i in range(n)]

    def feed_forward(l, n):
        keys = [key for key in load_plan() if key[1] == l and key[0] in ("gu", "dn")][1:-1]
        return [keys[i * len(keys) // n] for i in range(n)]

    def scan(l, n):
        spots = [(l, "scan", s, i) for s in range(8) for i in (0, 2)]
        return [spots[i * 16 // n] for i in range(n)]

    give([("win", 0, j) for j in range(8)] + [(0, "heads", t) for t in range(4)] + scan(0, 4))
    give(feed_forward(0, ADA))
    give([(1, "heads", t) for t in range(4)] + attention(1, 6) + scan(1, 6))
    give(feed_forward(1, 14))
    give(feed_forward(2, len(chunks)))
    return out


ROUNDS = 3


def ada_group(spot):
    if spot[0] in ("gu", "dn"):
        return "feed_forward", spot[1]
    if spot[0] == "win":
        return "projection", spot[1]
    return spot[0], spot[0]


def ada_engine(spot, j):
    if spot == ("start",):
        return "vector" if j % 2 else "tensor"
    return "vector" if spot[0] in ("win", "gu", "dn") or "attention" in spot else "tensor"


def attention_units(l):
    out = []
    if l < 2:
        for t in tiles_of(l, "ffn"):
            s = (0, 1, 2, 3) if t < 2 else (2, 3)
            for h in range(8):
                kv = h // 4
                out.append(dict(t=t, h=h, og=(t, 0), oc=h, keys=[(h // 2, kv, s[0] * P, len(s) * P, 0)], half=h % 2,
                                vals=[(i, OFF_V + DH * kv) for i in s], bias=None, size=len(s) * P))
    elif l == 2:
        for t in X_TILES:
            for h in range(16):
                out.append(dict(t=t, h=h, og=(t, h // 8), oc=h % 8, keys=[(h // 2, h // 4, 0, N, 0)], half=h % 2,
                                vals=[(i, 1280 + DH * (h // 4)) for i in X_TILES], bias=[(0, slopes(16)[h])], size=N))
    else:
        for t in X_TILES:
            for h in range(8):
                kv = h // 4
                out.append(dict(t=t, h=h, og=(t, 0), oc=h, half=h % 2, size=3 * N,
                                keys=[((8 * g + h) // 2, 2 * g + kv, 0, N, g * N) for g in range(3)],
                                vals=[(i, 1920 + DH * (2 * g + kv)) for g in range(3) for i in X_TILES],
                                bias=[(1 + g, slopes(24)[8 * g + h]) for g in range(3)]))
    return out


def out_groups(l):
    return list(dict.fromkeys(u["og"] for u in attention_units(l)))


OUT_COL = [OFF_Q, OFF_Q, 0, 0]
HEADS_Q = [8, 8, 16, 24]
HEADS_K = [2, 2, 4, 6]


def mix_banks(l):
    if l < 2:
        return [(2, [OFF_Q + P * i for i in range(4)]), (6, [OFF_G, OFF_G + P])]
    return [(4 * b, [P * (4 * b + i) for i in range(4)]) for b in range(2 if l == 2 else 1)]


KO = [8, 8, 8, 4]


def scan_steps(l):
    order = ((2, 3, 0, 1), (3, 2, 1, 0))
    return [(2 * i + d, order[d][i], d, l == 0 or order[d][i] < 2) for i in range(4) for d in range(2)]


def first_visit(l, s, t):
    return s == min(s2 for s2, t2, _, out in scan_steps(l) if t2 == t and out)


def half_buffer(l, s, p, q):
    n = sum(out for s2, _, _, out in scan_steps(l) if s2 < s)
    return (4 * n + 2 * p + q) % 3


def half_buffer_last(l, s, p, q):
    steps = [s2 for s2, _, _, out in scan_steps(l) if out]
    n = 4 * steps.index(s) + 2 * p + q - 3
    return None if n < 0 else (steps[n // 4], (n % 4) // 2, n % 2)


class Counts:

    def __init__(self, nc, ctx, first=None):
        self.nc, self.ctx, self.first = nc, ctx, first
        self.sems, self.count, self.at = {}, {}, {}
        self.banks, self.tenants = {}, []

    def sem(self, name):
        if name not in self.sems:
            self.sems[name] = self.ctx.enter_context(self.nc.semaphore(name))
        return self.sems[name]

    def made(self, name, *key, by=1):
        self.count[name] = self.count.get(name, 0) + by
        self.at[(name, *key)] = self.count[name]
        return self.sem(name), by

    def upto(self, name, *key):
        return self.sem(name), self.first.at[(name, *key)] if self.first else 1

    def drained(self, *key):
        if not self.first:
            return self.sem("drained_act"), 1
        if key[0] == "sc" and key[1] < 2:
            return self.upto("probs", *key[1:3])
        name = "drained_act" if ("drained_act", *key) in self.first.at else "drained_dve"
        return self.upto(name, *key)


def block_kernel(nc, io, first=None):
    ctx = ExitStack()
    with ctx:
        count = Counts(nc, ctx, first)
        made, upto, drained = count.made, count.upto, count.drained

        base = [-(-nc.sbuf_base // 32) * 32]

        def place(name, offset, shape, dt=F32):
            return nc.alloc_sbuf_tensor_at(name, shape, dt, offset=offset)

        def sb(name, shape, dt=F32):
            offset = base[0]
            n = int(np.prod(shape[1:])) * (1 if dt == U8 else 4)
            base[0] += -(-n // 32) * 32
            return place(name, offset, shape, dt)

        X = sb("X", [P, 4, D])
        hth_at = base[0]
        HTH = sb("HTH", [P, KD, 512], F32R)
        a1 = base[0]
        AWH = place("AWH", hth_at, [P, 2, 8, 256])
        A1 = sb("A1", [P, NF * 512])
        a2 = base[0]
        A2 = sb("A2", [P, 11264])
        HTL = place("HTL", a2, [P, KD, 512], F32R)
        hidden = {}
        for n_half in (2, 1):
            shape = [P, NF // n_half, 256 * n_half]
            hidden[n_half] = (place(f"hidden_high{n_half}", a1, shape, F32R),
                              place(f"hidden_low{n_half}", a1 + NF * 256 * 4, shape, F32R))
        LFH = place("LFH", a2 + 4 * 11008, [P, 256], F32R)
        LFL = place("LFL", a1 + 4 * 10560, [P, 256], F32R)
        raw_at = base[0]
        raw = sb("raw", [P, RAW, SLOT])
        wlow = place("wlow", raw_at, [P, RAW, SLOT], F32R)
        whigh = sb("whigh", [P, HIGH, SLOT], F32R)
        dist_at = base[0]
        SUMS = sb("SUMS", [P, 2, 8 * P], F32R)
        DIST = place("DIST", dist_at, [P, 4, 2, N])
        TAILS = sb("TAILS", [P, 2, P], F32R)
        tb_masks = sb("tb_masks", [P, 2, 8, P], U8)
        tb_cols = sb("tb_cols", [P, 2, P])
        tb_cos = sb("tb_cos", [P, 2, DH])
        tb_sin = sb("tb_sin", [P, 2, DH])
        ident = sb("ident", [P, P])
        ones = sb("ones", [P, P])
        lb = sb("lb", [P, 2, 256])
        grow = sb("grow", [P, 2, D])
        cond = sb("cond", [P, 3, 8])
        condt = sb("condt", [P, 2, 24])
        modc = sb("modc", [P, 4, 48, 2])
        scl = sb("scl", [P, 2, 8])
        gcol = sb("gcol", [P, 4, 8])
        ms = sb("ms", [P, 16])
        half_ms = sb("half_ms", [P, 16])
        rs = sb("rs", [P, 16])
        nw = sb("nw", [P, 16])
        nmax = sb("nmax", [P, 2, 16])
        lsum = sb("lsum", [P, 2, 16])
        sinkn = sb("sinkn", [P, 16])
        sinke = sb("sinke", [P, 2, 16])
        rinv = sb("rinv", [P, 8])
        ACC = sb("ACC", [P, 2, 2, 256])
        BIAS = sb("BIAS", [P, 256])
        TOT = sb("TOT", [P, 2, 2])

        assert base[0] <= 229344
        U = A1[:, 0:9216].rearrange("p (t c) -> p t c", t=4)
        XN = A1[:, 9216:11264].rearrange("p (b c) -> p b c", b=2)
        W4 = A1[:, 9216:9728].rearrange("p (k c) -> p k c", k=2)
        G10 = A1[:, 9728:10368].rearrange("p (h c) -> p h c", h=10)
        GROW3 = A1[:, 10368:10560].rearrange("p (h c) -> p h c", h=3)

        def cut(start, n):
            return A2[:, start:start + n]

        STAGE = A1[:, 0:4352]
        G = cut(4096, 1024).rearrange("p (b c) -> p b c", b=2)
        AWX = [cut(5120 + 2048 * b, 2048).rearrange("p (k c) -> p k c", k=8) for b in range(3)]
        DIAG = cut(5120, 2048).rearrange("p (i h k c) -> p i h k c", i=2, h=2, k=4)
        TCS = cut(4096, 1024).rearrange("p (k c) -> p k c", k=2)
        FA = cut(6656, 1024).rearrange("p (d c) -> p d c", d=2)
        LOGIT = cut(8192, 1024).rearrange("p (d l c) -> p d l c", d=2, l=2)
        QT = [cut(0, 3072).rearrange("p (k c) -> p k c", c=512 if l < 2 else 256) for l in range(4)]
        KT = [cut(3072, 1536).rearrange("p (k c) -> p k c", c=512 if l < 2 else 256) for l in range(4)]
        SB = cut(4608, 1536).rearrange("p (b c) -> p b c", b=2)
        PB = cut(6144, 1536).rearrange("p (b c) -> p b c", b=2)
        PT = cut(7680, 1536).rearrange("p (b c) -> p b c", b=2)
        KDUP = cut(9216, 768)
        QN, QM = cut(9984, 640), cut(10624, 640)
        QR = cut(4608, 640)
        HW = cut(0, 2304).rearrange("p (b j c) -> p b j c", b=2, j=9)
        QW = cut(2304, 3072).rearrange("p (b j h c) -> p b j h c", b=3, j=4, h=2)
        KW = cut(5376, 2048).rearrange("p (b j c) -> p b j c", b=2, j=8)
        AS = cut(7424, 1024).rearrange("p (d h c) -> p d h c", d=2, h=4)
        QP = cut(8448, 256).rearrange("p (b c) -> p b c", b=2)
        KT2 = cut(8704, 256).rearrange("p (k c) -> p k c", k=2)
        LF, HE, HS, SF = cut(8960, 256), cut(9216, 256), cut(9472, 256), cut(9728, 256)
        ST = cut(9984, 512).rearrange("p (d k c) -> p d k c", d=2, k=2)
        KS, HK = cut(10496, 256), cut(10752, 256)

        def scanned_sum(t):
            return U[:, t, OFF_K:OFF_K + 256]

        def qt2(t):
            return U[:, t, OFF_HQ:OFF_HQ + 256].rearrange("p (k c) -> p k c", k=2)

        bank = [ctx.enter_context(nc.psum_tensor(f"bank{b}", [P, 512], F32)) for b in range(NBANKS + 2)]
        obank = bank[NBANKS:]

        def psum(*key):
            return bank[(first or count).banks.get(key, 0)]

        loads = load_plan()
        index = {key: n for n, key in enumerate(loads)}
        ada_by = ada_plan()

        def load_size(key):
            kind, l = key[:2]
            if kind == "dn":
                return 512 * len(down_chunks(l, key[2])[key[4]])
            return SLOT

        def raw_slot(key):
            return raw[:, index[key] % RAW, 0:load_size(key)]

        def parts(key):
            n = index[key]
            return whigh[:, n % HIGH, 0:load_size(key)], wlow[:, n % RAW, 0:load_size(key)]

        def last_use(key):
            kind, l = key[:2]
            if kind == "win":
                t = [t for j, t in proj_jobs(l) if j == key[2]][-1]
                return upto("product", "u", l, key[2], t)
            if kind == "wo":
                return upto("product", "x1", l, key[2], tiles_of(l, "ffn")[-1])
            if kind == "gu":
                return upto("product", "up", l, key[2])
            if key[4] < len(down_chunks(l, key[2])) - 1:
                return upto("down_part", *key[1:])
            return upto("product", "x2", l, key[2], key[3], tiles_of(l, "ffn")[-1])

        def stage_done(l, st):
            if st == "mix":
                return ("x1", l, len(out_loads(l)) - 1, tiles_of(l, "ffn")[-1])
            return ("x2", l, halves(l) - 1, 1, tiles_of(l, "ffn")[-1])

        ada_chunks = [(l, j) for l in range(4) for j in range(ADA)]

        ada_spot = {c: spot for spot, cs in ada_by.items() for c in cs}

        def ada_place(l, j):
            group = ada_group(ada_spot[l, j])
            members = [c for c in ada_chunks if ada_group(ada_spot[c]) == group]
            slots = {"start": (0, 1, 2, 3), "projection": (2, 3, 4), "feed_forward": (2, 3, 4)}.get(group[0], (0, 1))
            n = members.index((l, j))
            slot = slots[n % len(slots)]
            return slot, AWH[:, slot] if slot < 2 else AWX[slot - 2], members[n - len(slots)] if n >= len(slots) else None

        def ada_used(l, j):
            if ada_engine(ada_spot[l, j], j) == "tensor":
                return upto("product", "mod", l, j)
            return upto("ada_sum", l, j)

        def sum_slot(l, j):
            todo = [c for c in ada_chunks if ada_engine(ada_spot[c], c[1]) == "vector"]
            n = todo.index((l, j))
            return n % 2, todo[n - 2] if n >= 2 else None

        def ada_w(l):
            w = io["w_ada"][l] if l < 2 else io["ada_w_2"][l - 2]
            b = io["b_ada"][l] if l < 2 else io["ada_b_2"][l - 2]
            return w, b

        block = ctx.enter_context(nc.Block())

        @block.sync
        def _(sp):
            for name, dst, src in (
                ("cond_in", cond[:, 0, :], io["c"][0].rearrange("(p k) -> p k", k=8)),
                ("cond_in", cond[:, 1, :], io["c_ctx"].rearrange("(p k) -> p k", k=8)),
                ("cond_in", cond[:, 2, :], io["c_2"][0].rearrange("(p k) -> p k", k=8)),
                ("ident_in", ident[:, :], io["t_ident"]),
            ):
                sp.dma_start(dst, src).then_inc(*made(name, by=16))

            def ada_load(l, j):
                slot, dst, before = ada_place(l, j)
                group = ada_group(ada_spot[l, j])
                if before:
                    sp.wait_ge(*ada_used(*before))
                elif group[0] == "projection":
                    sp.wait_ge(*upto("product", "mod", 0, STARTING - 1))
                elif group[0] == "feed_forward":
                    sp.wait_ge(*upto("product", "g", group[1], "ffn", 1 if group[1] == 0 else 0, 1))
                w, b = ada_w(l)
                sp.dma_start(dst, w.rearrange("(p k) c -> p k c", k=8)[:, :, 256 * j:256 * j + 256]) \
                    .then_inc(*made(f"ada_weights{slot}", l, j, by=16))

            for l in range(4):
                sp.dma_start(BIAS[ADA * l:ADA * l + ADA, :], ada_w(l)[1].rearrange("(j c) -> j c", c=256)) \
                    .then_inc(*made("bias_in", by=16))
            for j in range(STARTING):
                ada_load(0, j)
                if j == 3:
                    for t, name in ((0, "x"), (2, "ctx")):
                        sp.dma_start(X[:, t:t + 2, :], io[name][0].rearrange("(t p) d -> p t d", p=P)) \
                            .then_inc(*made("x_in", by=16))

            def rows(w, a, n):
                return w[a * P:(a + n) * P, :].rearrange("(k p) c -> p k c", p=P)

            def load_tables():
                for name, dst, src in (
                    ("stage_in", STAGE[:, 0:2048], io["t_sums"].rearrange("p d c -> p (d c)")),
                    ("stage_in", STAGE[:, 2048:2304], io["t_tails"].rearrange("p d c -> p (d c)")),
                    ("stage_in", STAGE[:, 2304:4352], io["t_masks"].rearrange("p d c -> p (d c)")),
                    ("tables_in", tb_cols[:, :, :], io["t_cols"]),
                    ("tables_in", tb_cos[:, :, :], io["t_cos"]),
                    ("tables_in", tb_sin[:, :, :], io["t_sin"]),
                ):
                    sp.dma_start(dst, src).then_inc(*made(name, by=16))

            beside_loads = [c for c in ada_chunks if ada_group(ada_spot[c])[0] in ("projection", "feed_forward")]
            for n, key in enumerate(loads):
                kind, l = key[:2]
                if n == RAW - 1:
                    load_tables()
                if n >= RAW:
                    used = n - RAW
                    sp.wait_ge(*last_use(loads[used]))
                to = raw_slot(key)
                sem = f"weights{n % RAW}"
                if kind == "win":
                    w = (io["w_in"][l] if l < 2 else io["a_w_in_2"][0] if l == 2 else io["b_w_in_2"][0])
                    a, b = col_groups(l)[key[2]]
                    sp.dma_start(to.rearrange("p (k c) -> p k c", k=KD), rows(w, 0, KD)[:, :, a:b]) \
                        .then_inc(*made(sem, key, by=16))
                elif kind == "wo":
                    w = (io["w_out"][l] if l < 2 else io["a_w_out_2"][0] if l == 2 else io["b_w_out_2"][0])
                    k, c = out_loads(l)[key[2]]
                    sp.dma_start(to.rearrange("p (k c) -> p k c", k=k), rows(w, 0, k)[:, :, c * key[2]:c * key[2] + c]) \
                        .then_inc(*made(sem, key, by=16))
                elif kind == "gu":
                    dst = to.rearrange("p (g k c) -> p g k c", g=2, k=KD)
                    if l < 2:
                        g, u = io["w_gate"][l], io["w_up"][l]
                    else:
                        g, u = io["ffn_w_in_2"][l - 2][:, 0:FF], io["ffn_w_in_2"][l - 2][:, FF:2 * FF]
                    for i, w in enumerate((g, u)):
                        sp.dma_start(dst[:, i], rows(w, 0, KD)[:, :, P * key[2]:P * key[2] + P]) \
                            .then_inc(*made(sem, key, by=16))
                else:
                    w = io["w_down"][l] if l < 2 else io["ffn_w_out_2"][l - 2]
                    f = down_chunks(l, key[2])[key[4]]
                    h = key[3]
                    sp.dma_start(to.rearrange("p (k c) -> p k c", k=len(f)),
                                 rows(w, f[0], len(f))[:, :, 512 * h:512 * h + 512]).then_inc(*made(sem, key, by=16))
                if n >= RAW:
                    if loads[used][0] == "win" and loads[used][2] == len(col_groups(loads[used][1])) - 1:
                        for spot, cs in ada_by.items():
                            if spot[0] == loads[used][1]:
                                for c in cs:
                                    ada_load(*c)
                    while beside_loads:
                        before = ada_place(*beside_loads[0])[2]
                        group, l2 = ada_group(ada_spot[beside_loads[0]])
                        free = 0 if group == "projection" else index[("wo", l2, len(out_loads(l2)) - 1)]
                        if used < (index[ada_spot[before]] if before else free):
                            break
                        ada_load(*beside_loads.pop(0))
            sp.wait_ge(*upto("final", 3))
            sp.dma_start(io["out"][0].rearrange("(t p) d -> p t d", p=P), X[:, 0:2, :]).then_inc(*made("out_written", by=16))
            sp.wait_ge(*upto("out_written"))

        @block.gpsimd
        def _(pool):
            nc.gpsimd.memset(ones[:, :], 1.0).then_inc(*made("ones_set"))

            with nc.allow_non_contiguous_dma(reason="eight gains to a partition"):
                for i in range(2):
                    for k, g in enumerate(("norm_mix_2", "norm_ffn_2")):
                        pool.dma_start(gcol[:, 2 * i + k, :], io[g][i].rearrange("(k p) -> p k", p=P)) \
                            .then_inc(*made("gains2_in", by=16))

            for l in range(4):
                pool.wait_ge(*upto("product", "h", l, "mix", tiles_of(l, "mix")[-1], 1))
                if l < 2:
                    pool.wait_ge(*upto("norm_low", l, "mix", tiles_of(l, "mix")[-1], 1))
                    pool.dma_start(TCS, io["t_cs"]).then_inc(*made("gains_in", l, by=16))
                    pool.dma_start(W4, io["w_four"][l].rearrange("(k p) c -> p k c", p=P)).then_inc(*made("gains_in", l, by=16))
                    for i, g in enumerate((io["q_norm"][l], io["k_norm"][l], io["hg_norm"][l])):
                        pool.dma_start(GROW3[:, i, :], g.partition_broadcast(P)).then_inc(*made("gains_in", l, by=16))
                    if l == 1:
                        for d in range(2):
                            pool.dma_start(LOGIT[:, d], io["hg_lb_logits"][d].partition_broadcast(P)) \
                                .then_inc(*made("logits_in", by=16))
                if l == 1:
                    pool.wait_ge(*upto("product", "m", 1, 1, 0))
                    pool.dma_start(DIST[:, :, :, :], io["t_dist"]).then_inc(*made("dist_in", by=16))
                    pool.dma_start(sinkn[:, :], io["a_sink_2"][0].partition_broadcast(P)).then_inc(*made("dist_in", by=16))
                if l in (1, 3):
                    pool.wait_ge(*drained(*stage_done(l, "ffn")))
                    g = io["final_norm"] if l == 1 else io["final_norm_2"]
                    pool.dma_start(grow[:, 0, :], g.partition_broadcast(P)).then_inc(*made("final_gain_in", l, by=16))

        @block.tensor
        def _(pe):
            tenants = []

            def open_bank(*key):
                b = len(tenants) % NBANKS
                if len(tenants) >= NBANKS:
                    pe.wait_ge(*drained(*tenants[-NBANKS]))
                tenants.append(key)
                count.banks[key] = b
                return bank[b]

            def mm(out, lhsT, rhs, start, stop):
                return nc.tensor.matmul(out, lhsT, rhs, start=start, stop=stop, skip_group_check=True)

            def mm3(out, left, right, first, last):
                (lh, ll), (rh, rl) = left, right
                mm(out, lh, rh, first, False)
                mm(out, lh, rl, False, False)
                return mm(out, ll, rh, False, last)

            def need_parts(key):
                pe.wait_ge(*upto("split_low", key))

            def turn(out, in_):
                k = in_.shape[0]
                return nc.tensor.transpose(out, in_, ident[0:k, 0:k])

            def modulation(l, j):
                if (l, j) == (0, 0):
                    pe.wait_ge(*upto("bias_in"))
                    pe.wait_ge(*upto("ones_set"))
                    pe.wait_ge(*upto("cond_ready"))
                direct = ada_engine(ada_spot[l, j], j) == "tensor"
                slot, w, _ = ada_place(l, j)
                if direct:
                    pe.wait_ge(*upto(f"ada_weights{slot}", l, j))
                else:
                    pe.wait_ge(*upto("ada_sum", l, j))
                    sums = ACC[:, sum_slot(l, j)[0]]
                ps = open_bank("mod", l, j)
                nc_, first_cond = len(conds_of(l, j)), conds_of(l, j)[0]
                row = ADA * l + j
                for c in range(2):
                    r = slice(P * c, P * c + P)
                    if direct:
                        for k in range(8):
                            mm(ps[:, 2 * c:2 * c + nc_], w[:, k, r], cond[:, first_cond:first_cond + nc_, k], k == 0, False)
                    for i in range(nc_):
                        o = ps[:, 2 * c + i:2 * c + i + 1]
                        if not direct:
                            mm(o, sums[:, i, r], ones[:, 0:1], True, False)
                        last = mm(o, BIAS[0:4 * ADA, r], ident[0:4 * ADA, row:row + 1], False, True)
                last.then_inc(*made("product", "mod", l, j))

            last_load = [None]

            def late(key):
                if last_load[0]:
                    beside(*last_load[0])
                last_load[0] = key

            def norm_turn(l, st):
                for t in tiles_of(l, st):
                    pe.wait_ge(*upto("normed", l, st, t))
                    for b in range(2):
                        ps = open_bank("h", l, st, t, b)
                        for i in range(4):
                            last = turn(ps[:, P * i:P * i + P], XN[:, t % 2, P * (4 * b + i):P * (4 * b + i) + P])
                        last.then_inc(*made("product", "h", l, st, t, b))

            def h_ready(l, st):
                for t in tiles_of(l, st):
                    for b in range(2):
                        pe.wait_ge(*upto("norm_low", l, st, t, b))

            def beside(*spot):
                for c in ada_by.get(spot, []):
                    modulation(*c)

            def project(l):
                h_ready(l, "mix")
                for j, (a, b) in enumerate(col_groups(l)):
                    key = ("win", l, j)
                    need_parts(key)
                    wh, wl = (w.rearrange("p (k c) -> p k c", k=KD) for w in parts(key))
                    for t in [t for j2, t in proj_jobs(l) if j2 == j]:
                        ps = open_bank("u", l, j, t)
                        r = slice(P * t, P * t + P)
                        for k in range(KD):
                            last = mm3(ps[:, 0:256], (HTH[:, k, r], HTL[:, k, r]), (wh[:, k, :], wl[:, k, :]), k == 0, k == KD - 1)
                        last.then_inc(*made("product", "u", l, j, t))
                    late(key)
                late(None)

            def need_u(l, t, a, b):
                for j, (a0, b0) in enumerate(col_groups(l)):
                    if a < b0 and a0 < b:
                        pe.wait_ge(*drained("u", l, j, t))

            def fourier(l, g):
                tt = (X_TILES, C_TILES)[g]
                for t in tt:
                    need_u(l, t, 0, 256)
                if g == 0:
                    pe.wait_ge(*upto("tables_in"))
                    pe.wait_ge(*upto("gains_in", l))
                for d in range(2):
                    ps = open_bank("fa", l, g, d)
                    for k in range(2):
                        last = mm(ps[:, :], U[:, tt[k], P * d:P * d + P], TCS[:, k, :], k == 0, k == 1)
                    last.then_inc(*made("product", "fa", l, g, d))
                ps = open_bank("fy", l, g)
                for d in range(2):
                    pe.wait_ge(*drained("fa", l, g, d))
                    for k in range(2):
                        last = mm(ps[:, N * d:N * d + N], tb_cols[:, k, :], FA[:, d, N * k:N * k + N], k == 0, k == 1)
                last.then_inc(*made("product", "fy", l, g))

            def fourier_out(l, g):
                pe.wait_ge(*drained("fy", l, g))
                ps = open_bank("ff", l, g)
                for c in range(2):
                    for k in range(2):
                        last = mm(ps[:, N * c:N * c + N], W4[:, k, P * c:P * c + P], U[:, 2 * g + k, 0:256], k == 0, k == 1)
                last.then_inc(*made("product", "ff", l, g))

            def head_turns(l):
                for t in tiles_of(l, "mix"):
                    beside(l, "heads", t)
                    pe.wait_ge(*upto("heads_ready", l, t))
                    if l >= 2:
                        need_u(l, t, 0, DH * HEADS_Q[l])
                    nq = HEADS_Q[l] // 2 if (l != 1 or t < 2) else 0
                    src = QN_of(l, t)
                    for b in range(0, nq, 4):
                        ps = open_bank("qT", l, t, b)
                        for i in range(4):
                            last = turn(ps[:, P * i:P * i + P], src[:, P * (b + i):P * (b + i) + P])
                        last.then_inc(*made("product", "qT", l, t, b))
                    for b in range(0, HEADS_K[l], 4):
                        ps = open_bank("kT", l, t, b)
                        for i in range(min(4, HEADS_K[l] - b)):
                            last = turn(ps[:, P * i:P * i + P], KDUP[:, P * (b + i):P * (b + i) + P])
                        last.then_inc(*made("product", "kT", l, t, b))

            def attention(l):
                units = attention_units(l)
                for t in tiles_of(l, "mix"):
                    for b in range(0, HEADS_Q[l] // 2 if (l != 1 or t < 2) else 0, 4):
                        pe.wait_ge(*drained("qT", l, t, b))
                    for b in range(0, HEADS_K[l], 4):
                        pe.wait_ge(*drained("kT", l, t, b))
                    need_u(l, t, *{2: (1280, 1536), 3: (1920, 2304)}.get(l, (OFF_V, OFF_Z)))

                def scores(n):
                    u = units[n]
                    r = slice(DH * u["half"], DH * u["half"] + DH)
                    ps = None
                    for i, (q, kv, s0, sn, at) in enumerate(u["keys"]):
                        if at % 512 == 0:
                            ps = open_bank("sc", l, n, at // 512)
                        last = mm(ps[:, at % 512:at % 512 + sn], QT[l][r, q, P * u["t"]:P * u["t"] + P],
                                  KT[l][r, kv, s0:s0 + sn], True, True)
                        if at % 512 + sn == 512 or i == len(u["keys"]) - 1:
                            last.then_inc(*made("product", "sc", l, n, at // 512))

                def turns(n):
                    u = units[n]
                    pe.wait_ge(*upto("probs", l, n))
                    for i in range(u["size"] // P):
                        if i % 4 == 0:
                            ps = open_bank("pt", l, n, i // 4)
                        last = turn(ps[:, P * (i % 4):P * (i % 4) + P], PB[:, n % 2, P * i:P * i + P])
                        if i % 4 == 3 or i == u["size"] // P - 1:
                            last.then_inc(*made("product", "pt", l, n, i // 4))

                groups = out_groups(l)

                def values(n):
                    u = units[n]
                    g = groups.index(u["og"])
                    for b in range((u["size"] + 511) // 512):
                        pe.wait_ge(*drained("pt", l, n, b))
                    if u["oc"] == 0 and g >= 2:
                        pe.wait_ge(*upto("attended", l, g - 2))
                    for i, (s, c) in enumerate(u["vals"]):
                        last = mm(obank[g % 2][:, DH * u["oc"]:DH * u["oc"] + DH], PT[:, n % 2, P * i:P * i + P],
                                  U[:, s, c:c + DH], i == 0, i == len(u["vals"]) - 1)
                    last.then_inc(*made("valued", l, n))

                for n in range(len(units) + 3):
                    if n < len(units):
                        scores(n)
                    if 1 <= n <= len(units):
                        turns(n - 1)
                    beside(l, "attention", n - ROUNDS)
                    if 2 <= n < len(units) + 2:
                        values(n - 2)

            def recurrence(l):
                steps = scan_steps(l)

                def prepare(s, t, d, has_out):
                    pe.wait_ge(*upto("gates", l, s))
                    pe.wait_ge(*upto("decays_low", l, s))
                    if s == 0 and l == 0:
                        pe.wait_ge(*upto("sums_set"))
                    if has_out:
                        if first_visit(l, s, t):
                            need_u(l, t, OFF_HQ, OFF_G)
                            ps = open_bank("qt2", l, t)
                            for p in range(2):
                                last = turn(ps[:, P * p:P * p + P], U[:, t, OFF_HQ + P * p:OFF_HQ + P * p + P])
                            last.then_inc(*made("product", "qt2", l, t))
                        ps = open_bank("kt2", l, s)
                        for p in range(2):
                            last = turn(ps[:, P * p:P * p + P], HK[:, P * p:P * p + P])
                        last.then_inc(*made("product", "kt2", l, s))
                        for p in range(2):
                            for b in range(2):
                                ps = open_bank("e", l, s, p, b)
                                r = slice(P * p, P * p + P)
                                mm(ps[:, :], LFH[:, r], SUMS[:, d, 512 * b:512 * b + 512], True, False)
                                mm(ps[:, :], LFL[:, r], SUMS[:, d, 512 * b:512 * b + 512], False, True) \
                                    .then_inc(*made("product", "e", l, s, p, b))
                    if s < 6:
                        ps = open_bank("sf", l, s)
                        mm(ps[:, 0:256], TAILS[:, d, :], LFH[:, :], True, False)
                        mm(ps[:, 0:256], TAILS[:, d, :], LFL[:, :], False, True)
                        for p in range(2):
                            last = mm(ps[:, 256 + p:257 + p], LF[:, P * p:P * p + P], ones[:, 0:1], True, True)
                        last.then_inc(*made("product", "sf", l, s))

                prepare(*steps[0])
                for n, (s, t, d, has_out) in enumerate(steps):
                    need_u(l, t, OFF_I, OFF_HQ)
                    if has_out:
                        for p in range(2):
                            for q in range(2):
                                pe.wait_ge(*upto("weighed", l, s, p, q))
                                hb = half_buffer(l, s, p, q)
                                for b in range(2):
                                    ps = open_bank("a", l, s, p, q, b)
                                    for i in range(2):
                                        j = 2 * b + i
                                        last = mm(ps[:, 256 * i:256 * i + 256], KW[:, p, 4 * q + j, :],
                                                  QW[:, hb, j].rearrange("p h c -> p (h c)"), True, True)
                                    last.then_inc(*made("product", "a", l, s, p, q, b))
                            if p == 0:
                                beside(l, "scan", s, 0)
                    else:
                        beside(l, "scan", s, 0)
                    beside(l, "scan", s, 1)
                    if n + 1 < len(steps):
                        prepare(*steps[n + 1])
                    if has_out:
                        o = obank[s % 2]
                        if s >= 2 and (l == 0 or s >= 6):
                            pe.wait_ge(*upto("scanned", l, s - 2))
                        for p in range(2):
                            if s >= 2:
                                pe.wait_ge(*drained("su", l, s - 2))
                                mm(o[:, P * p:P * p + P], QP[:, p, :], ST[:, d, p, :], True, False)
                            pe.wait_ge(*drained("a", l, s, p, 1, 1))
                            for h in (2 * p, 2 * p + 1):
                                last = mm(o[:, DH * h:DH * h + DH], AS[:, d, h, :], U[:, t, OFF_I + DH * h:OFF_I + DH * h + DH],
                                          s < 2, True)
                        last.then_inc(*made("read_out", l, s))
                    beside(l, "scan", s, 2)
                    beside(l, "scan", s, 3)
                    if s < 6:
                        pe.wait_ge(*upto("tailed", l, s))
                        ps = open_bank("su", l, s)
                        for p in range(2):
                            last = mm(ps[:, P * p:P * p + P], KS[:, P * p:P * p + P], U[:, t, OFF_I + P * p:OFF_I + P * p + P], True, True)
                        last.then_inc(*made("product", "su", l, s))

            def mixed_turns(l):
                for t in tiles_of(l, "ffn"):
                    if l < 2:
                        pe.wait_ge(*upto("mixed", l, t))
                    for g, og in enumerate(out_groups(l)):
                        if og[0] == t:
                            pe.wait_ge(*upto("attended", l, g))
                    for b, (k0, cols) in enumerate(mix_banks(l)):
                        ps = open_bank("m", l, t, b)
                        for i, c in enumerate(cols):
                            last = turn(ps[:, P * i:P * i + P], U[:, t, c:c + P])
                        last.then_inc(*made("product", "m", l, t, b))

            def gate_rows(l, st):
                for i in range(2 if l == 0 else 1):
                    for h in range(2):
                        pe.wait_ge(*upto("diagonal", l, st, i, h))
                        ps = open_bank("g", l, st, i, h)
                        mm(ps[:, :], ones[:, :], DIAG[:, i, h], True, True).then_inc(*made("product", "g", l, st, i, h))

            def project_out(l):
                for t in tiles_of(l, "ffn"):
                    for b in range(len(mix_banks(l))):
                        pe.wait_ge(*drained("m", l, t, b))
                if l < 2:
                    for g in range(2 if l == 0 else 1):
                        pe.wait_ge(*drained("ff", l, g))
                for j, (nk, nc_) in enumerate(out_loads(l)):
                    key = ("wo", l, j)
                    need_parts(key)
                    wh, wl = (w.rearrange("p (k c) -> p k c", k=nk) for w in parts(key))
                    for t in tiles_of(l, "ffn"):
                        ps = open_bank("x1", l, j, t)
                        r = slice(P * t, P * t + P)
                        for k in range(nk):
                            last = mm3(ps[:, 0:nc_], (HTH[:, k, r], HTL[:, k, r]), (wh[:, k, :], wl[:, k, :]), k == 0, k == nk - 1)
                        last.then_inc(*made("product", "x1", l, j, t))

            def open_down(l, half, h, t):
                if l == 0:
                    return open_bank("x2", l, half, h, t)
                if h:
                    pe.wait_ge(*drained("x2", l, half, 0, t))
                count.banks[("x2", l, half, h, t)] = NBANKS + t
                return obank[t]

            def feed_forward(l):
                n = P * len(tiles_of(l, "ffn"))
                ath, atl = hidden[halves(l)]
                h_ready(l, "ffn")
                for half in range(halves(l)):
                    fs = hidden_tiles(l, half)
                    for f in fs:
                        key = ("gu", l, f)
                        need_parts(key)
                        wh, wl = (w.rearrange("p (g k c) -> p g k c", g=2, k=KD) for w in parts(key))
                        for g, name in enumerate(("gate", "up")):
                            ps = open_bank(name, l, f)
                            for k in range(KD):
                                last = mm3(ps[:, 0:n], (wh[:, g, k, :], wl[:, g, k, :]), (HTH[:, k, 0:n], HTL[:, k, 0:n]),
                                           k == 0, k == KD - 1)
                            last.then_inc(*made("product", name, l, f))
                        late(key)
                    chunks = down_chunks(l, half)
                    for h in range(2):
                        ps = {t: open_down(l, half, h, t) for t in tiles_of(l, "ffn")}
                        for c, f4 in enumerate(chunks):
                            key = ("dn", l, half, h, c)
                            need_parts(key)
                            wh, wl = (w.rearrange("p (k c) -> p k c", k=len(f4)) for w in parts(key))
                            if h == 0:
                                pe.wait_ge(*upto("hidden", l, f4[-1]))
                            for t in tiles_of(l, "ffn"):
                                r = slice(P * t, P * t + P)
                                for k, f in enumerate(f4):
                                    last = mm3(ps[t][:, :], (ath[:, f - fs[0], r], atl[:, f - fs[0], r]), (wh[:, k, :], wl[:, k, :]),
                                               f == fs[0], f == fs[-1])
                                if c == len(chunks) - 1:
                                    last.then_inc(*made("product", "x2", l, half, h, t))
                            if c < len(chunks) - 1:
                                last.then_inc(*made("down_part", *key[1:]))
                            late(key)
                late(None)

            def QN_of(l, t):
                return QN if l < 2 else U[:, t, :]

            pe.wait_ge(*upto("ident_in"))
            for j in START_ORDER:
                modulation(0, j)
            for l in range(4):
                norm_turn(l, "mix")
                project(l)
                if l < 2:
                    for g in range(2 if l == 0 else 1):
                        fourier(l, g)
                head_turns(l)
                attention(l)
                if l < 2:
                    recurrence(l)
                    for g in range(2 if l == 0 else 1):
                        fourier_out(l, g)
                gate_rows(l, "mix")
                mixed_turns(l)
                project_out(l)
                norm_turn(l, "ffn")
                gate_rows(l, "ffn")
                feed_forward(l)

        @block.scalar
        def _(act):
            def take(*key):
                act.wait_ge(*upto("product", *key))
                return psum(*key)

            def split(n):
                if n < len(loads):
                    act.wait_ge(*upto(f"weights{n % RAW}", loads[n]))
                    if n >= HIGH:
                        act.wait_ge(*last_use(loads[n - HIGH]))
                    nc.scalar.activation(parts(loads[n])[0], raw_slot(loads[n]), ACT.Copy).then_inc(*made("split_high", loads[n]))

            def beside(*spot):
                for c in ada_by.get(spot, []):
                    modulation(*c)

            last_load = [None]

            def late(key):
                if last_load[0]:
                    beside(*last_load[0])
                last_load[0] = key

            def modulation(l, j):
                ps = take("mod", l, j)
                nc_ = len(conds_of(l, j))
                nc.scalar.activation(modc[:, l, 2 * j:2 * j + 2, 0:nc_],
                                     ps[:, 0:4].rearrange("p (c i) -> p c i", i=2)[:, :, 0:nc_], ACT.Copy) \
                    .then_inc(*made("drained_act", "mod", l, j))

            def squares(l, st, tiles):
                for n, t in enumerate(tiles):
                    if st == "mix" and l == 0:
                        act.wait_ge(*upto("x_in"))
                    elif st == "mix" and l == 2:
                        act.wait_ge(*upto("final", 1))
                    elif st == "ffn":
                        act.wait_ge(*drained(*stage_done(l, "mix")))
                    else:
                        m = l if st == "final" else l - 1
                        act.wait_ge(*drained(*stage_done(m, "ffn")))
                    if n >= 2:
                        act.wait_ge(*upto("squared", l, st, tiles[n - 2]))
                    nc.scalar.activation(XN[:, t % 2, :], X[:, t, :], ACT.Square, accum_out=lsum[:, 0, t:t + 1]) \
                        .then_inc(*made("squared", l, st, t))

            def norm_take(l, st):
                act.wait_ge(*upto("scales", l, st))
                base = 0 if st == "mix" else 24
                for t in tiles_of(l, st):
                    i = cond_of_tile(t) if l < 2 else 0
                    if last_norm[0]:
                        act.wait_ge(*upto("norm_low", *last_norm[0], 0))
                    ps = take("h", l, st, t, 0)
                    for k in range(4):
                        last = nc.scalar.activation(G[:, 0, P * k:P * k + P], ps[:, P * k:P * k + P], ACT.Identity,
                                                    scale=scl[:, i, k:k + 1], bias=modc[:, l, base + k, i:i + 1])
                    last.then_inc(*made("drained_act", "h", l, st, t, 0))
                    for b in range(2):
                        act.wait_ge(*drained("h", l, st, t, b))
                        nc.scalar.activation(HTH[:, 4 * b:4 * b + 4, P * t:P * t + P],
                                             G[:, b, :].rearrange("p (k c) -> p k c", k=4), ACT.Copy) \
                            .then_inc(*made("norm_high", l, st, t, b))
                    last_norm[0] = (l, st, t)

            last_norm = [None]

            def project(l):
                for j in range(len(col_groups(l))):
                    for t in [t for j2, t in proj_jobs(l) if j2 == j]:
                        ps = take("u", l, j, t)
                        a, b = col_groups(l)[j]
                        nc.scalar.activation(U[:, t, a:b], ps[:, 0:b - a], ACT.Copy).then_inc(*made("drained_act", "u", l, j, t))
                    split(index[("win", l, j)] + HIGH)
                    late(("win", l, j))
                late(None)

            def fourier(l, g):
                for d in range(2):
                    ps = take("fa", l, g, d)
                    nc.scalar.activation(FA[:, d, :], ps[:, :], ACT.Copy).then_inc(*made("drained_act", "fa", l, g, d))

            def fourier_out(l, g):
                ps = take("ff", l, g)
                nc.scalar.activation(HTH[:, 0:2, N * g:N * g + N], ps[:, :].rearrange("p (c n) -> p c n", c=2), ACT.Copy) \
                    .then_inc(*made("mixed_high", "ff", l, g))

            def head_turns(l):
                for t in tiles_of(l, "mix"):
                    beside(l, "heads", t)
                    nq = HEADS_Q[l] // 2 if (l != 1 or t < 2) else 0
                    for b in range(0, nq, 4):
                        ps = take("qT", l, t, b)
                        nc.scalar.activation(QT[l][:, b:b + 4, P * t:P * t + P], ps[:, :].rearrange("p (k c) -> p k c", k=4),
                                             ACT.Copy, scale=1.0 if l < 2 else 0.125) \
                            .then_inc(*made("drained_act", "qT", l, t, b))
                    for b in range(0, HEADS_K[l], 4):
                        n = min(4, HEADS_K[l] - b)
                        ps = take("kT", l, t, b)
                        nc.scalar.activation(KT[l][:, b:b + n, P * t:P * t + P],
                                             ps[:, 0:P * n].rearrange("p (k c) -> p k c", k=n), ACT.Copy) \
                            .then_inc(*made("drained_act", "kT", l, t, b))

            def attention(l):
                units = attention_units(l)
                groups = out_groups(l)

                def probs(n):
                    u = units[n]
                    g = groups.index(u["og"])
                    act.wait_ge(*upto("maximum", l, n))
                    if n >= 2:
                        for b in range((units[n - 2]["size"] + 511) // 512):
                            act.wait_ge(*upto("product", "pt", l, n - 2, b))
                    src = SB[:, n % 2, 0:u["size"]] if u["bias"] else psum("sc", l, n, 0)[:, 0:u["size"]]
                    col = u["oc"]
                    if u["oc"] == 0 and g >= 2:
                        act.wait_ge(*upto("attended", l, g - 2))
                    nc.scalar.activation(PB[:, n % 2, 0:u["size"]], src, ACT.Exp, bias=nmax[:, g % 2, col:col + 1],
                                         accum_out=lsum[:, g % 2, col:col + 1]) \
                        .then_inc(*made("probs", l, n))
                    if l == 2:
                        h = u["h"]
                        nc.scalar.activation(sinke[:, g % 2, col:col + 1], sinkn[:, h:h + 1], ACT.Exp, scale=-1.0,
                                             bias=nmax[:, g % 2, col:col + 1]).then_inc(*made("sink_term", l, n))

                def take_turned(n):
                    u = units[n]
                    for b in range((u["size"] + 511) // 512):
                        if (n + b) % 2 == 0 or u["size"] == 512:
                            w = min(512, u["size"] - 512 * b)
                            ps = take("pt", l, n, b)
                            if n >= 2:
                                act.wait_ge(*upto("valued", l, n - 2))
                            nc.scalar.activation(PT[:, n % 2, 512 * b:512 * b + w], ps[:, 0:w], ACT.Copy) \
                                .then_inc(*made("drained_act", "pt", l, n, b))

                for n in range(len(units) + 3):
                    if n < len(units):
                        probs(n)
                    if 1 <= n <= len(units):
                        take_turned(n - 1)
                    beside(l, "attention", n - ROUNDS)

            def recurrence(l):
                steps = scan_steps(l)

                def gates(n):
                    s, t, d, has_out = steps[n]
                    act.wait_ge(*upto("gate_in", l, s))
                    nc.scalar.activation(HE, HS, ACT.Exp, scale=-1.0).then_inc(*made("gate_exp", l, s))
                    act.wait_ge(*upto("gates", l, s))
                    if n:
                        s2 = steps[n - 1][0]
                        act.wait_ge(*(upto("product", "sf", l, s2) if s2 < 6 else upto("product", "e", l, s2, 1, 1)))
                    nc.scalar.activation(LF, HS, ACT.Ln).then_inc(*made("decays", l, s))
                    act.wait_ge(*upto("decays", l, s))
                    nc.scalar.activation(LFH[:, :], LF, ACT.Copy).then_inc(*made("decays_high", l, s))

                gates(0)
                for n, (s, t, d, has_out) in enumerate(steps):
                    if has_out:
                        if first_visit(l, s, t):
                            ps = take("qt2", l, t)
                            nc.scalar.activation(qt2(t), ps[:, 0:256].rearrange("p (k c) -> p k c", k=2), ACT.Copy) \
                                .then_inc(*made("drained_act", "qt2", l, t))
                        ps = take("kt2", l, s)
                        nc.scalar.activation(KT2, ps[:, 0:256].rearrange("p (k c) -> p k c", k=2), ACT.Copy) \
                            .then_inc(*made("drained_act", "kt2", l, s))
                        for p in range(2):
                            for b in range(2):
                                ps = take("e", l, s, p, b)
                                nc.scalar.activation(HW[:, p, 1 + 4 * b:5 + 4 * b, :],
                                                     ps[:, :].rearrange("p (j c) -> p j c", j=4), ACT.Exp) \
                                    .then_inc(*made("drained_act", "e", l, s, p, b))
                    if s < 6:
                        ps = take("sf", l, s)
                        nc.scalar.activation(SF, ps[:, 0:256], ACT.Exp)
                        nc.scalar.activation(TOT[:, s % 2, :], ps[:, 256:258], ACT.Exp).then_inc(*made("drained_act", "sf", l, s))
                    if n:
                        beside(l, "scan", steps[n - 1][0], 2)
                        beside(l, "scan", steps[n - 1][0], 3)
                    if n + 1 < len(steps):
                        gates(n + 1)
                    beside(l, "scan", s, 0)
                    beside(l, "scan", s, 1)
                beside(l, "scan", steps[-1][0], 2)
                beside(l, "scan", steps[-1][0], 3)

            def readout(l, t):
                act.wait_ge(*upto("gain_done", l, t))
                act.wait_ge(*drained("u", l, OFF_G // 256, t))
                nc.scalar.activation(HE, U[:, t, OFF_G:OFF_G + 256], ACT.Exp, scale=-1.0).then_inc(*made("silu_exp", l, t))

            def mixed_turns(l, t):
                for b, (k0, cols) in enumerate(mix_banks(l)):
                    n = len(cols)
                    ps = take("m", l, t, b)
                    nc.scalar.activation(HTH[:, k0:k0 + n, P * t:P * t + P],
                                         ps[:, 0:P * n].rearrange("p (k c) -> p k c", k=n), ACT.Copy) \
                        .then_inc(*made("mixed_high", "m", l, t, b))

            def gate_rows(l, st):
                for i in range(2 if l == 0 else 1):
                    for h in range(2):
                        ps = take("g", l, st, i, h)
                        if st == "ffn":
                            act.wait_ge(*drained(*stage_done(l, "mix")))
                        nc.scalar.activation(grow[:, i, 512 * h:512 * h + 512], ps[:, :], ACT.Copy) \
                            .then_inc(*made("drained_act", "g", l, st, i, h))

            def project_out(l):
                for j in range(len(out_loads(l))):
                    split(index[("wo", l, j)] + HIGH)

            def feed_forward(l):
                n = P * len(tiles_of(l, "ffn"))
                ath, atl = hidden[halves(l)]
                for half in range(halves(l)):
                    fs = hidden_tiles(l, half)

                    def high(f):
                        act.wait_ge(*drained("up", l, f))
                        if f == fs[0] and half:
                            act.wait_ge(*last_use(("dn", l, 0, 1, len(down_chunks(l, 0)) - 1)))
                        nc.scalar.activation(ath[:, f - fs[0], 0:n], G[:, f % 2, 0:n], ACT.Copy).then_inc(*made("hidden_high", l, f))

                    for f in fs:
                        ps = take("gate", l, f)
                        if f >= 2:
                            act.wait_ge(*upto("hidden", l, f - 2))
                        nc.scalar.activation(G[:, f % 2, 0:n], ps[:, 0:n], ACT.Silu).then_inc(*made("drained_act", "gate", l, f))
                        if f > fs[0]:
                            high(f - 1)
                        split(index[("gu", l, f)] + HIGH)
                        late(("gu", l, f))
                    high(fs[-1])
                    for h in range(2):
                        for c in range(len(down_chunks(l, half))):
                            key = ("dn", l, half, h, c)
                            split(index[key] + HIGH)
                            late(key)
                late(None)

            act.wait_ge(*upto("cond_in"))
            nc.scalar.activation(condt[:, 0, :], cond[:, :, :].rearrange("p i k -> p (i k)"), ACT.Exp, scale=-1.0) \
                .then_inc(*made("cond_exp"))
            squares(0, "mix", tiles_of(0, "mix"))
            for n in range(HIGH):
                split(n)
            for j in START_ORDER:
                modulation(0, j)
            act.wait_ge(*upto("stage_in"))
            nc.scalar.activation(SUMS[:, :, :].rearrange("p d c -> p (d c)"), STAGE[:, 0:2048], ACT.Copy)
            nc.scalar.activation(tb_masks[:, :, :, :].rearrange("p d j c -> p (d j c)"), STAGE[:, 2304:4352], ACT.Copy)
            nc.scalar.activation(TAILS[:, :, :].rearrange("p d c -> p (d c)"), STAGE[:, 2048:2304], ACT.Copy) \
                .then_inc(*made("sums_set"))
            for l in range(4):
                if l:
                    squares(l, "mix", tiles_of(l, "mix"))
                norm_take(l, "mix")
                project(l)
                if l < 2:
                    if l == 1:
                        act.wait_ge(*upto("logits_less"))
                        nc.scalar.activation(LOGIT, LOGIT, ACT.Exp).then_inc(*made("logits_exp"))
                    for g in range(2 if l == 0 else 1):
                        fourier(l, g)
                head_turns(l)
                attention(l)
                if l < 2:
                    recurrence(l)
                    for g in range(2 if l == 0 else 1):
                        fourier_out(l, g)
                gate_rows(l, "mix")
                tiles = tiles_of(l, "ffn")
                for n, t in enumerate(tiles):
                    if l < 2:
                        readout(l, t)
                    if n:
                        mixed_turns(l, tiles[n - 1])
                mixed_turns(l, tiles[-1])
                project_out(l)
                squares(l, "ffn", tiles_of(l, "ffn"))
                norm_take(l, "ffn")
                gate_rows(l, "ffn")
                feed_forward(l)
                if l in (1, 3):
                    squares(l, "final", X_TILES)

        @block.vector
        def _(dve):
            V = nc.vector

            def link(ins):
                ins.then_inc(*made("dve_link"))
                dve.wait_ge(count.sem("dve_link"), count.count["dve_link"])

            def take(*key):
                dve.wait_ge(*upto("product", *key))
                return psum(*key)

            def as_float(ap):
                return ap.bitcast(F32)

            def split(n):
                if n < len(loads):
                    dve.wait_ge(*upto("split_high", loads[n]))
                    high, low = parts(loads[n])
                    V.tensor_tensor(low, raw_slot(loads[n]), as_float(high), ALU.subtract).then_inc(*made("split_low", loads[n]))

            def ada_sum(l, j, k0=0, k1=8):
                slot, w, _ = ada_place(l, j)
                (b, user), cs = sum_slot(l, j), conds_of(l, j)
                if k0 == 0:
                    dve.wait_ge(*upto(f"ada_weights{slot}", l, j))
                    if user:
                        dve.wait_ge(*upto("product", "mod", *user))
                for k in range(k0, k1):
                    for i in range(len(cs)):
                        a = ACC[:, b, i, :]
                        if k == 0:
                            last = V.tensor_scalar(a, w[:, 0, :], cond[:, cs[i], 0:1], None, ALU.mult)
                        else:
                            last = V.scalar_tensor_tensor(out=a, in0=w[:, k, :], scalar=cond[:, cs[i], k:k + 1], in1=a,
                                                          op0=ALU.mult, op1=ALU.add)
                    if k < 7:
                        link(last)
                if k1 == 8:
                    last.then_inc(*made("ada_sum", l, j))

            def beside(*spot):
                for c in ada_by.get(spot, []):
                    ada_sum(*c)

            def refine(*key, n):
                dve.wait_ge(*upto("mean_square", *key))
                m, half, root, t = ms[:, 0:n], half_ms[:, 0:n], rs[:, 0:n], nw[:, 0:n]
                V.tensor_scalar(half, m, -0.5, None, ALU.mult)
                link(V.tensor_scalar(root.bitcast(I32), m.bitcast(I32), 1, None, ALU.arith_shift_right))
                link(V.tensor_scalar(root.bitcast(I32), root.bitcast(I32), -1, 0x5F3759DF, ALU.mult, ALU.add))
                for _ in range(3):
                    link(V.tensor_tensor(t, root, root, ALU.mult))
                    link(V.tensor_tensor(t, t, half, ALU.mult))
                    link(V.scalar_tensor_tensor(out=root, in0=t, scalar=1.5, in1=root, op0=ALU.add, op1=ALU.mult))

            def row_norms(l, st, tiles):
                for t in tiles:
                    dve.wait_ge(*upto("squared", l, st, t))
                n = len(tiles)
                V.tensor_scalar(ms[:, 0:n], lsum[:, 0, 0:n], 1.0 / D, EPS, ALU.mult, ALU.add) \
                    .then_inc(*made("mean_square", l, st))
                refine(l, st, n=n)

            def scales(l, st):
                base = 8 if st == "mix" else 32
                n = len(conds_of(l, 0 if st == "mix" else 16))
                for j in range(STARTING) if st == "mix" else range(STARTING, ADA):
                    dve.wait_ge(*drained("mod", l, j))
                src = modc[:, l, base:base + 8, 0:n].rearrange("p k i -> p i k")
                if l < 2:
                    V.tensor_scalar(scl[:, 0:n, :], src, 1.0, None, ALU.add).then_inc(*made("scales", l, st))
                else:
                    dve.wait_ge(*upto("gains2_in"))
                    link(V.tensor_scalar(scl[:, 0:n, :], src, 1.0, None, ALU.add))
                    V.tensor_tensor(scl[:, 0, :], scl[:, 0, :], gcol[:, 2 * (l - 2) + (st == "ffn"), :], ALU.mult) \
                        .then_inc(*made("scales", l, st))

            last_norm = [None]

            def norm(l, st):
                tiles = tiles_of(l, st)
                if st == "ffn":
                    dve.wait_ge(*drained("h", l, "mix", tiles_of(l, "mix")[-1], 1))
                elif l:
                    dve.wait_ge(*drained("h", l - 1, "ffn", tiles_of(l - 1, "ffn")[-1], 1))
                row_norms(l, st, tiles)
                for n, t in enumerate(tiles):
                    if n >= 2:
                        dve.wait_ge(*upto("product", "h", l, st, tiles[n - 2], 1))
                    V.tensor_scalar(XN[:, t % 2, :], X[:, t, :], rs[:, t:t + 1], None, ALU.mult) \
                        .then_inc(*made("normed", l, st, t))
                    if n == 1:
                        if (l, st) == (0, "mix"):
                            for j in range(HIGH):
                                split(j)
                        scales(l, st)
                        dve.wait_ge(*upto("scales", l, st))
                    if n:
                        norm_take(l, st, tiles[n - 1])
                norm_take(l, st, tiles[-1])

            def norm_take(l, st, t):
                base = 0 if st == "mix" else 24
                i = cond_of_tile(t) if l < 2 else 0
                ps = take("h", l, st, t, 1)
                if last_norm[0]:
                    dve.wait_ge(*upto("norm_low", *last_norm[0], 1))
                last_norm[0] = (l, st, t)
                for k in range(4):
                    last = V.tensor_scalar(G[:, 1, P * k:P * k + P], ps[:, P * k:P * k + P], scl[:, i, 4 + k:5 + k],
                                           modc[:, l, base + 4 + k, i:i + 1], ALU.mult, ALU.add)
                last.then_inc(*made("drained_dve", "h", l, st, t, 1))
                for b in range(2):
                    dve.wait_ge(*upto("norm_high", l, st, t, b))
                    r = slice(P * t, P * t + P)
                    V.tensor_tensor(HTL[:, 4 * b:4 * b + 4, r], G[:, b, :].rearrange("p (k c) -> p k c", k=4),
                                    as_float(HTH[:, 4 * b:4 * b + 4, r]), ALU.subtract).then_inc(*made("norm_low", l, st, t, b))

            def project(l):
                for j in range(len(col_groups(l))):
                    split(index[("win", l, j)] + HIGH)
                    beside("win", l, j)

            def project_out(l):
                for j, (_, n) in enumerate(out_loads(l)):
                    for t in tiles_of(l, "ffn"):
                        i = cond_of_tile(t) if l < 2 else 0
                        dve.wait_ge(*drained("g", l, "mix", i, n * j // 512))
                        ps = take("x1", l, j, t)
                        link(V.tensor_tensor(ps[:, 0:n], ps[:, 0:n], grow[:, i, n * j:n * j + n], ALU.mult))
                        x = X[:, t, n * j:n * j + n]
                        V.tensor_tensor(x, ps[:, 0:n], x, ALU.add).then_inc(*made("drained_dve", "x1", l, j, t))
                    split(index[("wo", l, j)] + HIGH)

            def need_u(l, t, a, b):
                for j, (a0, b0) in enumerate(col_groups(l)):
                    if a < b0 and a0 < b:
                        dve.wait_ge(*drained("u", l, j, t))

            def fourier(l, g):
                ps = take("fy", l, g)
                V.tensor_copy(U[:, 2 * g:2 * g + 2, 0:256], ps[:, :].rearrange("p (d n) -> p d n", d=2)) \
                    .then_inc(*made("drained_dve", "fy", l, g))

            def fourier_out(l, g):
                dve.wait_ge(*upto("mixed_high", "ff", l, g))
                V.tensor_tensor(HTL[:, 0:2, N * g:N * g + N], psum("ff", l, g)[:, :].rearrange("p (c n) -> p c n", c=2),
                                as_float(HTH[:, 0:2, N * g:N * g + N]), ALU.subtract).then_inc(*made("drained_dve", "ff", l, g))

            def mixed_turns(l, t):
                for b, (k0, cols) in enumerate(mix_banks(l)):
                    n = len(cols)
                    dve.wait_ge(*upto("mixed_high", "m", l, t, b))
                    r = slice(P * t, P * t + P)
                    V.tensor_tensor(HTL[:, k0:k0 + n, r], psum("m", l, t, b)[:, 0:P * n].rearrange("p (k c) -> p k c", k=n),
                                    as_float(HTH[:, k0:k0 + n, r]), ALU.subtract).then_inc(*made("drained_dve", "m", l, t, b))

            def gains(l):
                dve.wait_ge(*upto("gains_in", l))
                V.tensor_scalar(G10[:, 0:8, :], GROW3[:, 0, :].unsqueeze(1).broadcast_to([P, 8, DH]), 0.125, None, ALU.mult)
                link(V.tensor_copy(G10[:, 8:10, :], GROW3[:, 1, :].unsqueeze(1).broadcast_to([P, 2, DH])))
                if l == 0:
                    dve.wait_ge(*upto("tables_in"))
                    return
                dve.wait_ge(*upto("logits_in"))
                link(V.tensor_tensor(lb[:, :, :], LOGIT[:, :, 0, :], LOGIT[:, :, 1, :], ALU.max))
                V.tensor_tensor(LOGIT, LOGIT, lb[:, :, :].unsqueeze(2).broadcast_to([P, 2, 2, 256]), ALU.subtract) \
                    .then_inc(*made("logits_less"))
                dve.wait_ge(*upto("logits_exp"))
                link(V.tensor_tensor(lb[:, :, :], LOGIT[:, :, 0, :], LOGIT[:, :, 1, :], ALU.add))
                link(V.reciprocal(lb[:, :, :], lb[:, :, :]))
                link(V.tensor_tensor(lb[:, :, :], LOGIT[:, :, 1, :], lb[:, :, :], ALU.mult))

            def heads(l):
                tiles = tiles_of(l, "mix")
                for n, t in enumerate(tiles):
                    if l >= 2:
                        nk, c = HEADS_K[l], DH * HEADS_Q[l]
                        need_u(l, t, c, c + DH * nk)
                        if n:
                            dve.wait_ge(*upto("product", "kT", l, tiles[n - 1], 4 * ((nk - 1) // 4)))
                        V.tensor_copy(KDUP[:, 0:P * nk].rearrange("p (k a c) -> p k a c", k=nk, a=2),
                                      U[:, t, c:c + DH * nk].rearrange("p (k c) -> p k c", k=nk)
                                      .unsqueeze(2).broadcast_to([P, nk, 2, DH])).then_inc(*made("heads_ready", l, t))
                        continue
                    has_q = l == 0 or t < 2
                    nh, c = (10, OFF_Q) if has_q else (2, OFF_K)
                    g0 = 10 - nh
                    need_u(l, t, c, OFF_V)
                    if n:
                        dve.wait_ge(*upto("product", "kT", l, tiles[n - 1], 0))
                    u = U[:, t, c:c + DH * nh].rearrange("p (h c) -> p h c", h=nh)
                    qn = QN[:, 0:DH * nh].rearrange("p (h c) -> p h c", h=nh)
                    qm = QM[:, 0:DH * nh].rearrange("p (h c) -> p h c", h=nh)
                    link(V.tensor_tensor(qn, u, u, ALU.mult))
                    link(V.tensor_reduce(nw[:, 0:nh], qn, AX.X, ALU.add))
                    V.tensor_scalar(ms[:, 0:nh], nw[:, 0:nh], 1.0 / DH, EPS, ALU.mult, ALU.add) \
                        .then_inc(*made("mean_square", l, "heads", t))
                    refine(l, "heads", t, n=nh)
                    link(V.tensor_tensor(qn, u, rs[:, 0:nh].unsqueeze(2).broadcast_to([P, nh, DH]), ALU.mult))
                    link(V.tensor_tensor(qn, qn, G10[:, g0:10, :], ALU.mult))
                    if t < 2:
                        v = QN.rearrange("p (h a s c) -> p h a s c", h=10, a=2, s=2)
                        w = QR.rearrange("p (h a s c) -> p h a s c", h=10, a=2, s=2)
                        sn = tb_sin[:, t, :].rearrange("p (a s c) -> p a s c", a=2, s=2)
                        for s in range(2):
                            V.tensor_tensor(w[:, :, :, s, :], v[:, :, :, 1 - s, :],
                                            sn[:, :, s, :].unsqueeze(1).broadcast_to([P, 10, 2, 16]), ALU.mult)
                        link(V.tensor_tensor(qm, qn, tb_cos[:, t, :].unsqueeze(1).broadcast_to([P, 10, DH]), ALU.mult))
                        link(V.tensor_tensor(qn, qm, QR.rearrange("p (h c) -> p h c", h=10), ALU.add))
                    V.tensor_copy(KDUP[:, 0:256].rearrange("p (k a c) -> p k a c", k=2, a=2),
                                  qn[:, nh - 2:nh, :].unsqueeze(2).broadcast_to([P, 2, 2, DH])) \
                        .then_inc(*made("heads_ready", l, t))

            def attention(l):
                units = attention_units(l)
                groups = out_groups(l)
                if l == 2:
                    dve.wait_ge(*upto("dist_in"))
                    link(V.tensor_scalar(sinkn[:, :], sinkn[:, :], -1.0, None, ALU.mult))

                def maximum(n):
                    u = units[n]
                    g, col = groups.index(u["og"]), u["oc"]
                    nm = nmax[:, g % 2, col:col + 1]
                    for b in range((u["size"] + 511) // 512):
                        take("sc", l, n, b)
                    if n >= 2:
                        dve.wait_ge(*upto("probs", l, n - 2))
                    if u["oc"] == 0 and g >= 2:
                        dve.wait_ge(*upto("attended", l, g - 2))
                    if u["bias"] is None:
                        V.tensor_reduce(nm, psum("sc", l, n, 0)[:, 0:u["size"]], AX.X, ALU.max, negate=True) \
                            .then_inc(*made("maximum", l, n))
                        return
                    for i, (g_, slope) in enumerate(u["bias"]):
                        at = u["keys"][i][4]
                        last = V.scalar_tensor_tensor(out=SB[:, n % 2, at:at + N], in0=DIST[:, g_, u["t"], :], scalar=slope,
                                                      in1=psum("sc", l, n, at // 512)[:, at % 512:at % 512 + N],
                                                      op0=ALU.mult, op1=ALU.add)
                        if at % 512 == 256 or i == len(u["bias"]) - 1:
                            last.then_inc(*made("drained_dve", "sc", l, n, at // 512))
                    dve.wait_ge(*count_now("drained_dve"))
                    last = V.tensor_reduce(nm, SB[:, n % 2, 0:u["size"]], AX.X, ALU.max, negate=True)
                    if l == 2:
                        link(last)
                        last = V.tensor_tensor(nm, nm, sinkn[:, u["h"]:u["h"] + 1], ALU.min)
                    last.then_inc(*made("maximum", l, n))

                def take_turned(n):
                    u = units[n]
                    for b in range((u["size"] + 511) // 512):
                        if not ((n + b) % 2 == 0 or u["size"] == 512):
                            w = min(512, u["size"] - 512 * b)
                            ps = take("pt", l, n, b)
                            if n >= 2:
                                dve.wait_ge(*upto("valued", l, n - 2))
                            V.tensor_copy(PT[:, n % 2, 512 * b:512 * b + w], ps[:, 0:w]).then_inc(*made("drained_dve", "pt", l, n, b))

                def normalise(n):
                    u = units[n]
                    g = groups.index(u["og"])
                    dve.wait_ge(*upto("valued", l, n))
                    if l == 2:
                        dve.wait_ge(*upto("sink_term", l, n))
                        link(V.tensor_tensor(lsum[:, g % 2, 0:8], lsum[:, g % 2, 0:8], sinke[:, g % 2, 0:8], ALU.add))
                    link(V.reciprocal(rinv[:, :], lsum[:, g % 2, 0:8]))
                    c = OUT_COL[l] + 512 * u["og"][1]
                    V.tensor_tensor(U[:, u["t"], c:c + 512].rearrange("p (h c) -> p h c", h=8),
                                    obank[g % 2][:, :].rearrange("p (h c) -> p h c", h=8),
                                    rinv[:, :].unsqueeze(2).broadcast_to([P, 8, DH]), ALU.mult) \
                        .then_inc(*made("attended", l, g))

                for n in range(len(units) + 3):
                    if n < len(units):
                        maximum(n)
                    if 1 <= n <= len(units):
                        take_turned(n - 1)
                    for c in ada_by.get((l, "attention", n - n % ROUNDS), []):
                        ada_sum(*c, *((0, 3), (3, 6), (6, 8))[n % ROUNDS])
                    if n >= 3 and units[n - 3]["oc"] == 7:
                        normalise(n - 3)

            def count_now(name):
                return count.sem(name), count.count[name]

            def recurrence(l):
                steps = scan_steps(l)
                V.memset(ST, 0.0)
                V.memset(AS, 0.0)
                V.memset(QW, 0.0)
                link(V.memset(HW[:, :, 0, :], 1.0))

                def gates(n):
                    s, t, d, has_out = steps[n]
                    need_u(l, t, OFF_Z + 256 * d, OFF_Z + 256 * d + 256)
                    if n:
                        dve.wait_ge(*upto("decays", l, steps[n - 1][0]))
                        if steps[n - 1][3]:
                            dve.wait_ge(*upto("product", "kt2", l, steps[n - 1][0]))
                    V.tensor_scalar(HS, U[:, t, OFF_Z + 256 * d:OFF_Z + 256 * d + 256], -80.0, None, ALU.max) \
                        .then_inc(*made("gate_in", l, s))
                    dve.wait_ge(*upto("gate_exp", l, s))
                    link(V.tensor_scalar(HS, HE, 1.0, None, ALU.add))
                    link(V.reciprocal(HS, HS))
                    if l:
                        link(V.tensor_tensor(HK, HS, lb[:, d, :], ALU.mult))
                        link(V.tensor_tensor(HS, HS, HK, ALU.subtract))
                    last = V.tensor_tensor(HK, HS, HE, ALU.mult)
                    if l:
                        link(last)
                        last = V.tensor_tensor(HS, HS, lb[:, d, :], ALU.add)
                    last.then_inc(*made("gates", l, s))

                def low(n):
                    s = steps[n][0]
                    dve.wait_ge(*upto("decays_high", l, s))
                    V.tensor_tensor(LFL[:, :], LF, as_float(LFH[:, :]), ALU.subtract).then_inc(*made("decays_low", l, s))

                gates(0)
                low(0)
                for n, (s, t, d, has_out) in enumerate(steps):
                    if s < 6:
                        dve.wait_ge(*drained("sf", l, s))
                        if n:
                            dve.wait_ge(*upto("product", "su", l, s - 1))
                        V.tensor_tensor(KS, HK, SF, ALU.mult).then_inc(*made("tailed", l, s))
                        dve.wait_ge(*upto("tailed", l, s))
                    if has_out:
                        dve.wait_ge(*drained("qt2", l, t))
                        dve.wait_ge(*drained("kt2", l, s))
                        for p in range(2):
                            for q in range(2):
                                dve.wait_ge(*drained("e", l, s, p, q))
                                if q == 0:
                                    V.tensor_tensor(KW[:, p, 0:4, :], HW[:, p, 0:4, :],
                                                    KT2[:, p, :].unsqueeze(1).broadcast_to([P, 4, P]), ALU.mult)
                                else:
                                    V.tensor_tensor(KW[:, p, 4:8, :], HW[:, p, 4:8, :],
                                                    KT2[:, p, :].unsqueeze(1).broadcast_to([P, 4, P]), ALU.mult)
                                    V.tensor_tensor(QP[:, p, :], HW[:, p, 8, :], qt2(t)[:, p, :], ALU.mult)
                                user = half_buffer_last(l, s, p, q)
                                if user:
                                    dve.wait_ge(*upto("product", "a", l, *user, 1))
                                hb = half_buffer(l, s, p, q)
                                for hh in range(2):
                                    r = slice(DH * hh, DH * hh + DH)
                                    last = V.tensor_tensor(QW[r, hb, :, hh, :], HW[r, p, 4 * q:4 * q + 4, :],
                                                           qt2(t)[r, p, :].unsqueeze(1).broadcast_to([DH, 4, P]), ALU.mult)
                                last.then_inc(*made("weighed", l, s, p, q))
                    if n + 1 < len(steps):
                        gates(n + 1)
                        low(n + 1)
                    if has_out:
                        for p in range(2):
                            for q in range(2):
                                for b in range(2):
                                    ps = take("a", l, s, p, q, b)
                                    for i in range(2):
                                        j = 4 * q + 2 * b + i
                                        if i:
                                            link(last)
                                        elif q or b:
                                            dve.wait_ge(*count_now("drained_dve"))
                                        last = V.copy_predicated(AS[:, d, 2 * p:2 * p + 2, :],
                                                                 tb_masks[:, d, j, :].unsqueeze(1).broadcast_to([P, 2, P]),
                                                                 ps[:, 256 * i:256 * i + 256].rearrange("p (h c) -> p h c", h=2))
                                    last.then_inc(*made("drained_dve", "a", l, s, p, q, b))
                        dve.wait_ge(*upto("read_out", l, s))
                        o = obank[s % 2][:, 0:256]
                        if first_visit(l, s, t):
                            V.tensor_copy(scanned_sum(t), o).then_inc(*made("scanned", l, s))
                        else:
                            for s2, t2, _, o2 in steps:
                                if t2 == t and s2 < s and o2:
                                    dve.wait_ge(*upto("scanned", l, s2))
                            V.tensor_tensor(scanned_sum(t), o, scanned_sum(t), ALU.add).then_inc(*made("scanned", l, s))
                    if s < 6:
                        ps = take("su", l, s)
                        for p in range(2):
                            for hh in range(2):
                                r = slice(DH * hh, DH * hh + DH)
                                a = ST[r, d, p, DH * hh:DH * hh + DH]
                                last = V.scalar_tensor_tensor(out=a, in0=a, scalar=TOT[r, s % 2, p:p + 1],
                                                              in1=ps[r, P * p + DH * hh:P * p + DH * hh + DH],
                                                              op0=ALU.mult, op1=ALU.add)
                        last.then_inc(*made("drained_dve", "su", l, s))
                        dve.wait_ge(*drained("su", l, s))

            def readout(l, t):
                o4 = scanned_sum(t).rearrange("p (h c) -> p h c", h=4)
                for s, t2, _, o2 in scan_steps(l):
                    if t2 == t and o2:
                        dve.wait_ge(*upto("scanned", l, s))
                hs4 = HS.rearrange("p (h c) -> p h c", h=4)
                link(V.tensor_tensor(hs4, o4, o4, ALU.mult))
                link(V.tensor_reduce(nw[:, 0:4], hs4, AX.X, ALU.add))
                V.tensor_scalar(ms[:, 0:4], nw[:, 0:4], 1.0 / DH, EPS, ALU.mult, ALU.add) \
                    .then_inc(*made("mean_square", l, "scan", t))
                refine(l, "scan", t, n=4)
                link(V.tensor_tensor(hs4, o4, rs[:, 0:4].unsqueeze(2).broadcast_to([P, 4, DH]), ALU.mult))
                V.tensor_tensor(hs4, hs4, GROW3[:, 2, :].unsqueeze(1).broadcast_to([P, 4, DH]), ALU.mult) \
                    .then_inc(*made("gain_done", l, t))
                dve.wait_ge(*upto("gain_done", l, t))
                dve.wait_ge(*upto("silu_exp", l, t))
                need_u(l, t, OFF_G, OFF_G + 256)
                g = U[:, t, OFF_G:OFF_G + 256]
                link(V.tensor_scalar(HE, HE, 1.0, None, ALU.add))
                link(V.reciprocal(HE, HE))
                link(V.tensor_tensor(HE, HE, g, ALU.mult))
                V.tensor_tensor(g, HE, HS, ALU.mult).then_inc(*made("mixed", l, t))
                dve.wait_ge(*upto("mixed", l, t))

            def gate_rows(l, st):
                base = 16 if st == "mix" else 40
                if st == "ffn":
                    dve.wait_ge(*upto("product", "g", l, "mix", 1 if l == 0 else 0, 1))
                for i in range(2 if l == 0 else 1):
                    for h in range(2):
                        for c in range(4):
                            k = base + 4 * h + c
                            last = V.tensor_scalar(DIAG[:, i, h, c, :], ident[:, :], modc[:, l, k, i:i + 1], None, ALU.mult)
                        last.then_inc(*made("diagonal", l, st, i, h))

            def feed_forward(l):
                n = P * len(tiles_of(l, "ffn"))
                ath, atl = hidden[halves(l)]
                for half in range(halves(l)):
                    fs = hidden_tiles(l, half)

                    def low(f):
                        dve.wait_ge(*upto("hidden_high", l, f))
                        V.tensor_tensor(atl[:, f - fs[0], 0:n], G[:, f % 2, 0:n], as_float(ath[:, f - fs[0], 0:n]), ALU.subtract) \
                            .then_inc(*made("hidden", l, f))

                    for f in fs:
                        ps = take("up", l, f)
                        dve.wait_ge(*drained("gate", l, f))
                        V.tensor_tensor(G[:, f % 2, 0:n], ps[:, 0:n], G[:, f % 2, 0:n], ALU.mult) \
                            .then_inc(*made("drained_dve", "up", l, f))
                        if f > fs[0]:
                            low(f - 1)
                        beside("gu", l, f)
                        split(index[("gu", l, f)] + HIGH)
                    low(fs[-1])
                    for h in range(2):
                        for c in range(len(down_chunks(l, half))):
                            key = ("dn", l, half, h, c)
                            beside(*key)
                            split(index[key] + HIGH)
                        for t in tiles_of(l, "ffn"):
                            i = cond_of_tile(t) if l < 2 else 0
                            dve.wait_ge(*drained("g", l, "ffn", i, h))
                            ps = take("x2", l, half, h, t)
                            link(V.tensor_tensor(ps[:, :], ps[:, :], grow[:, i, 512 * h:512 * h + 512], ALU.mult))
                            x = X[:, t, 512 * h:512 * h + 512]
                            V.tensor_tensor(x, ps[:, :], x, ALU.add).then_inc(*made("drained_dve", "x2", l, half, h, t))

            dve.wait_ge(*upto("ident_in"))
            dve.wait_ge(*upto("cond_exp"))
            flat = cond[:, :, :].rearrange("p i k -> p (i k)")
            link(V.tensor_scalar(condt[:, 0, :], condt[:, 0, :], 1.0, None, ALU.add))
            link(V.reciprocal(condt[:, 1, :], condt[:, 0, :]))
            V.tensor_tensor(flat, flat, condt[:, 1, :], ALU.mult).then_inc(*made("cond_ready"))
            dve.wait_ge(*upto("cond_ready"))
            for j in range(1, STARTING, 2):
                ada_sum(0, j)
            for l in range(4):
                norm(l, "mix")
                project(l)
                if l < 2:
                    gains(l)
                    for g in range(2 if l == 0 else 1):
                        fourier(l, g)
                heads(l)
                attention(l)
                if l < 2:
                    recurrence(l)
                gate_rows(l, "mix")
                if l < 2:
                    for g in range(2 if l == 0 else 1):
                        fourier_out(l, g)
                tiles = tiles_of(l, "ffn")
                for n, t in enumerate(tiles):
                    if l < 2:
                        readout(l, t)
                    if n:
                        mixed_turns(l, tiles[n - 1])
                mixed_turns(l, tiles[-1])
                project_out(l)
                gate_rows(l, "ffn")
                norm(l, "ffn")
                feed_forward(l)
                if l in (1, 3):
                    row_norms(l, "final", X_TILES)
                    dve.wait_ge(*upto("final_gain_in", l))
                    for t in X_TILES:
                        last = V.scalar_tensor_tensor(out=X[:, t, :], in0=X[:, t, :], scalar=rs[:, t:t + 1],
                                                      in1=grow[:, 0, :], op0=ALU.mult, op1=ALU.mult)
                    last.then_inc(*made("final", l))

        return count


_INS = ["x", "c", "ctx", "c_ctx", "w_ada", "b_ada", "w_in", "w_four", "q_norm", "k_norm", "hg_lb_logits", "hg_norm",
        "w_out", "w_gate", "w_up", "w_down", "final_norm", "c_2", "ada_w_2", "ada_b_2", "norm_mix_2", "norm_ffn_2",
        "ffn_w_in_2", "ffn_w_out_2", "a_w_in_2", "a_w_out_2", "a_sink_2", "b_w_in_2", "b_w_out_2", "final_norm_2"]


def kernel(**inputs):
    import concourse.bacc as bacc
    from concourse.bass_utils import run_bass_kernel_spmd as run

    consts = tables()
    arrays = {f"in_{n}": np.ascontiguousarray(inputs[n]) for n in _INS}
    arrays.update({f"in_{n}": a for n, a in consts.items()})
    counts = None
    for _ in range(2):
        nc = bacc.Bacc("TRN2", target_bir_lowering=False, num_devices=1)
        io = {n[3:]: nc.dram_tensor(n, a.shape, mybir.dt.from_np(a.dtype), kind="ExternalInput").ap()
              for n, a in arrays.items()}
        io["out"] = nc.dram_tensor("out_0", (1, N, D), F32, kind="ExternalOutput").ap()
        counts = block_kernel(nc, io, counts)
    r = run(nc, [arrays], core_ids=[0])
    return r.results[0]["out_0"]
```
